# Optimizing a Trainium2 kernel written in Bass

```python
import jax
import jax.numpy as jnp
from jax import lax
import numpy as np

D_MODEL = 1024
BATCH = 1
SEQ = 256
DEPTH = 2

GRID_W = 64
CTX_LEN = 256
N_MIXERS = 2
N_HEADS = 16
N_KV_HEADS = 4
HEAD_DIM = 64
GROUP = N_HEADS // N_KV_HEADS
Q_DIM = N_HEADS * HEAD_DIM
KV_DIM = N_KV_HEADS * HEAD_DIM
WINDOW = 128
BLOCK = 128
ROPE_BASE = 10000.0
ROPE_HALF = HEAD_DIM // 4
POOL_WINDOWS = (2, 4, 8, 16)
N_POOL_GROUPS = len(POOL_WINDOWS)
POOL_GROUP_DIM = D_MODEL // N_POOL_GROUPS
D_FF = 2816
N_EXPERTS = 8
TOP_K = 2
D_FF_EXPERT = 3584
NORM_EPS = 1e-6
NEG_INF = -1e30
N_ATTN_LAYERS = (DEPTH + 1) // 2
N_POOL_LAYERS = DEPTH // 2

kernel_name = 'hybrid_swa_pool_moe_dit'

def rmsnorm(x, g):
    xf = x.astype(jnp.float32)
    y = xf * lax.rsqrt(jnp.mean(xf * xf, axis=-1, keepdims=True) + NORM_EPS)
    return (y * g.astype(jnp.float32)).astype(x.dtype)

def ada_mod(cond, w, b):
    m = jax.nn.silu(cond) @ w + b
    return jnp.split(m[..., None, :], 6, axis=-1)

def modulate(h, shift, scale):
    return h * (1 + scale) + shift

def axial_rope_tables(n_tokens):
    rows = n_tokens // GRID_W
    row = jnp.broadcast_to(jnp.arange(rows)[:, None], (rows, GRID_W)).reshape(-1).astype(jnp.float32)
    col = jnp.broadcast_to(jnp.arange(GRID_W)[None, :], (rows, GRID_W)).reshape(-1).astype(jnp.float32)
    inv_freq = ROPE_BASE ** (-jnp.arange(ROPE_HALF, dtype=jnp.float32) / ROPE_HALF)
    ang_r = row[:, None] * inv_freq
    ang_c = col[:, None] * inv_freq
    return (jnp.cos(ang_r), jnp.sin(ang_r), jnp.cos(ang_c), jnp.sin(ang_c))

def _rotate(v, cos, sin):
    v1, v2 = v[..., :ROPE_HALF], v[..., ROPE_HALF:]
    return jnp.concatenate([v1 * cos - v2 * sin, v2 * cos + v1 * sin], axis=-1)

def apply_axial_rope(t, tables):
    bshape = (t.shape[1],) + (1,) * (t.ndim - 3) + (ROPE_HALF,)
    cos_r, sin_r, cos_c, sin_c = [a.reshape(bshape) for a in tables]
    tf = t.astype(jnp.float32)
    half = HEAD_DIM // 2
    out = jnp.concatenate([_rotate(tf[..., :half], cos_r, sin_r),
                           _rotate(tf[..., half:], cos_c, sin_c)], axis=-1)
    return out.astype(t.dtype)

def q_proj(h, w_qkv):
    B, T = h.shape[:2]
    return (h @ w_qkv[:, :Q_DIM]).reshape(B, T, N_KV_HEADS, GROUP, HEAD_DIM)

def kv_proj(h, w_qkv):
    B, T = h.shape[:2]
    k, v = jnp.split(h @ w_qkv[:, Q_DIM:], 2, axis=-1)
    return k.reshape(B, T, N_KV_HEADS, HEAD_DIM), v.reshape(B, T, N_KV_HEADS, HEAD_DIM)

def sink_softmax(scores, sink):
    m = sink
    for s in scores:
        m = jnp.maximum(m, jnp.max(s, axis=-1, keepdims=True))
    probs = [jnp.exp(s - m) for s in scores]
    denom = jnp.exp(sink - m)
    for p in probs:
        denom = denom + jnp.sum(p, axis=-1, keepdims=True)
    return [p / denom for p in probs]

def latent_window_attention(q, k, v, k_ctx, v_ctx, sink):
    B, L = q.shape[:2]
    nb = L // BLOCK
    scale = HEAD_DIM ** -0.5
    qb = q.reshape(B, nb, BLOCK, N_KV_HEADS, GROUP, HEAD_DIM)

    def band(t):
        tp = jnp.pad(t, ((0, 0), (BLOCK, BLOCK), (0, 0), (0, 0))).reshape(B, nb + 2, BLOCK, N_KV_HEADS, HEAD_DIM)
        return jnp.concatenate([tp[:, :-2], tp[:, 1:-1], tp[:, 2:]], axis=2)

    kb, vb = band(k), band(v)
    s_loc = jnp.einsum('bnqhgd,bnkhd->bnhgqk', qb, kb, preferred_element_type=jnp.float32) * scale
    q_pos = jnp.arange(nb)[:, None] * BLOCK + jnp.arange(BLOCK)[None, :]
    k_pos = (jnp.arange(nb)[:, None] - 1) * BLOCK + jnp.arange(3 * BLOCK)[None, :]
    rel = k_pos[:, None, :] - q_pos[:, :, None]
    valid = (jnp.abs(rel) <= WINDOW) & (k_pos[:, None, :] >= 0) & (k_pos[:, None, :] < L)
    s_loc = jnp.where(valid[None, :, None, None, :, :], s_loc, NEG_INF)
    s_ctx = jnp.einsum('bnqhgd,bchd->bnhgqc', qb, k_ctx, preferred_element_type=jnp.float32) * scale
    p_loc, p_ctx = sink_softmax([s_loc, s_ctx], sink)
    o = (jnp.einsum('bnhgqk,bnkhd->bnqhgd', p_loc.astype(vb.dtype), vb)
         + jnp.einsum('bnhgqc,bchd->bnqhgd', p_ctx.astype(v_ctx.dtype), v_ctx))
    return o.reshape(B, L, Q_DIM)

def context_attention(q, k, v, sink):
    B, C = q.shape[:2]
    s = jnp.einsum('bqhgd,bkhd->bhgqk', q, k, preferred_element_type=jnp.float32) * HEAD_DIM ** -0.5
    (p,) = sink_softmax([s], sink)
    o = jnp.einsum('bhgqk,bkhd->bqhgd', p.astype(v.dtype), v)
    return o.reshape(B, C, Q_DIM)

def window_mean(h, w):
    T = h.shape[1]
    cs = jnp.pad(jnp.cumsum(h.astype(jnp.float32), axis=1), ((0, 0), (1, 0), (0, 0)))
    t = jnp.arange(T)
    lo = jnp.clip(t - w // 2, 0, T)
    hi = jnp.clip(t - w // 2 + w, 0, T)
    total = jnp.take(cs, hi, axis=1) - jnp.take(cs, lo, axis=1)
    return total / (hi - lo).astype(jnp.float32)[None, :, None]

def pool_mixer(h, pool_w, pool_b, pool_scale):
    B, T, _ = h.shape
    groups = jnp.split(h, N_POOL_GROUPS, axis=-1)
    d = jnp.stack([window_mean(g, w) - g.astype(jnp.float32) for g, w in zip(groups, POOL_WINDOWS)], axis=2)
    y = jnp.einsum('btgc,gcd->btgd', d.astype(h.dtype), pool_w) + pool_b.reshape(N_POOL_GROUPS, POOL_GROUP_DIM)
    return y.reshape(B, T, D_MODEL) * pool_scale

def swiglu(h, w_gu, w_down):
    g, u = jnp.split(h @ w_gu, 2, axis=-1)
    return (jax.nn.silu(g) * u) @ w_down

def moe_swiglu(h, router_w, router_b, w_gu, w_down):
    logits = (h @ router_w).astype(jnp.float32) + router_b.astype(jnp.float32)
    top_v, top_i = lax.top_k(logits, TOP_K)
    gates = jax.nn.softmax(top_v, axis=-1)
    combine = jnp.einsum('btk,btke->bte', gates, jax.nn.one_hot(top_i, N_EXPERTS, dtype=jnp.float32))
    y = jnp.zeros(h.shape, jnp.float32)
    for e in range(N_EXPERTS):
        y = y + combine[..., e:e + 1] * swiglu(h, w_gu[e], w_down[e]).astype(jnp.float32)
    return y.astype(h.dtype)

def setup_inputs(seed: int = 0) -> dict:
    key = jax.random.key(seed)
    ks = jax.random.split(key, 20)
    f32 = jnp.float32

    def dense(k, shape, fan_in):
        return jax.random.normal(k, shape, f32) * fan_in ** -0.5

    return {
        'x': jax.random.normal(ks[0], (BATCH, SEQ, D_MODEL), f32),
        'c': jax.random.normal(ks[1], (BATCH, D_MODEL), f32),
        'ctx': jax.random.normal(ks[2], (BATCH, CTX_LEN, D_MODEL), f32),
        'c_ctx': jax.random.normal(ks[3], (D_MODEL,), f32),
        'ada_w': 0.5 * dense(ks[4], (DEPTH, D_MODEL, 6 * D_MODEL), D_MODEL),
        'ada_b': 0.02 * jax.random.normal(ks[5], (DEPTH, 6 * D_MODEL), f32),
        'norm_g': 1.0 + 0.1 * jax.random.normal(ks[6], (DEPTH, 4, D_MODEL), f32),
        'attn_w_qkv': dense(ks[7], (N_ATTN_LAYERS, D_MODEL, Q_DIM + 2 * KV_DIM), D_MODEL),
        'attn_w_o': dense(ks[8], (N_ATTN_LAYERS, Q_DIM, D_MODEL), Q_DIM),
        'attn_sink': jax.random.normal(ks[9], (N_ATTN_LAYERS, N_HEADS), f32),
        'pool_w': dense(ks[10], (N_POOL_LAYERS, N_POOL_GROUPS, POOL_GROUP_DIM, POOL_GROUP_DIM), POOL_GROUP_DIM),
        'pool_b': 0.02 * jax.random.normal(ks[11], (N_POOL_LAYERS, D_MODEL), f32),
        'pool_scale': 1.0 + 0.1 * jax.random.normal(ks[12], (N_POOL_LAYERS, D_MODEL), f32),
        'ffn_w_gu': dense(ks[13], (N_ATTN_LAYERS, D_MODEL, 2 * D_FF), D_MODEL),
        'ffn_w_down': dense(ks[14], (N_ATTN_LAYERS, D_FF, D_MODEL), D_FF),
        'router_w': dense(ks[15], (N_POOL_LAYERS, D_MODEL, N_EXPERTS), D_MODEL),
        'router_b': 0.01 * jax.random.normal(ks[16], (N_POOL_LAYERS, N_EXPERTS), f32),
        'moe_w_gu': dense(ks[17], (N_POOL_LAYERS, N_EXPERTS, D_MODEL, 2 * D_FF_EXPERT), D_MODEL),
        'moe_w_down': dense(ks[18], (N_POOL_LAYERS, N_EXPERTS, D_FF_EXPERT, D_MODEL), D_FF_EXPERT),
    }

def reference(x, c, ctx, c_ctx, ada_w, ada_b, norm_g, attn_w_qkv, attn_w_o, attn_sink,
              pool_w, pool_b, pool_scale, ffn_w_gu, ffn_w_down, router_w, router_b,
              moe_w_gu, moe_w_down):
    rope = axial_rope_tables(x.shape[1])
    is_attn = [i % N_MIXERS == 0 for i in range(DEPTH)]
    for i in range(DEPTH):
        slot = i // N_MIXERS
        ctx_needed_later = any(is_attn[i + 1:])
        ctx_needed_now = is_attn[i] or ctx_needed_later
        sh_m, sc_m, gt_m, sh_f, sc_f, gt_f = ada_mod(c, ada_w[i], ada_b[i])
        g_pre_mix, g_post_mix, g_pre_ffn, g_post_ffn = norm_g[i]

        h = modulate(rmsnorm(x, g_pre_mix), sh_m, sc_m)
        if ctx_needed_now:
            csh_m, csc_m, cgt_m, csh_f, csc_f, cgt_f = ada_mod(c_ctx, ada_w[i], ada_b[i])
            hc = modulate(rmsnorm(ctx, g_pre_mix), csh_m, csc_m)
        if is_attn[i]:
            w_qkv = attn_w_qkv[slot]
            sink = attn_sink[slot].astype(jnp.float32).reshape(N_KV_HEADS, GROUP, 1, 1)
            q = apply_axial_rope(q_proj(h, w_qkv), rope)
            k, v = kv_proj(h, w_qkv)
            k = apply_axial_rope(k, rope)
            k_c, v_c = kv_proj(hc, w_qkv)
            y = latent_window_attention(q, k, v, k_c, v_c, sink) @ attn_w_o[slot]
            if ctx_needed_later:
                yc = context_attention(q_proj(hc, w_qkv), k_c, v_c, sink) @ attn_w_o[slot]
        else:
            y = pool_mixer(h, pool_w[slot], pool_b[slot], pool_scale[slot])
            if ctx_needed_later:
                yc = pool_mixer(hc, pool_w[slot], pool_b[slot], pool_scale[slot])
        x = x + gt_m * rmsnorm(y, g_post_mix)

        h = modulate(rmsnorm(x, g_pre_ffn), sh_f, sc_f)
        if i % 2 == 0:
            f = swiglu(h, ffn_w_gu[slot], ffn_w_down[slot])
        else:
            f = moe_swiglu(h, router_w[slot], router_b[slot], moe_w_gu[slot], moe_w_down[slot])
        x = x + gt_f * rmsnorm(f, g_post_ffn)

        if ctx_needed_later:
            ctx = ctx + cgt_m * rmsnorm(yc, g_post_mix)
            hc = modulate(rmsnorm(ctx, g_pre_ffn), csh_f, csc_f)
            if i % 2 == 0:
                fc = swiglu(hc, ffn_w_gu[slot], ffn_w_down[slot])
            else:
                fc = moe_swiglu(hc, router_w[slot], router_b[slot], moe_w_gu[slot], moe_w_down[slot])
            ctx = ctx + cgt_f * rmsnorm(fc, g_post_ffn)
    return x


_drawn_inputs = setup_inputs


def setup_inputs(seed=0):
    import zlib

    import numpy as np

    out = dict(_drawn_inputs(seed))
    spreads = {}
    factors = {'attn_sink': 8.0, 'pool_b': 3.937, 'router_b': 2.918}
    for name, (base, spread) in spreads.items():
        noise = np.random.default_rng([zlib.crc32(name.encode()), seed]).standard_normal(out[name].shape)
        drawn = base * np.exp(spread * noise) if base else spread * noise
        out[name] = jnp.asarray(drawn.astype(out[name].dtype))
    for name, factor in factors.items():
        out[name] = (out[name] * factor).astype(out[name].dtype)
    return out
```

```python
from contextlib import ExitStack

import numpy as np

import concourse.bass as bass
from concourse import mybir

P = 128
D = 1024
KC = D // P
T = 256
TB = T // P
C = 256
CB = C // P
H, HKV, HD = 16, 4, 64
GROUP = H // HKV
QD, KVD = H * HD, HKV * HD
KEYS = T + C
WINDOW = 128
GRID_W = 64
ROPE_HALF = HD // 4
POOL_WINDOWS = (2, 4, 8, 16)
NG = len(POOL_WINDOWS)
GD = D // NG
FF = 2816
FS = 256
FSTEPS = FF // FS
E = 8
FE = 3584
MS = 512
MSTEPS = FE // MS
SLOTS = 128
MAX_JOBS = E + (2 * T) // (SLOTS + 1)
EPS = 1e-6
NEG = -8e30

F32 = mybir.dt.float32
F32R = mybir.dt.float32r
I32 = mybir.dt.int32
U32 = mybir.dt.uint32
ALU = mybir.AluOpType
ACT = mybir.ActivationFunctionType
AX = mybir.AxisListType

K_ID, K_UP, K_IOTA, K_ONE = 0, P, 2 * P, 3 * P
K_COS, K_SIN = 4 * P, 4 * P + TB * HD
K_MASK = K_SIN + TB * HD
K_END = K_MASK + TB * P


def constants():
    t = np.zeros((P, K_END), np.float32)
    t[:, K_ID:K_ID + P] = np.eye(P)
    t[:, K_UP:K_UP + P] = np.arange(P)[:, None] < np.arange(P)[None, :]
    t[:, K_IOTA:K_IOTA + P] = np.arange(P)[None, :]
    t[:, K_ONE:K_ONE + P] = 1.0
    inv = np.float32(10000.0) ** (-np.arange(ROPE_HALF, dtype=np.float32) / np.float32(ROPE_HALF))
    for b in range(TB):
        tok = b * P + np.arange(P)
        for half, pos in enumerate((tok // GRID_W, tok % GRID_W)):
            ang = pos[:, None].astype(np.float32) * inv
            for part, sign in ((0, -1.0), (1, 1.0)):
                at = b * HD + half * 2 * ROPE_HALF + part * ROPE_HALF
                t[:, K_COS + at:K_COS + at + ROPE_HALF] = np.cos(ang)
                t[:, K_SIN + at:K_SIN + at + ROPE_HALF] = sign * np.sin(ang)
        key = (1 - b) * P + np.arange(P)
        t[:, K_MASK + b * P:K_MASK + (b + 1) * P] = np.where(
            np.abs(key[None, :] - tok[:, None]) <= WINDOW, 0.0, NEG)
    pool = np.zeros((T, NG, T), np.float32)
    for g, w in enumerate(POOL_WINDOWS):
        for i in range(T):
            lo, hi = max(i - w // 2, 0), min(i - w // 2 + w, T)
            pool[lo:hi, g, i] = 1.0 / (hi - lo)
            pool[i, g, i] -= 1.0
    pool = np.ascontiguousarray(pool.reshape(TB, P, NG, T).transpose(1, 0, 2, 3)).reshape(P, TB * NG * T)
    return t, pool


class Done:

    def __init__(self, eng):
        self.eng, self.n = eng, {}

    def __call__(self, ins, sem, wait=True):
        self.n[sem] = self.n.get(sem, 0) + 1
        ins.then_inc(sem, 1)
        if wait:
            self.eng.wait_ge(sem, self.n[sem])
        return self.n[sem]


def build(nc, x, c, ctx_in, c_ctx, ada_w, ada_b, norm_g, w_qkv, w_o, sink, pool_w, pool_b, pool_scale,
          ffn_gu, ffn_down, router_w, router_b, moe_gu, moe_down, consts, pool_m, out):
    KB = 1024
    base = (nc.sbuf_base + 63) // 64 * 64

    def sb(name, shape, dt, at):
        return nc.alloc_sbuf_tensor_at(name, [shape[0], *shape[1:]], dt, offset=base + at)

    R0, R1, R2 = 0, 48 * KB, 144 * KB
    wqkv = sb("wqkv", [P, KC, QD + 2 * KVD], F32, R0)
    m_raw = [sb(f"m_raw{k}", [P, 4, MS] if k < 4 else [P, 2, D], F32, R0 + 8 * KB * k) for k in range(6)]
    f_raw = [sb(f"f_raw{k}", [P, 4, 2 * FS] if k < 2 else [P, 2, D], F32, R0 + 24 * KB + 8 * KB * k)
             for k in range(3)]

    wo_sb = sb("wo_sb", [P, KC, D], F32, R1)
    qT = sb("qT", [P, KC, T], F32, R1 + 32 * KB)
    kT = sb("kT", [P, HKV, KEYS], F32, R1 + 40 * KB)
    ada_ring = [sb(f"ada{i}", [P, KC, 512], F32, R1 + 48 * KB + 16 * KB * i) for i in range(3)]
    f_hi = [sb(f"f_hi{k}", [P, 4, 2 * FS] if k < 2 else [P, 2, D], F32R, R1 + 16 * KB * k) for k in range(3)]
    f_lo = [sb(f"f_lo{k}", [P, 4, 2 * FS] if k < 2 else [P, 2, D], F32R, R1 + 16 * KB * k + 8 * KB)
            for k in range(3)]
    m_hi = [sb(f"m_hi{k}", [P, 4, MS] if k < 4 else [P, 2, D], F32R, R1 + 16 * KB * k) for k in range(6)]
    m_lo = [sb(f"m_lo{k}", [P, 4, MS] if k < 4 else [P, 2, D], F32R, R1 + 16 * KB * k + 8 * KB)
            for k in range(6)]
    pool_mat = sb("pool_mat", [P, TB, NG, T], F32, R1 + 64 * KB)
    pool_w_sb = sb("pool_w_sb", [P, NG, 2, GD], F32, R1 + 72 * KB)
    pool_b_row = sb("pool_b_row", [P, D], F32, R1 + 80 * KB)
    pool_s_row = sb("pool_s_row", [P, D], F32, R1 + 84 * KB)
    mod_rows = sb("mod_rows", [P, 2, D], F32, R1 + 88 * KB)

    ct = sb("consts_sb", [P, K_END], F32, R2)
    cols = sb("cols", [P, 480], F32, R2 + 4 * KB)
    small = sb("small", [P, 256], F32, R2 + 6 * KB)
    ada_acc = sb("ada_acc", [P, 512], F32, R2 + 7 * KB)
    route = sb("route", [P, 256], F32, R2 + 9 * KB)
    tok = sb("tok", [P, TB, D], F32, R2 + 10 * KB)
    S = [R2 + 18 * KB + 8 * KB * i for i in range(6)]
    ctx_tok = sb("ctx_tok", [P, CB, D], F32, S[0])
    rows_in = sb("rows_in", [P, 2, P], F32, S[5])
    ctx_junk = sb("ctx_junk", [P, 2, D], F32, S[4])
    hT = sb("hT", [P, KC, T], F32, S[1])
    hcT = sb("hcT", [P, KC, C], F32, S[2])
    xn = sb("xn", [P, 2, D], F32, S[3])
    q_tok = sb("q_tok", [P, TB, QD], F32, S[0])
    rope_a = sb("rope_a", [P, 512], F32, S[3])
    rope_b = sb("rope_b", [P, 512], F32, S[3] + 2 * KB)
    k_tok = sb("k_tok", [P, TB + CB, HKV, 2, HD], F32, S[4])
    v_tok = sb("v_tok", [P, TB + CB, KVD], F32, S[5])
    probs = sb("probs", [P, 2, KEYS], F32, S[3])
    probsT = sb("probsT", [P, 2, KEYS], F32, S[3] + 4 * KB)
    o_tok = sb("o_tok", [P, TB, QD], F32, S[1])
    oT = sb("oT", [P, KC, T], F32, S[2])
    g_row = sb("g_row", [P, D], F32, S[0])
    y_tmp = sb("y_tmp", [P, D], F32, S[0] + 4 * KB)
    hf = sb("hf", [P, KC, T], F32, S[2])
    hf_hi = sb("hf_hi", [P, KC, T], F32R, S[4])
    hf_lo = sb("hf_lo", [P, KC, T], F32R, S[1])
    f_act = sb("f_act", [P, TB, FS], F32, S[3])
    fT_hi = sb("fT_hi", [P, 2, TB, P], F32R, S[3] + 2 * KB)
    fT_lo = sb("fT_lo", [P, 2, TB, P], F32R, S[3] + 4 * KB)
    sq_junk = sb("sq_junk", [P, 2, D], F32, S[0])
    pool_y = sb("pool_y", [P, TB, D], F32, S[3])
    g1m_row = sb("g1m_row", [P, D], F32, S[5])
    h_tok = sb("h_tok", [P, TB, D], F32, S[2])
    dT = sb("dT", [P, KC, T], F32, S[1])
    hr = sb("hr", [P, KC, T], F32, S[2])
    xm = sb("xm", [P, TB, D], F32, S[3])
    acc = sb("acc", [P, TB, D], F32, S[1])
    xs_full = sb("xs_full", [P, KC, SLOTS], F32, S[0])
    y_slots = sb("y_slots", [P, D], F32, S[0] + 4 * KB)
    xs_hi = sb("xs_hi", [P, KC, SLOTS], F32R, S[2])
    xs_lo = sb("xs_lo", [P, KC, SLOTS], F32R, S[2] + 4 * KB)
    m_act = sb("m_act", [P, MS], F32, S[4])
    mT_hi = sb("mT_hi", [P, 4, SLOTS], F32R, S[4] + 2 * KB)
    mT_lo = sb("mT_lo", [P, 4, SLOTS], F32R, S[4] + 4 * KB)
    hot = sb("hot", [P, TB, SLOTS], F32, S[4] + 6 * KB)
    hot_g = sb("hot_g", [P, TB, SLOTS], F32, S[4] + 7 * KB)
    hotT = sb("hotT", [P, TB, P], F32, S[5])
    route_w = sb("route_w", [P, KC, E], F32, S[5] + 4 * KB)
    jobs_i = sb("jobs_i", [P, 16], I32, S[5] + 4 * KB + 256)
    jobs_f = sb("jobs_f", [P, 16], F32, S[5] + 4 * KB + 320)
    job_table = sb("job_table", [P, 4, 12], F32, S[5] + 4 * KB + 384)
    job_col = sb("job_col", [P, 4], F32, S[5] + 4 * KB + 576)
    top_i = sb("top_i", [P, 2 * E], U32, S[5] + 4 * KB + 608)

    ident = ct[:, K_ID:K_ID + P]
    upper = ct[:, K_UP:K_UP + P]
    iota = ct[:, K_IOTA:K_IOTA + P]
    ones = ct[:, K_ONE:K_ONE + P]

    def cos_of(b):
        return ct[:, K_COS + b * HD:K_COS + (b + 1) * HD]

    def sin_of(b):
        return ct[:, K_SIN + b * HD:K_SIN + (b + 1) * HD]

    def col(a, n):
        return cols[:, a:a + n]

    N_GAIN = 0
    N_B = 80
    N_M0, N_MC, N_M1 = 176, 224, 240
    N_SC = 288
    N_A = 304
    N_G = 344
    N_SINK, N_NSINK, N_RB = 376, 392, 408

    def gain(layer, which):
        return col(N_GAIN + 16 + (layer * 4 + which) * KC, KC)

    R_L, R_TOP, R_TOPI = 0, 16, 32
    R_D, R_EX, R_DEN, R_G1, R_G2 = 48, 50, 52, 54, 56
    R_H1, R_H2, R_MASK, R_GATE, R_POS, R_CNT, R_OVER, R_RANK = 64, 72, 80, 96, 112, 128, 136, 144
    R_SEL, R_TMP, R_JUNK = 152, 176, 192

    SM_NM, SM_SUM, SM_MAX, SM_ES, SM_DEN, SM_RDEN = 64, 96, 128, 160, 192, 224

    ps = nc.alloc_psum_tensor("ps", [P, 8, 512], F32)

    def bank(i):
        return ps[:, i, :]

    names = """x_in ctx_in consts_in rows_in sink_in rb_in wqkv_in wo_in ada_in0 ada_in1 ada_in2 ada_late_in
        pool_in cols_turned cols_ready silu_ready ada_used acc_ready colsum_ready mod_ready a_ready nsink_ready
        sumsq_ready msq_ready sqrt_ready rstd_ready dve_step xn_ready turn_ready turned_taken
        qkv_ready kv_lat_taken kv_ctx_taken q_taken tr2_ready tr2_taken
        scores_ready max_ready nmax_ready probs_ready pt_ready pt_taken pv_ready esink_in esink_ready o_taken
        row_ready row_taken wo_ready y_normed
        f_in0 f_in1 f_in2 f_split0 f_split1 f_split2 f_hi0 f_hi1 f_hi2 f_used0 f_used1 f_used2
        f_silu f_act_ready f_turned f_thi f_tlo hf_hi_ready hf_ready
        pooled pooled_taken poolmix_ready poolbias_ready
        router_ready diff_ready exp_ready mask_ready ranks_ready route_ready
        m_in0 m_in1 m_in2 m_in3 m_in4 m_in5 m_hi0 m_hi1 m_hi2 m_hi3 m_hi4 m_hi5
        m_split0 m_split1 m_split2 m_split3 m_split4 m_split5 m_used0 m_used1 m_used2 m_used3 m_used4 m_used5
        m_silu m_act_ready m_turned m_thi m_tlo job_col_ready hot_ready gathered xs_ready xs_hi_ready xs_split
        y_taken scattered hotg_ready hotg_turned hotT_ready acc_added tok_ready out_done""".split()
    s = {n: nc.alloc_semaphore(n) for n in names}

    ada_v = ada_w.rearrange("l (k p) n -> l p k n", p=P)
    PIECES = 12
    PE_PIECES = 4
    EARLY = PIECES - PE_PIECES + 1
    L1_LATE = PIECES - 1
    assert L1_LATE == FSTEPS
    gu_v = ffn_gu[0].rearrange("(k p) n -> p k n", p=P)
    dn_v = ffn_down[0].rearrange("(s q p) n -> s p q n", p=P, q=FS // P)
    mgu_v = moe_gu[0].rearrange("e (k p) n -> e p k n", p=P)
    mdn_v = moe_down[0].rearrange("e (q p) n -> e p q n", p=P)

    NORM_LAT, NORM_CTX, NORM_Y, NORM_F, NORM_POOL_PRE, NORM_POOL, NORM_MOE_PRE, NORM_LAST = 0, 1, 2, 6, 7, 8, 9, 10
    SUMS = [2, 2, 1, 1, 1, 1, 2, 2, 2, 2, 2]
    SUMS_UNTIL = [sum(SUMS[:n + 1]) for n in range(len(SUMS))]

    def stat(n, what):
        at = 8 * (n % 8) + 2 * what
        return small[:, at:at + SUMS[n]]

    block = nc.Block()
    block.__enter__()

    @block.sync
    def _(sp):
        sp.dma_start(ct[:], consts).then_inc(s["consts_in"], 16)
        sp.dma_start(rows_in[0:8, 0, :], c.rearrange("a (k p) -> (a k) p", p=P)).then_inc(s["rows_in"], 16)
        sp.dma_start(rows_in[8:16, 0, :], c_ctx.rearrange("(k p) -> k p", p=P)).then_inc(s["rows_in"], 16)
        sp.dma_start(rows_in[16:80, 0, :], norm_g.rearrange("l w (k p) -> (l w k) p", p=P)).then_inc(s["rows_in"], 16)
        sp.dma_start(rows_in[0:96, 1, :], ada_b.rearrange("l (k p) -> (l k) p", p=P)).then_inc(s["rows_in"], 16)
        sp.dma_start(tok[:], x[0].rearrange("(b p) d -> p b d", p=P)).then_inc(s["x_in"], 16)
        sp.dma_start(ctx_tok[:], ctx_in[0].rearrange("(b p) d -> p b d", p=P)).then_inc(s["ctx_in"], 16)
        sp.dma_start(col(N_SINK, H), sink[0].partition_broadcast(P)).then_inc(s["sink_in"], 16)
        sp.dma_start(col(N_RB, E), router_b[0].partition_broadcast(P)).then_inc(s["rb_in"], 16)
        sp.dma_start(route_w[:], router_w[0].rearrange("(k p) e -> p k e", p=P)).then_inc(s["rb_in"], 16)
        sp.wait_ge(s["ada_in0"], 16)
        qkv_v = w_qkv[0].rearrange("(k p) n -> p k n", p=P)
        for i in (2, 0, 1):
            sp.dma_start(wqkv[:, :, 512 * i:512 * i + 512], qkv_v[:, :, 512 * i:512 * i + 512]).then_inc(s["wqkv_in"], 16)
        sp.dma_start(wo_sb[:], w_o[0].rearrange("(k p) n -> p k n", p=P)).then_inc(s["wo_in"], 16)

        def dense_step(st):
            for k in range(2):
                if not isinstance(st, int):
                    sp.wait_ge(s[f"f_split{k}"], st)
                for half, at in ((0, 0), (1, FF)):
                    sp.dma_start(f_raw[k][:, :, half * FS:half * FS + FS],
                                 gu_v[:, 4 * k:4 * k + 4, bass.ds(st * FS + at, FS)]).then_inc(s[f"f_in{k}"], 16)
            if not isinstance(st, int):
                sp.wait_ge(s["f_split2"], st)
            sp.dma_start(f_raw[2][:], dn_v[bass.ds(st, 1)].rearrange("a p q n -> p (a q) n")
                         if not isinstance(st, int) else dn_v[st]).then_inc(s["f_in2"], 16)

        sp.wait_ge(s["qkv_ready"], 8)
        dense_step(0)
        with sp.Fori(1, FSTEPS) as st:
            dense_step(st)

        def expert_load(k, e, i, step):
            if not isinstance(step, int):
                sp.wait_ge(s[f"m_split{k}"], step + 1)
            if k < 4:
                src = mgu_v[bass.ds(e, 1), :, 4 * (k % 2):4 * (k % 2) + 4, bass.ds(i * MS + (k // 2) * FE, MS)]
            else:
                src = mdn_v[bass.ds(e, 1), :, bass.ds(i * (MS // P) + 2 * (k - 4), 2), :]
            sp.dma_start(m_raw[k][:], src.rearrange("e p k n -> p (e k) n")).then_inc(s[f"m_in{k}"], 16)

        def job_loads(j, e, e_next):
            step = j * MSTEPS
            with sp.Fori(0, MSTEPS - 1) as i:
                for k in range(4):
                    expert_load(k, e, i + 1, step + i + 1)
                for k in (4, 5):
                    expert_load(k, e, i, step + i)
            if e_next is not None:
                for k in range(4):
                    expert_load(k, e_next, 0, step + MSTEPS)
            for k in (4, 5):
                expert_load(k, e, MSTEPS - 1, step + MSTEPS - 1)

        for k in range(4):
            if k == 3:
                sp.wait_ge(s["f_split0"], FSTEPS)
            expert_load(k, 0, 0, 0)
        for k in (1, 2):
            sp.wait_ge(s[f"f_split{k}"], FSTEPS)
        with sp.Fori(0, E - 2) as j:
            job_loads(j, j, j + 1)
        sp.wait_ge(s["route_ready"], 1)
        last_job = sp.value_load(jobs_i[0:1, 15:16], min_val=E - 1, max_val=MAX_JOBS - 1)
        with sp.Fori(E - 2, last_job) as j:
            e = sp.value_load(jobs_i[0:1, bass.ds(j, 1)], min_val=0, max_val=E - 1)
            e_next = sp.value_load(jobs_i[0:1, bass.ds(j + 1, 1)], min_val=0, max_val=E - 1)
            job_loads(j, e, e_next)
        job_loads(last_job, sp.value_load(jobs_i[0:1, bass.ds(last_job, 1)], min_val=0, max_val=E - 1), None)

        for b in range(TB):
            sp.wait_ge(s["tok_ready"], b + 1)
            sp.dma_start(out[0].rearrange("(b p) d -> p b d", p=P)[:, b, :], tok[:, b, :]).then_inc(s["out_done"], 16)
        sp.wait_ge(s["out_done"], 16 * TB)

    @block.gpsimd
    def _(pool):
        for i in range(PIECES + PIECES - L1_LATE):
            l, n = divmod(i, PIECES)
            if i >= 3:
                if i - 3 < PE_PIECES:
                    pool.wait_ge(s["ada_used"], i - 2)
                else:
                    pool.wait_ge(s["acc_ready"], KC * (i - 2 - PE_PIECES))
            pool.dma_start(ada_ring[i % 3][:], ada_v[l, :, :, 512 * n:512 * n + 512]).then_inc(s[f"ada_in{i % 3}"], 16)
        with pool.Fori(0, L1_LATE) as n:
            pool.wait_ge(s["acc_ready"], (n + EARLY) * KC)
            pool.dma_start(ada_ring[0][:], ada_v[1, :, :, bass.ds(n * 512 + 512 * (PIECES - L1_LATE), 512)]
                           ).then_inc(s["ada_late_in"], 16)
        pool.dma_start(pool_mat[:], pool_m.rearrange("p (b g t) -> p b g t", b=TB, g=NG)).then_inc(s["pool_in"], 16)
        pool.dma_start(pool_w_sb[:], pool_w[0].rearrange("g (k p) n -> p g k n", p=P)).then_inc(s["pool_in"], 16)
        pool.dma_start(pool_b_row[:], pool_b[0].partition_broadcast(P)).then_inc(s["pool_in"], 16)
        pool.dma_start(pool_s_row[:], pool_scale[0].partition_broadcast(P)).then_inc(s["pool_in"], 16)

    FILL_BANKS = (1, 2)

    @block.tensor
    def _(pe):
        for k in (4, 5):
            pe.sem_inc(s[f"m_used{k}"], 1)
        pe.sem_inc(s["f_used2"], 1)
        pe.sem_inc(s["f_turned"], 1)
        pe.sem_inc(s["m_turned"], 1)

        pe.wait_ge(s["rows_in"], 64)
        pe.wait_ge(s["consts_in"], 16)
        pe.transpose(ps[:, 0, 0:80], rows_in[0:80, 0, :], ident[0:80, 0:80])
        pe.transpose(ps[:, 0, 80:176], rows_in[0:96, 1, :], ident[0:96, 0:96]).then_inc(s["cols_turned"], 1)

        pe.wait_ge(s["silu_ready"], 1)
        for i in range(PE_PIECES):
            pe.wait_ge(s[f"ada_in{i % 3}"], 16 * (i // 3 + 1))
            for n in range(4):
                at = 2 * (4 * i + n)
                for k in range(KC):
                    mm = pe.matmul(ps[:, 0, at:at + 2], ada_ring[i % 3][:, k, n * P:n * P + P],
                                   cols[:, N_SC + 2 * k:N_SC + 2 * k + 2], start=(k == 0), stop=(k == KC - 1))
            mm.then_inc(s["ada_used"], 1)

        fills = [0]

        def turn_fill(src, f):
            n = fills[0]
            fills[0] += 1
            if n >= 2:
                pe.wait_ge(s["turned_taken"], n - 1)
            for k in range(2):
                for b in range(2):
                    tr = pe.transpose(ps[:, FILL_BANKS[n % 2], (2 * k + b) * P:(2 * k + b + 1) * P],
                                      src[:, b, (2 * f + k) * P:(2 * f + k + 1) * P], ident)
            tr.then_inc(s["turn_ready"], 1)

        for seq in range(2):
            pe.wait_ge(s["xn_ready"], 2 * seq + 2)
            for f in range(4):
                turn_fill((xn, ctx_tok)[seq], f)

        def column_sums(q):
            pe.wait_ge(s["acc_ready"], (q + 1) * KC)
            if isinstance(q, int) and q == 0:
                pe.wait_ge(s["a_ready"], 1)
            else:
                pe.wait_ge(s["mod_ready"], q)
            for n in range(4):
                mm = pe.matmul(ps[:, 0, n:n + 1], ada_acc[:, n * P:n * P + P], ones[:, 0:1], start=True, stop=True)
            mm.then_inc(s["colsum_ready"], 1)

        UNITS = [("lat", 0, 2), ("lat", 1, 2), ("ctx", 0, 2), ("ctx", 1, 2),
                 ("lat", 0, 0), ("lat", 1, 0), ("lat", 0, 1), ("lat", 1, 1)]
        for u, (seq, b, n) in enumerate(UNITS):
            if u == 0:
                pe.wait_ge(s["turned_taken"], 4)
                pe.wait_ge(s["wqkv_in"], 16 * 3)
            if u == 2:
                pe.wait_ge(s["turned_taken"], 8)
            if u in (4, 5):
                pe.wait_ge(s["kv_lat_taken"], u - 3)
            if u in (6, 7):
                pe.wait_ge(s["kv_ctx_taken"], u - 5)
            src = hT if seq == "lat" else hcT
            for k in range(KC):
                mm = pe.matmul(bank(3 + u % 4), src[:, k, b * P:(b + 1) * P],
                               wqkv[:, k, 512 * n:512 * n + 512], start=(k == 0), stop=(k == KC - 1))
            mm.then_inc(s["qkv_ready"], 1)
            if u >= 1:
                column_sums(u - 1)

        pe.wait_ge(s["kv_lat_taken"], 2)
        pe.wait_ge(s["kv_ctx_taken"], 2)
        for g in range(HKV):
            if g >= 2:
                pe.wait_ge(s["tr2_taken"], g - 1)
            else:
                pe.wait_ge(s["turned_taken"], 7 + g)
            for t in range(4):
                tr = pe.transpose(ps[:, 1 + g % 2, t * P:(t + 1) * P], k_tok[:, t, g, :, :], ident)
            tr.then_inc(s["tr2_ready"], 1)
        for f in range(4):
            pe.wait_ge(s["q_taken"], 2 * (f // 2) + 2)
            pe.wait_ge(s["tr2_taken"], 3 + f)
            for k in range(2):
                for b in range(TB):
                    tr = pe.transpose(ps[:, 1 + f % 2, (2 * k + b) * P:(2 * k + b + 1) * P],
                                      q_tok[:, b, (2 * f + k) * P:(2 * f + k + 1) * P], ident)
            tr.then_inc(s["tr2_ready"], 1)

        OB = [7, 1, 2, 7]
        OFF = TB - 1

        def scores(u):
            b, h = divmod(u, H)
            g, half = h // GROUP, HD * (h % 2)
            if u >= 2:
                pe.wait_ge(s["probs_ready"], u - 1)
            if u == 0:
                pe.wait_ge(s["tr2_taken"], 8)
                pe.wait_ge(s["q_taken"], 4)
            lhs = qT[half:half + HD, h // 2, b * P:(b + 1) * P]
            other = 1 - b
            pe.matmul(ps[:, 3 + u % 2, other * P:(other + 1) * P], ident, ct[:, K_MASK + b * P:K_MASK + (b + 1) * P],
                      start=True, stop=False)
            parts = [(other * P, other * P + P)] + ([(0, P), (2 * P, KEYS)] if b == 0 else [(P, KEYS)])
            for n, (at, to) in enumerate(parts):
                mm = pe.matmul(ps[:, 3 + u % 2, at:to], lhs, kT[half:half + HD, g, at:to], start=(n > 0), stop=True)
            mm.then_inc(s["scores_ready"], 1)

        def turn_probs(u):
            pe.wait_ge(s["probs_ready"], u + 1)
            if u >= 2:
                pe.wait_ge(s["pt_taken"], u - 1)
            for t in range(4):
                tr = pe.transpose(ps[:, 5 + u % 2, t * P:(t + 1) * P], probs[:, u % 2, t * P:(t + 1) * P], ident)
            tr.then_inc(s["pt_ready"], 1)

        def weigh_values(u):
            b, h = divmod(u, H)
            og = u // 8
            if u == 24:
                pe.wait_ge(s["o_taken"], 1)
            pe.wait_ge(s["pt_taken"], u + 1)
            at = (h % 8) * HD
            for t in range(4):
                mm = pe.matmul(ps[:, OB[og], at:at + HD], probsT[:, u % 2, t * P:(t + 1) * P],
                               v_tok[:, t, (h // GROUP) * HD:(h // GROUP + 1) * HD], start=(t == 0), stop=(t == 3))
            mm.then_inc(s["pv_ready"], 1)

        NU = TB * H
        for u in range(NU + 2):
            if u < NU:
                scores(u)
            if 1 <= u <= NU:
                turn_probs(u - 1)
            if u >= 2:
                weigh_values(u - 2)
            if u == 2:
                column_sums(EARLY - 2)
            if u == NU // 2 + 4:
                column_sums(EARLY - 1)

        for og in range(4):
            pe.wait_ge(s["o_taken"], og + 1)
            pe.wait_ge(s["pt_taken"], NU - 1 + og)
            for k in range(4):
                tr = pe.transpose(ps[:, 5 + og % 2, k * P:(k + 1) * P],
                                  o_tok[:, og // 2, (4 * (og % 2) + k) * P:(4 * (og % 2) + k + 1) * P], ident)
            tr.then_inc(s["pt_ready"], 1)

        def spread_row(src_col, banks, n):
            for f in range(2):
                if n + f >= 2:
                    pe.wait_ge(s["row_taken"], n + f - 1)
                for k in range(4):
                    v = cols[:, src_col + 4 * f + k:src_col + 4 * f + k + 1].to_broadcast([P, P])
                    mm = pe.matmul(ps[:, banks[f], k * P:(k + 1) * P], v, ident, start=True, stop=True)
                mm.then_inc(s["row_ready"], 1)

        pe.wait_ge(s["a_ready"], 3)
        pe.wait_ge(s["o_taken"], 4)
        spread_row(N_G, (0, 7), 0)

        pe.wait_ge(s["wo_in"], 16)
        for b in range(TB):
            pe.wait_ge(s["pt_taken"], NU + 2 * b + 2)
            for half in range(2):
                for k in range(KC):
                    mm = pe.matmul(bank((3, 1)[b] + half), oT[:, k, b * P:(b + 1) * P],
                                   wo_sb[:, k, 512 * half:512 * half + 512], start=(k == 0), stop=(k == KC - 1))
                mm.then_inc(s["wo_ready"], 1)

        pe.wait_ge(s["y_normed"], 2)
        pe.wait_ge(s["xn_ready"], 6)
        for f in range(4):
            turn_fill(xn, f)
        spread_row(N_G + KC, (0, 7), 2)

        def gate_up(st, k, peeled):
            pe.wait_ge(s[f"f_split{k}"], st + 1)
            pe.wait_ge(s["hf_ready"], k + 1)
            if k == 0 and not (peeled and st == 0):
                pe.wait_ge(s["f_act_ready"], st)
            for kk in range(4):
                for b in range(TB):
                    hi = hf_hi[:, 4 * k + kk, b * P:(b + 1) * P]
                    lo = hf_lo[:, 4 * k + kk, b * P:(b + 1) * P]
                    first, last = k == 0 and kk == 0, k == 1 and kk == 3
                    pe.matmul(bank(1 + b), hi, f_hi[k][:, kk, :], start=first, stop=False)
                    pe.matmul(bank(1 + b), hi, f_lo[k][:, kk, :], start=False, stop=False)
                    mm = pe.matmul(bank(1 + b), lo, f_hi[k][:, kk, :], start=False, stop=last)
            mm.then_inc(s[f"f_used{k}"], 1)

        def turn_act(st):
            pe.wait_ge(s["f_act_ready"], st + 1)
            if not (isinstance(st, int) and st == 0):
                pe.wait_ge(s["f_tlo"], st)
            for q in range(2):
                for b in range(TB):
                    tr = pe.transpose(ps[:, 7, (2 * q + b) * P:(2 * q + b + 1) * P],
                                      f_act[:, b, q * P:(q + 1) * P], ident)
            tr.then_inc(s["f_turned"], 1)

        def down(st, first=False, last=False):
            pe.wait_ge(s["f_split2"], st + 1)
            pe.wait_ge(s["f_tlo"], st + 1)
            for q in range(2):
                for b in range(TB):
                    for lhs, rhs in ((fT_hi, f_hi[2]), (fT_hi, f_lo[2]), (fT_lo, f_hi[2])):
                        for half in range(2):
                            mm = pe.matmul(bank(3 + 2 * b + half), lhs[:, q, b, :], rhs[:, q, 512 * half:512 * half + 512],
                                           start=(first and q == 0 and lhs is fT_hi and rhs is f_hi[2]),
                                           stop=(last and q == 1 and lhs is fT_lo), skip_group_check=True)
            mm.then_inc(s["f_used2"], 1)

        pe.wait_ge(s["row_taken"], 4)
        gate_up(0, 0, True)
        gate_up(0, 1, True)
        gate_up(1, 0, True)
        turn_act(0)
        gate_up(1, 1, True)
        column_sums(EARLY)
        down(0, first=True)
        with pe.Fori(2, FSTEPS) as st:
            gate_up(st, 0, False)
            turn_act(st - 1)
            gate_up(st, 1, False)
            column_sums(st + EARLY - 1)
            down(st - 1)
        turn_act(FSTEPS - 1)
        column_sums(EARLY + L1_LATE - 1)
        down(FSTEPS - 1, last=True)

        pe.wait_ge(s["a_ready"], 4)
        pe.wait_ge(s["f_act_ready"], FSTEPS)
        for r, src in enumerate((N_A + 3 * KC, N_M1, N_G + 2 * KC)):
            spread_row(src, (1, 2), 2 * r + 4)

        pe.wait_ge(s["xn_ready"], 8)
        pe.wait_ge(s["pool_in"], 64)
        for f in range(4):
            if f >= 2:
                pe.wait_ge(s["pooled_taken"], f - 1)
            for k in range(2):
                kc = 2 * f + k
                for b in range(TB):
                    mm = pe.matmul(ps[:, (7, 0)[f % 2], k * T:(k + 1) * T], h_tok[:, b, kc * P:(kc + 1) * P],
                                   pool_mat[:, b, kc * P // GD, :], start=(b == 0), stop=(b == TB - 1))
            mm.then_inc(s["pooled"], 1)
        pe.wait_ge(s["pooled_taken"], 4)
        for b in range(TB):
            for g in range(NG):
                for k in range(2):
                    mm = pe.matmul(ps[:, 3 + 2 * b + g // 2, (g % 2) * GD:(g % 2 + 1) * GD],
                                   dT[:, 2 * g + k, b * P:(b + 1) * P], pool_w_sb[:, g, k, :],
                                   start=(k == 0), stop=(k == 1))
            mm.then_inc(s["poolmix_ready"], 1)

        pe.wait_ge(s["row_taken"], 10)
        pe.wait_ge(s["xn_ready"], 10)
        for f in range(4):
            turn_fill(xm, f)
        pe.wait_ge(s["turned_taken"], 16)
        pe.wait_ge(s["rb_in"], 16 * 2)
        for b in range(TB):
            for k in range(KC):
                mm = pe.matmul(ps[:, 7, b * E:(b + 1) * E], hr[:, k, b * P:(b + 1) * P], route_w[:, k, :],
                               start=(k == 0), stop=(k == KC - 1))
        mm.then_inc(s["router_ready"], 1)
        pe.wait_ge(s["mask_ready"], 1)
        m0, m1 = route[:, R_MASK:R_MASK + E], route[:, R_MASK + E:R_MASK + 2 * E]
        pe.matmul(ps[:, 0, 0:E], upper, m0, start=True, stop=True)
        pe.matmul(ps[:, 0, E:2 * E], upper, m1, start=True, stop=False)
        pe.matmul(ps[:, 0, E:2 * E], ones, m0, start=False, stop=True)
        pe.matmul(ps[:, 0, 2 * E:3 * E], ones, m0, start=True, stop=False)
        pe.matmul(ps[:, 0, 2 * E:3 * E], ones, m1, start=False, stop=True).then_inc(s["ranks_ready"], 1)

        def gather():
            for k in range(KC):
                for b in range(TB):
                    mm = pe.matmul(ps[:, 5 + k // 4, (k % 4) * P:(k % 4 + 1) * P], xm[:, b, k * P:(k + 1) * P],
                                   hot[:, b, :], start=(b == 0), stop=(b == TB - 1))
            mm.then_inc(s["gathered"], 1)

        def expert_gate_up(k, step):
            pe.wait_ge(s[f"m_split{k}"], step + 2)
            b = 1 + k // 2
            for kk in range(4):
                kc = 4 * (k % 2) + kk
                first, last = kc == 0, kc == KC - 1
                pe.matmul(bank(b), xs_hi[:, kc, :], m_hi[k][:, kk, :], start=first, stop=False)
                pe.matmul(bank(b), xs_hi[:, kc, :], m_lo[k][:, kk, :], start=False, stop=False)
                mm = pe.matmul(bank(b), xs_lo[:, kc, :], m_hi[k][:, kk, :], start=False, stop=last)
            mm.then_inc(s[f"m_used{k}"], 1)

        def expert_turn(step):
            pe.wait_ge(s["m_act_ready"], step + 2)
            pe.wait_ge(s["m_tlo"], step + 1)
            for q in range(4):
                tr = pe.transpose(ps[:, 7, q * P:(q + 1) * P], m_act[:, q * P:(q + 1) * P], ident)
            tr.then_inc(s["m_turned"], 1)

        def expert_down(step, first=False, last=False):
            pe.wait_ge(s["m_tlo"], step + 2)
            for k in (4, 5):
                pe.wait_ge(s[f"m_split{k}"], step + 2)
                for q in range(2):
                    for lhs, rhs in ((mT_hi, m_hi[k]), (mT_hi, m_lo[k]), (mT_lo, m_hi[k])):
                        for half in range(2):
                            mm = pe.matmul(bank(3 + half), lhs[:, 2 * (k - 4) + q, :], rhs[:, q, 512 * half:512 * half + 512],
                                           start=(first and k == 4 and q == 0 and lhs is mT_hi and rhs is m_hi[k]),
                                           stop=(last and k == 5 and q == 1 and lhs is mT_lo), skip_group_check=True)
                mm.then_inc(s[f"m_used{k}"], 1)

        def scatter(j, n):
            b, half = divmod(n, 2)
            pe.matmul(bank((5, 6, 0, 5)[n]), hotT[:, b, :], y_slots[:, 512 * half:512 * half + 512],
                      start=True, stop=True).then_inc(s["scattered"], 1)

        def job(j, last):
            step = j * MSTEPS
            pe.wait_ge(s["xs_split"], j + 1)
            pe.wait_ge(s["m_act_ready"], step + 1)
            for k in range(4):
                expert_gate_up(k, step)
            pe.wait_ge(s["m_act_ready"], step + 2)
            expert_gate_up(0, step + 1)
            expert_gate_up(1, step + 1)
            expert_turn(step)
            pe.wait_ge(s["y_taken"], j + 1)
            pe.wait_ge(s["hotT_ready"], j + 1)
            for n in range(3):
                scatter(j, n)
            expert_gate_up(2, step + 1)
            expert_gate_up(3, step + 1)
            pe.wait_ge(s["acc_added"], 4 * j + 1)
            scatter(j, 3)
            pe.wait_ge(s["acc_added"], 4 * j + 2)
            pe.wait_ge(s["hotg_ready"], j + 1)
            for b in range(TB):
                tr = pe.transpose(ps[:, 6, b * P:(b + 1) * P], hot_g[:, b, :], ident)
            tr.then_inc(s["hotg_turned"], 1)
            expert_down(step, first=True)
            with pe.Fori(2, MSTEPS) as i:
                st = step + i
                pe.wait_ge(s["m_act_ready"], st + 1)
                expert_gate_up(0, st)
                expert_gate_up(1, st)
                expert_turn(st - 1)
                expert_gate_up(2, st)
                expert_gate_up(3, st)
                expert_down(st - 1)
            expert_turn(step + MSTEPS - 1)
            if not last:
                pe.wait_ge(s["hot_ready"], j + 2)
                pe.wait_ge(s["hotT_ready"], j + 2)
                pe.wait_ge(s["acc_added"], 4 * j + 4)
                gather()
            else:
                pe.wait_ge(s["hotT_ready"], j + 2)
                pe.wait_ge(s["acc_added"], 4 * j + 4)
                for f in range(2):
                    for k in range(4):
                        at = N_G + 3 * KC + 4 * f + k
                        mm = pe.matmul(ps[:, 5 + f, k * P:(k + 1) * P], cols[:, at:at + 1].to_broadcast([P, P]),
                                       ident, start=True, stop=True)
                    mm.then_inc(s["row_ready"], 1)
            expert_down(step + MSTEPS - 1, last=True)

        pe.wait_ge(s["route_ready"], 1)
        last_job = pe.value_load(jobs_i[0:1, 15:16], min_val=E - 1, max_val=MAX_JOBS - 1)
        pe.wait_ge(s["hot_ready"], 1)
        gather()
        with pe.Fori(0, last_job) as j:
            job(j, False)
        j = last_job
        job(j, True)
        pe.wait_ge(s["y_taken"], j + 2)
        pe.wait_ge(s["row_taken"], 12)
        for n in range(3):
            scatter(j, n)
        pe.wait_ge(s["acc_added"], 4 * j + 5)
        scatter(j, 3)

    @block.scalar
    def _(act):
        def squares(n, pairs):
            for b, (src, junk) in enumerate(pairs):
                act.activation(junk, src, ACT.Square, accum_out=stat(n, 0)[:, b:b + 1]).then_inc(s["sumsq_ready"], 1)

        def root(n):
            act.wait_ge(s["msq_ready"], n + 1)
            act.activation(stat(n, 2), stat(n, 1), ACT.Sqrt).then_inc(s["sqrt_ready"], 1)

        act.wait_ge(s["x_in"], 16)
        squares(NORM_LAT, [(tok[:, b, :], xn[:, b, :]) for b in range(TB)])
        root(NORM_LAT)
        act.wait_ge(s["ctx_in"], 16)
        squares(NORM_CTX, [(ctx_tok[:, b, :], ctx_junk[:, b, :]) for b in range(CB)])
        root(NORM_CTX)
        act.wait_ge(s["cols_ready"], 1)
        act.activation(cols[:, N_SC:N_SC + 2 * KC].rearrange("p (k a) -> p k a", a=2),
                       cols[:, 0:2 * KC].rearrange("p (a k) -> p k a", a=2), ACT.Silu).then_inc(s["silu_ready"], 1)

        for b in range(CB):
            act.wait_ge(s["qkv_ready"], 3 + b)
            kv = bank(3 + 2 + b)
            for twice in range(2):
                act.activation(k_tok[:, TB + b, :, twice, :], kv[:, 0:KVD].rearrange("p (g d) -> p g d", g=HKV), ACT.Copy)
            act.activation(v_tok[:, TB + b, :], kv[:, KVD:2 * KVD], ACT.Copy).then_inc(s["kv_ctx_taken"], 1)
        for g in range(HKV):
            act.wait_ge(s["tr2_ready"], g + 1)
            act.activation(kT[:, g, :], bank(1 + g % 2), ACT.Copy).then_inc(s["tr2_taken"], 1)
        for f in range(4):
            act.wait_ge(s["tr2_ready"], 5 + f)
            act.activation(qT[:, 2 * f:2 * f + 2, :], bank(1 + f % 2).rearrange("p (k t) -> p k t", k=2),
                           ACT.Copy).then_inc(s["tr2_taken"], 1)

        NU = TB * H

        def take_turned(u):
            act.wait_ge(s["pt_ready"], u + 1)
            if u >= 2:
                act.wait_ge(s["pv_ready"], u - 1)
            act.activation(probsT[:, u % 2, :], bank(5 + u % 2), ACT.Copy).then_inc(s["pt_taken"], 1)

        for u in range(NU):
            act.wait_ge(s["nmax_ready"], u + 1)
            if u >= 2:
                act.wait_ge(s["pt_ready"], u - 1)
            act.activation(probs[:, u % 2, :], bank(3 + u % 2), ACT.Exp, bias=small[:, SM_NM + u:SM_NM + u + 1],
                           scale=HD ** -0.5, accum_out=small[:, SM_SUM + u:SM_SUM + u + 1]).then_inc(s["probs_ready"], 1)
            if u >= 1:
                take_turned(u - 1)
            if u % 8 == 7:
                og = u // 8
                act.wait_ge(s["esink_in"], og + 1)
                act.activation(small[:, SM_ES + 8 * og:SM_ES + 8 * og + 8], small[:, SM_ES + 8 * og:SM_ES + 8 * og + 8],
                               ACT.Exp).then_inc(s["esink_ready"], 1)
        take_turned(NU - 1)
        for og in range(4):
            act.wait_ge(s["pt_ready"], NU + og + 1)
            act.activation(oT[:, 4 * (og % 2):4 * (og % 2) + 4, (og // 2) * P:(og // 2 + 1) * P],
                           bank(5 + og % 2).rearrange("p (k t) -> p k t", k=4), ACT.Copy).then_inc(s["pt_taken"], 1)

        def take_row(dst, banks, n):
            for f in range(2):
                act.wait_ge(s["row_ready"], n + f + 1)
                act.activation(dst[:, 512 * f:512 * f + 512], bank(banks[f]), ACT.Copy).then_inc(s["row_taken"], 1)

        take_row(g_row, (0, 7), 0)
        for b in range(TB):
            act.wait_ge(s["wo_ready"], 2 * b + 2)
            y = ps[:, (3, 1)[b]:(3, 1)[b] + 2, :]
            if b == 1:
                act.wait_ge(s["y_normed"], 1)
            squares(NORM_Y + 2 * b, [(y, y_tmp[:].rearrange("p (a n) -> p a n", a=2))])
            root(NORM_Y + 2 * b)
            act.wait_ge(s["y_normed"], b + 1)
            squares(NORM_Y + 2 * b + 1, [(tok[:, b, :], xn[:, b, :])])
            root(NORM_Y + 2 * b + 1)

        def dense_hi(k, st):
            act.wait_ge(s[f"f_in{k}"], (st + 1) * (32 if k < 2 else 16))
            if k == 2:
                act.wait_ge(s["f_used2"], st + 1)
            elif not (isinstance(st, int) and st == 0):
                act.wait_ge(s[f"f_used{k}"], st)
            act.activation(f_hi[k][:], f_raw[k][:], ACT.Copy).then_inc(s[f"f_hi{k}"], 1)

        def dense_silu(st):
            act.wait_ge(s["f_used1"], st + 1)
            act.wait_ge(s["f_turned"], st + 1)
            act.activation(f_act[:], ps[:, 1:3, 0:FS], ACT.Silu).then_inc(s["f_silu"], 1)

        def dense_turned_hi(st):
            act.wait_ge(s["f_turned"], st + 2)
            act.wait_ge(s["f_used2"], st + 1)
            act.activation(fT_hi[:].rearrange("p q b t -> p (q b t)"), bank(7), ACT.Copy).then_inc(s["f_thi"], 1)

        dense_hi(0, 0)
        for half in range(2):
            act.wait_ge(s["turned_taken"], 8 + 2 * half + 2)
            act.activation(hf_hi[:, 4 * half:4 * half + 4, :], hf[:, 4 * half:4 * half + 4, :],
                           ACT.Copy).then_inc(s["hf_hi_ready"], 1)
        dense_hi(1, 0)
        act.wait_ge(s["y_normed"], 2)
        take_row(g_row, (0, 7), 2)

        def dense_iteration(st, first=False, last=False):
            if not first:
                dense_turned_hi(st - 1)
            if not last:
                dense_hi(0, st + 1)
            dense_silu(st)
            if not last:
                dense_hi(1, st + 1)
            dense_hi(2, st)

        dense_iteration(0, first=True)
        with act.Fori(1, FSTEPS - 1) as st:
            dense_iteration(st)
        dense_iteration(FSTEPS - 1, last=True)
        dense_turned_hi(FSTEPS - 1)

        take_row(mod_rows[:, 0, :], (1, 2), 4)
        take_row(mod_rows[:, 1, :], (1, 2), 6)
        take_row(g1m_row, (1, 2), 8)
        act.wait_ge(s["f_used2"], FSTEPS + 1)
        squares(NORM_F, [(ps[:, 3 + 2 * b:5 + 2 * b, :], xn[:, b, :].rearrange("p (a n) -> p a n", a=2))
                         for b in range(TB)])
        root(NORM_F)
        act.wait_ge(s["y_normed"], 4)
        squares(NORM_POOL_PRE, [(tok[:, b, :], xn[:, b, :]) for b in range(TB)])
        root(NORM_POOL_PRE)

        def expert_hi(k, step):
            act.wait_ge(s[f"m_in{k}"], (step + 1) * 16)
            if k >= 4:
                act.wait_ge(s[f"m_used{k}"], step + 1)
            elif not (isinstance(step, int) and step == 0):
                act.wait_ge(s[f"m_used{k}"], step)
            act.activation(m_hi[k][:], m_raw[k][:], ACT.Copy).then_inc(s[f"m_hi{k}"], 1)

        for k in (0, 1):
            expert_hi(k, 0)
        for f in range(4):
            act.wait_ge(s["pooled"], f + 1)
            act.activation(dT[:, 2 * f:2 * f + 2, :], bank((7, 0)[f % 2]).rearrange("p (k t) -> p k t", k=2),
                           ACT.Copy).then_inc(s["pooled_taken"], 1)
        for k in (2, 3):
            expert_hi(k, 0)
        act.wait_ge(s["poolbias_ready"], 2 * TB)
        squares(NORM_POOL, [(pool_y[:, b, :], sq_junk[:, b, :]) for b in range(TB)])
        root(NORM_POOL)
        act.wait_ge(s["y_normed"], 6)
        squares(NORM_MOE_PRE, [(tok[:, b, :], sq_junk[:, b, :]) for b in range(TB)])
        root(NORM_MOE_PRE)
        act.wait_ge(s["diff_ready"], 1)
        act.activation(route[:, R_EX:R_EX + 2], route[:, R_D:R_D + 2], ACT.Exp).then_inc(s["exp_ready"], 1)

        def tokens_hi(j):
            act.wait_ge(s["xs_ready"], j + 1)
            act.activation(xs_hi[:], xs_full[:], ACT.Copy).then_inc(s["xs_hi_ready"], 1)

        def expert_silu(step):
            act.wait_ge(s["m_used3"], step + 1)
            act.wait_ge(s["m_turned"], step + 1)
            act.activation(m_act[:], bank(1), ACT.Silu).then_inc(s["m_silu"], 1)

        def expert_turned_hi(step):
            act.wait_ge(s["m_turned"], step + 2)
            act.wait_ge(s["m_used5"], step + 1)
            act.activation(mT_hi[:].rearrange("p q t -> p (q t)"), bank(7), ACT.Copy).then_inc(s["m_thi"], 1)

        def iteration(step, first=False, ahead=True):
            if ahead:
                expert_hi(0, step + 1)
                expert_hi(1, step + 1)
            if not first:
                expert_turned_hi(step - 1)
            if ahead:
                expert_hi(2, step + 1)
            expert_silu(step)
            if ahead:
                expert_hi(3, step + 1)
            expert_hi(4, step)
            expert_hi(5, step)

        def job(j, last):
            step = j * MSTEPS
            iteration(step, first=True)
            with act.Fori(1, MSTEPS - 1) as i:
                iteration(step + i)
            end = step + MSTEPS - 1
            iteration(end, ahead=not last)
            expert_turned_hi(end)
            if not last:
                act.wait_ge(s["m_used3"], end + 1)
                tokens_hi(j + 1)
            act.wait_ge(s["m_used5"], end + 2)
            act.wait_ge(s["scattered"], 4 * j + 4)
            act.activation(y_slots[:].rearrange("p (a n) -> p a n", a=2), ps[:, 3:5, :],
                           ACT.Copy).then_inc(s["y_taken"], 1)

        act.wait_ge(s["route_ready"], 1)
        last_job = act.value_load(jobs_i[0:1, 15:16], min_val=E - 1, max_val=MAX_JOBS - 1)
        tokens_hi(0)
        with act.Fori(0, last_job) as j:
            job(j, False)
        j = last_job
        job(j, True)
        take_row(xs_full[:].rearrange("p k t -> p (k t)"), (5, 6), 10)
        act.wait_ge(s["acc_added"], 4 * j + 8)
        squares(NORM_LAST, [(acc[:, b, :], xm[:, b, :]) for b in range(TB)])
        root(NORM_LAST)

    @block.vector
    def _(dve):
        done = Done(dve)
        step_ = s["dve_step"]
        for k in range(6):
            dve.sem_inc(s[f"m_split{k}"], 1)
        dve.sem_inc(s["m_act_ready"], 1)
        dve.sem_inc(s["m_tlo"], 1)

        def inverse_root(n):
            dve.wait_ge(s["sumsq_ready"], SUMS_UNTIL[n])
            dve.tensor_scalar(stat(n, 1), stat(n, 0), 1.0 / D, EPS, ALU.mult, ALU.add).then_inc(s["msq_ready"], 1)
            dve.wait_ge(s["sqrt_ready"], n + 1)
            done(dve.reciprocal(stat(n, 3), stat(n, 2)), s["rstd_ready"])

        dve.wait_ge(s["cols_turned"], 1)
        done(dve.tensor_copy(cols[:, 0:N_M0], ps[:, 0, 0:N_M0]), s["cols_ready"])
        dve.wait_ge(s["sink_in"], 16)
        done(dve.tensor_scalar(col(N_NSINK, H), col(N_SINK, H), -1.0, None, ALU.mult), s["nsink_ready"])
        inverse_root(NORM_LAT)
        for b in range(TB):
            done(dve.tensor_scalar(xn[:, b, :], tok[:, b, :], stat(NORM_LAT, 3)[:, b:b + 1], None, ALU.mult),
                 s["xn_ready"], wait=False)
        inverse_root(NORM_CTX)
        for b in range(CB):
            done(dve.tensor_scalar(ctx_tok[:, b, :], ctx_tok[:, b, :], stat(NORM_CTX, 3)[:, b:b + 1], None, ALU.mult),
                 s["xn_ready"], wait=False)

        def scale_column(at, scale, gain_col, sem=step_):
            done(dve.scalar_tensor_tensor(col(at, KC), scale, 1.0, gain_col, ALU.add, ALU.mult), sem)

        dve.wait_ge(s["ada_used"], PE_PIECES)
        got = ps[:, 0, 0:4 * KC].rearrange("p (n a) -> p a n", a=2)
        for a, at in ((0, N_M0), (1, N_MC)):
            done(dve.tensor_tensor(col(at, 2 * KC), got[:, a, :], col(N_B, 2 * KC), ALU.add), step_)
        scale_column(N_A, col(N_M0 + KC, KC), gain(0, 0))
        scale_column(N_A + KC, col(N_MC + KC, KC), gain(0, 0), s["a_ready"])

        taken = [0]

        def take_turned(dst, a, shift):
            for f in range(4):
                n = taken[0]
                taken[0] += 1
                dve.wait_ge(s["turn_ready"], n + 1)
                for k in range(2):
                    kc = 2 * f + k
                    ins = dve.tensor_scalar(dst[:, kc, :], ps[:, FILL_BANKS[n % 2], k * T:(k + 1) * T],
                                            cols[:, a + kc:a + kc + 1], cols[:, shift + kc:shift + kc + 1], ALU.mult, ALU.add)
                done(ins, s["turned_taken"], wait=False)

        take_turned(hT, N_A, N_M0)
        take_turned(hcT, N_A + KC, N_MC)

        def take_columns(q):
            dve.wait_ge(s["colsum_ready"], q + 1)
            if isinstance(q, int):
                at = (N_M0 + 16 + 4 * q) if q < 8 else N_M1 + 4 * (q - 8)
                bias = N_B + 16 + 4 * q
                dst, src = col(at, 4), col(bias, 4)
            else:
                dst, src = cols[:, bass.ds(q * 4 + (N_M1 - 32), 4)], cols[:, bass.ds(q * 4 + (N_B + 16), 4)]
            dve.tensor_tensor(dst, ps[:, 0, 0:4], src, ALU.add).then_inc(s["mod_ready"], 1)

        def sum_piece(q, w):
            for k in range(KC):
                v = cols[:, N_SC + 2 * k:N_SC + 2 * k + 1]
                if k == 0:
                    ins = dve.tensor_scalar(ada_acc[:], w[:, k, :], v, None, ALU.mult)
                else:
                    ins = dve.scalar_tensor_tensor(ada_acc[:], w[:, k, :], v, ada_acc[:], ALU.mult, ALU.add)
                ins.then_inc(s["acc_ready"], 1)
                dve.wait_ge(s["acc_ready"], q * KC + k + 1)

        def early_piece(q):
            if q >= 1:
                take_columns(q - 1)
            i = q + PE_PIECES
            dve.wait_ge(s[f"ada_in{i % 3}"], 16 * (i // 3 + 1))
            sum_piece(q, ada_ring[i % 3])

        def rope(src, b, heads, dsts, sem, wait=True):
            def table(t, part=None):
                v = t.rearrange("p (x a r) -> p x a r", x=2, a=2)
                return v if part is None else v[:, :, part:part + 1, :]
            w = heads * HD
            xv = src.rearrange("p (h x a r) -> p h x a r", h=heads, x=2, a=2)
            av = rope_a[:, 0:w].rearrange("p (h d) -> p h d", h=heads)
            bv = rope_b[:, 0:w].rearrange("p (h x a r) -> p h x a r", h=heads, x=2, a=2)
            done(dve.tensor_tensor(av, src.rearrange("p (h d) -> p h d", h=heads),
                                   cos_of(b).unsqueeze(1).to_broadcast([P, heads, HD]), ALU.mult), step_, wait=False)
            sn = sin_of(b).rearrange("p (x a r) -> p x a r", x=2, a=2)
            for part in range(2):
                for half in range(2):
                    ins = dve.tensor_tensor(bv[:, :, half, part, :], xv[:, :, half, 1 - part, :],
                                            sn[:, half, part, :].unsqueeze(1).to_broadcast([P, heads, ROPE_HALF]), ALU.mult)
            done(ins, step_)
            for n, dst in enumerate(dsts):
                ins = dve.tensor_tensor(dst, av, rope_b[:, 0:w].rearrange("p (h d) -> p h d", h=heads), ALU.add)
            done(ins, sem, wait)

        UNITS = [("kv", 0), ("kv", 1), None, None, (0, 0), (1, 0), (0, 1), (1, 1)]
        for u, what in enumerate(UNITS):
            if what is not None:
                dve.wait_ge(s["qkv_ready"], u + 1)
                src = bank(3 + u % 4)
                if what[0] == "kv" and u < 2:
                    b = what[1]
                    done(dve.tensor_copy(v_tok[:, b, :], src[:, KVD:2 * KVD]), step_, wait=False)
                    rope(src[:, 0:KVD], b, HKV, [k_tok[:, b, :, i, :] for i in range(2)], s["kv_lat_taken"])
                else:
                    b, n = what
                    rope(src, b, 8, [q_tok[:, b, 512 * n:512 * n + 512].rearrange("p (h d) -> p h d", h=8)], s["q_taken"])
            early_piece(u)

        NU = TB * H
        OB = [7, 1, 2, 7]

        def normalise(og):
            c8 = slice(8 * og, 8 * og + 8)
            part = lambda at: small[:, at + 8 * og:at + 8 * og + 8]
            dve.wait_ge(s["esink_ready"], og + 1)
            done(dve.tensor_tensor(part(SM_DEN), part(SM_SUM), part(SM_ES), ALU.add), step_)
            done(dve.reciprocal(part(SM_RDEN), part(SM_DEN)), step_)
            dve.wait_ge(s["pv_ready"], 8 * (og + 1))
            b, half = divmod(og, 2)
            done(dve.tensor_tensor(o_tok[:, b, 512 * half:512 * half + 512].rearrange("p (h d) -> p h d", h=8),
                                   bank(OB[og]).rearrange("p (h d) -> p h d", h=8),
                                   part(SM_RDEN).unsqueeze(2).to_broadcast([P, 8, HD]), ALU.mult), s["o_taken"], wait=False)

        for u in range(NU):
            h = u % H
            dve.wait_ge(s["scores_ready"], u + 1)
            done(dve.tensor_reduce(small[:, SM_MAX + u:SM_MAX + u + 1], bank(3 + u % 2), AX.X, ALU.max), s["max_ready"])
            done(dve.tensor_scalar(small[:, SM_NM + u:SM_NM + u + 1], small[:, SM_MAX + u:SM_MAX + u + 1], -(HD ** -0.5),
                                   cols[:, N_NSINK + h:N_NSINK + h + 1], ALU.mult, ALU.min), s["nmax_ready"], wait=(u % 8 == 7))
            if u % 8 == 7:
                og = u // 8
                h0 = 8 * (og % 2)
                done(dve.tensor_tensor(small[:, SM_ES + 8 * og:SM_ES + 8 * og + 8], small[:, SM_NM + 8 * og:SM_NM + 8 * og + 8],
                                       col(N_SINK + h0, 8), ALU.add), s["esink_in"], wait=False)
            if u % 8 == 3 and u > 8:
                normalise(u // 8 - 1)
            if u == NU // 2:
                early_piece(EARLY - 1)
        take_columns(EARLY - 1)
        done.n[s["mod_ready"]] = EARLY
        dve.wait_ge(s["mod_ready"], EARLY)
        scale_column(N_A + 2 * KC, col(N_M0 + 4 * KC, KC), gain(0, 2), s["a_ready"])
        done(dve.tensor_tensor(col(N_G + KC, KC), col(N_M0 + 5 * KC, KC), gain(0, 3), ALU.mult), step_)
        done(dve.tensor_tensor(col(N_G, KC), col(N_M0 + 2 * KC, KC), gain(0, 1), ALU.mult), s["a_ready"])
        normalise(3)

        def add_normed(n, b, y, row, scratch, rstd):
            done(dve.scalar_tensor_tensor(scratch, y, rstd, row, ALU.mult, ALU.mult), step_)
            done(dve.tensor_tensor(tok[:, b, :], tok[:, b, :], y_flat(scratch), ALU.add), s["y_normed"])

        def two(v):
            return v.rearrange("p (a n) -> p a n", a=2)

        def y_flat(v):
            return v if len(v.shape) == 2 else v.rearrange("p a n -> p (a n)")

        dve.wait_ge(s["row_taken"], 2)
        for b in range(TB):
            inverse_root(NORM_Y + 2 * b)
            first = (3, 1)[b]
            add_normed(NORM_Y, b, ps[:, first:first + 2, :], two(g_row[:]), two(y_tmp[:]), stat(NORM_Y + 2 * b, 3))
            inverse_root(NORM_Y + 2 * b + 1)
            done(dve.tensor_scalar(xn[:, b, :], tok[:, b, :], stat(NORM_Y + 2 * b + 1, 3), None, ALU.mult),
                 s["xn_ready"], wait=False)

        def dense_lo(k, st):
            dve.wait_ge(s[f"f_hi{k}"], st + 1)
            dve.tensor_tensor(f_lo[k][:], f_raw[k][:], f_hi[k][:].bitcast(F32), ALU.subtract).then_inc(s[f"f_split{k}"], 1)

        dense_lo(0, 0)
        take_turned(hf, N_A + 2 * KC, N_M0 + 3 * KC)
        for half in range(2):
            dve.wait_ge(s["hf_hi_ready"], half + 1)
            part = slice(4 * half, 4 * half + 4)
            dve.tensor_tensor(hf_lo[:, part, :], hf[:, part, :], hf_hi[:, part, :].bitcast(F32),
                              ALU.subtract).then_inc(s["hf_ready"], 1)
        dense_lo(1, 0)

        def dense_turned_lo(st):
            dve.wait_ge(s["f_thi"], st + 1)
            dve.tensor_tensor(fT_lo[:].rearrange("p q b t -> p (q b t)"), bank(7),
                              fT_hi[:].rearrange("p q b t -> p (q b t)").bitcast(F32), ALU.subtract).then_inc(s["f_tlo"], 1)

        def dense_iteration(st, first=False, last=False):
            if not first:
                dense_turned_lo(st - 1)
            if not last:
                dense_lo(0, st + 1)
            dve.wait_ge(s["f_silu"], st + 1)
            dve.tensor_tensor(f_act[:], f_act[:], ps[:, 1:3, FS:2 * FS], ALU.mult).then_inc(s["f_act_ready"], 1)
            if not last:
                dense_lo(1, st + 1)
            dense_lo(2, st)
            if not first:
                take_columns(st + EARLY - 1)
            dve.wait_ge(s["ada_late_in"], (st + 1) * 16)
            sum_piece(st + EARLY, ada_ring[0])

        dense_iteration(0, first=True)
        with dve.Fori(1, FSTEPS - 1) as st:
            dense_iteration(st)
        dense_iteration(FSTEPS - 1, last=True)
        dense_turned_lo(FSTEPS - 1)
        take_columns(EARLY + L1_LATE - 1)
        dve.wait_ge(s["mod_ready"], EARLY + L1_LATE)
        scale_column(N_A + 3 * KC, col(N_M1 + KC, KC), gain(1, 0))
        scale_column(N_A + 4 * KC, col(N_M1 + 4 * KC, KC), gain(1, 2))
        done(dve.tensor_tensor(col(N_G + 3 * KC, KC), col(N_M1 + 5 * KC, KC), gain(1, 3), ALU.mult), step_)
        done(dve.tensor_tensor(col(N_G + 2 * KC, KC), col(N_M1 + 2 * KC, KC), gain(1, 1), ALU.mult), s["a_ready"])

        dve.wait_ge(s["row_taken"], 4)
        inverse_root(NORM_F)
        for b in range(TB):
            add_normed(NORM_F, b, ps[:, 3 + 2 * b:5 + 2 * b, :], two(g_row[:]), two(y_tmp[:]), stat(NORM_F, 3)[:, b:b + 1])
        inverse_root(NORM_POOL_PRE)
        dve.wait_ge(s["row_taken"], 8)
        for b in range(TB):
            done(dve.scalar_tensor_tensor(h_tok[:, b, :], tok[:, b, :], stat(NORM_POOL_PRE, 3)[:, b:b + 1], mod_rows[:, 0, :],
                                          ALU.mult, ALU.mult), step_)
            done(dve.tensor_tensor(h_tok[:, b, :], h_tok[:, b, :], mod_rows[:, 1, :], ALU.add), s["xn_ready"], wait=False)

        def expert_lo(k, step):
            dve.wait_ge(s[f"m_hi{k}"], step + 1)
            dve.tensor_tensor(m_lo[k][:], m_raw[k][:], m_hi[k][:].bitcast(F32), ALU.subtract).then_inc(s[f"m_split{k}"], 1)

        for k in range(4):
            expert_lo(k, 0)
        for b in range(TB):
            dve.wait_ge(s["poolmix_ready"], b + 1)
            done(dve.tensor_tensor(two(pool_y[:, b, :]), ps[:, 3 + 2 * b:5 + 2 * b, :], two(pool_b_row[:]), ALU.add),
                 s["poolbias_ready"])
            done(dve.tensor_tensor(pool_y[:, b, :], pool_y[:, b, :], pool_s_row[:], ALU.mult), s["poolbias_ready"])
        done(dve.memset(acc[:], 0.0), step_, wait=False)
        dve.wait_ge(s["row_taken"], 10)
        inverse_root(NORM_POOL)
        for b in range(TB):
            add_normed(NORM_POOL, b, pool_y[:, b, :], g1m_row[:], pool_y[:, b, :], stat(NORM_POOL, 3)[:, b:b + 1])
        inverse_root(NORM_MOE_PRE)
        for b in range(TB):
            done(dve.tensor_scalar(xm[:, b, :], tok[:, b, :], stat(NORM_MOE_PRE, 3)[:, b:b + 1], None, ALU.mult),
                 s["xn_ready"], wait=False)
        take_turned(hr, N_A + 4 * KC, N_M1 + 3 * KC)

        def r(at, n=E):
            return route[:, at:at + n]

        def both(at):
            return route[:, at:at + 2 * E].rearrange("p (b e) -> p b e", b=TB)

        done(dve.memset(job_table[:], -1.0), step_)
        done(dve.memset(jobs_f[:], 0.0), step_)
        dve.wait_ge(s["router_ready"], 1)
        for b in range(TB):
            done(dve.tensor_tensor(r(R_L + b * E), ps[:, 7, b * E:(b + 1) * E], col(N_RB, E), ALU.add), step_)
            done(dve.max(r(R_TOP + b * E), r(R_L + b * E)), step_)
            done(dve.max_index(top_i[:, b * E:(b + 1) * E], r(R_TOP + b * E), r(R_L + b * E)), step_)
        done(dve.tensor_copy(r(R_TOPI, 2 * E), top_i[:]), step_)
        done(dve.tensor_tensor(route[:, R_D:R_D + 2], both(R_TOP)[:, :, 1], both(R_TOP)[:, :, 0], ALU.subtract), s["diff_ready"])
        dve.wait_ge(s["exp_ready"], 1)
        done(dve.tensor_scalar(route[:, R_DEN:R_DEN + 2], route[:, R_EX:R_EX + 2], 1.0, None, ALU.add), step_)
        done(dve.reciprocal(route[:, R_G1:R_G1 + 2], route[:, R_DEN:R_DEN + 2]), step_)
        done(dve.tensor_tensor(route[:, R_G2:R_G2 + 2], route[:, R_EX:R_EX + 2], route[:, R_G1:R_G1 + 2], ALU.mult), step_)
        experts = ct[:, K_IOTA:K_IOTA + E]
        for b in range(TB):
            for n, at in ((0, R_H1), (1, R_H2)):
                i = R_TOPI + b * E + n
                done(dve.tensor_scalar(r(at), experts, route[:, i:i + 1], None, ALU.is_equal), step_)
            done(dve.tensor_scalar(r(R_GATE + b * E), r(R_H1), route[:, R_G1 + b:R_G1 + b + 1], None, ALU.mult), step_)
            done(dve.scalar_tensor_tensor(r(R_GATE + b * E), r(R_H2), route[:, R_G2 + b:R_G2 + b + 1], r(R_GATE + b * E),
                                          ALU.mult, ALU.add), step_)
            done(dve.tensor_tensor(r(R_MASK + b * E), r(R_H1), r(R_H2), ALU.add), step_ if b == 0 else s["mask_ready"])
        dve.wait_ge(s["ranks_ready"], 1)
        done(dve.scalar_tensor_tensor(r(R_POS, 2 * E), ps[:, 0, 0:2 * E], 1.0, r(R_MASK, 2 * E), ALU.add, ALU.mult), step_)
        done(dve.tensor_scalar(r(R_POS, 2 * E), r(R_POS, 2 * E), -1.0, None, ALU.add), step_)
        done(dve.tensor_copy(r(R_CNT), ps[:, 0, 2 * E:3 * E]), step_)
        done(dve.tensor_scalar(r(R_OVER), r(R_CNT), float(SLOTS), None, ALU.is_gt), step_)
        done(dve.memset(r(R_RANK), 0.0), step_)
        for e in range(1, E):
            done(dve.tensor_tensor(r(R_RANK + e, 1), r(R_RANK + e - 1, 1), r(R_OVER + e - 1, 1), ALU.add), step_)
        done(dve.tensor_copy(job_table[:, 0:2, 0:E], both(R_POS)), step_)
        done(dve.tensor_copy(job_table[:, 2:4, 0:E], both(R_GATE)), step_)
        done(dve.tensor_copy(jobs_f[:, 0:E], experts), step_)
        done(dve.tensor_scalar(r(R_TMP, 2 * E), r(R_POS, 2 * E), -float(SLOTS), None, ALU.add), step_)

        def pick(dst, what, n):
            done(dve.tensor_tensor_reduce(r(R_JUNK), r(R_SEL + n * E), what, 1.0, 0.0, ALU.mult, ALU.add, dst), step_)

        for n in range(MAX_JOBS - E):
            done(dve.scalar_tensor_tensor(r(R_SEL + n * E), r(R_RANK), float(n), r(R_OVER), ALU.is_equal, ALU.mult), step_)
            pick(jobs_f[:, E + n:E + n + 1], experts, n)
            for b in range(TB):
                pick(job_table[:, b, E + n:E + n + 1], r(R_TMP + b * E), n)
                pick(job_table[:, TB + b, E + n:E + n + 1], r(R_GATE + b * E), n)
        done(dve.tensor_reduce(r(R_JUNK, 1), r(R_OVER), AX.X, ALU.add), step_)
        done(dve.tensor_scalar(jobs_f[:, 15:16], r(R_JUNK, 1), float(E - 1), None, ALU.add), step_)
        done(dve.tensor_copy(jobs_i[:], jobs_f[:]), s["route_ready"])
        last_job = dve.value_load(jobs_i[0:1, 15:16], min_val=E - 1, max_val=MAX_JOBS - 1)

        def job_column(j, count):
            dve.tensor_copy(job_col[:], job_table[:, :, bass.ds(j, 1)] if not isinstance(j, int) else job_table[:, :, j]
                            ).then_inc(s["job_col_ready"], 1)
            dve.wait_ge(s["job_col_ready"], count)

        def one_hot():
            for b in range(TB):
                ins = dve.tensor_scalar(hot[:, b, :], iota, job_col[:, b:b + 1], None, ALU.is_equal)
            ins.then_inc(s["hot_ready"], 1)

        def tokens(j):
            dve.wait_ge(s["gathered"], j + 1)
            for k in range(KC):
                a, b = N_A + 4 * KC + k, N_M1 + 3 * KC + k
                ins = dve.tensor_scalar(xs_full[:, k, :], ps[:, 5 + k // 4, (k % 4) * P:(k % 4 + 1) * P],
                                        cols[:, a:a + 1], cols[:, b:b + 1], ALU.mult, ALU.add)
            ins.then_inc(s["xs_ready"], 1)
            dve.wait_ge(s["xs_hi_ready"], j + 1)
            dve.tensor_tensor(xs_lo[:], xs_full[:], xs_hi[:].bitcast(F32), ALU.subtract).then_inc(s["xs_split"], 1)

        def add_piece(j, n):
            b, half = divmod(n, 2)
            dve.wait_ge(s["scattered"], 4 * j + n + 1)
            part = acc[:, b, 512 * half:512 * half + 512]
            dve.tensor_tensor(part, part, bank((5, 6, 0, 5)[n]), ALU.add).then_inc(s["acc_added"], 1)

        def expert_turned_lo(step):
            dve.wait_ge(s["m_thi"], step + 1)
            dve.tensor_tensor(mT_lo[:].rearrange("p q t -> p (q t)"), bank(7),
                              mT_hi[:].rearrange("p q t -> p (q t)").bitcast(F32), ALU.subtract).then_inc(s["m_tlo"], 1)

        def expert_act(step):
            dve.wait_ge(s["m_silu"], step + 1)
            dve.tensor_tensor(m_act[:], m_act[:], bank(2), ALU.mult).then_inc(s["m_act_ready"], 1)

        def iteration(step, first=False, ahead=True, before=None, after=None):
            if ahead:
                expert_lo(0, step + 1)
                expert_lo(1, step + 1)
            if not first:
                expert_turned_lo(step - 1)
            if before:
                before()
            if ahead:
                expert_lo(2, step + 1)
            expert_act(step)
            if after:
                after()
            if ahead:
                expert_lo(3, step + 1)
            expert_lo(4, step)
            expert_lo(5, step)

        def job(j, last):
            step = j * MSTEPS

            def adds():
                for n in range(3):
                    add_piece(j, n)
                job_column(j, 2 * j + 2)
                for b in range(TB):
                    ins = dve.tensor_scalar(hot_g[:, b, :], iota, job_col[:, b:b + 1], job_col[:, TB + b:TB + b + 1],
                                            ALU.is_equal, ALU.mult)
                ins.then_inc(s["hotg_ready"], 1)

            def turned():
                add_piece(j, 3)
                dve.wait_ge(s["hotg_turned"], j + 1)
                dve.tensor_copy(hotT[:].rearrange("p b t -> p (b t)"), ps[:, 6, 0:TB * P]).then_inc(s["hotT_ready"], 1)
                job_column(j + 1, 2 * j + 3)
                dve.wait_ge(s["gathered"], j + 1)
                one_hot()

            iteration(step, first=True)
            iteration(step + 1, before=adds, after=turned)
            with dve.Fori(2, MSTEPS - 1) as i:
                iteration(step + i)
            end = step + MSTEPS - 1
            iteration(end, ahead=not last)
            expert_turned_lo(end)
            if not last:
                tokens(j + 1)

        done(dve.memset(y_slots[:], 0.0), s["y_taken"], wait=False)
        done(dve.memset(hotT[:], 0.0), s["hotT_ready"], wait=False)
        job_column(0, 1)
        one_hot()
        tokens(0)
        with dve.Fori(0, last_job) as j:
            job(j, False)
        j = last_job
        job(j, True)
        for n in range(4):
            add_piece(j + 1, n)
        dve.wait_ge(s["row_taken"], 12)
        inverse_root(NORM_LAST)
        last_row = xs_full[:].rearrange("p k t -> p (k t)")
        for b in range(TB):
            done(dve.scalar_tensor_tensor(acc[:, b, :], acc[:, b, :], stat(NORM_LAST, 3)[:, b:b + 1], last_row,
                                          ALU.mult, ALU.mult), step_)
            done(dve.tensor_tensor(tok[:, b, :], tok[:, b, :], acc[:, b, :], ALU.add), s["tok_ready"], wait=False)

    block.__exit__(None, None, None)


_INS = ['x', 'c', 'ctx', 'c_ctx', 'ada_w', 'ada_b', 'norm_g', 'attn_w_qkv', 'attn_w_o', 'attn_sink', 'pool_w', 'pool_b',
        'pool_scale', 'ffn_w_gu', 'ffn_w_down', 'router_w', 'router_b', 'moe_w_gu', 'moe_w_down']


def kernel(**inputs):
    import concourse.bacc as bacc
    from concourse.bass_utils import run_bass_kernel_spmd

    nc = bacc.Bacc("TRN2", target_bir_lowering=False, num_devices=1)
    arrays = {f"in_{name}": np.ascontiguousarray(inputs[name]) for name in _INS}
    arrays["in_consts"], arrays["in_pool_m"] = constants()
    args = [nc.dram_tensor(name, a.shape, F32, kind="ExternalInput").ap() for name, a in arrays.items()]
    out = nc.dram_tensor("out_0", (1, T, D), F32, kind="ExternalOutput").ap()
    build(nc, *args, out)
    r = run_bass_kernel_spmd(nc, [arrays], core_ids=[0])
    return np.asarray(r.results[0]["out_0"])
```

```python
from contextlib import ExitStack

import numpy as np

import concourse.bass as bass
from concourse import mybir

P = 128
D = 1024
KC = D // P
T = 256
TB = T // P
C = 256
CB = C // P
H, HKV, HD = 16, 4, 64
GROUP = H // HKV
QD, KVD = H * HD, HKV * HD
KEYS = T + C
WINDOW = 128
GRID_W = 64
ROPE_HALF = HD // 4
POOL_WINDOWS = (2, 4, 8, 16)
NG = len(POOL_WINDOWS)
GD = D // NG
FF = 2816
FS = 256
FSTEPS = FF // FS
E = 8
FE = 3584
MS = 512
MSTEPS = FE // MS
SLOTS = 128
EXTRA = (2 * T) // (SLOTS + 1)
MAX_JOBS = E + EXTRA
EPS = 1e-6
KEY_ORDER = (0, 2, 3, 1)
NEG = -8e30

F32 = mybir.dt.float32
F32R = mybir.dt.float32r
I32 = mybir.dt.int32
U32 = mybir.dt.uint32
ALU = mybir.AluOpType
ACT = mybir.ActivationFunctionType
AX = mybir.AxisListType

K_ID, K_UP, K_IOTA, K_ONE = 0, P, 2 * P, 3 * P
K_COS, K_SIN = 4 * P, 4 * P + TB * HD
K_MASK = K_SIN + TB * HD
K_END = K_MASK + TB * P


def constants():
    t = np.zeros((P, K_END), np.float32)
    t[:, K_ID:K_ID + P] = np.eye(P)
    t[:, K_UP:K_UP + P] = np.arange(P)[:, None] < np.arange(P)[None, :]
    t[:, K_IOTA:K_IOTA + P] = np.arange(P)[None, :]
    t[:, K_ONE:K_ONE + P] = 1.0
    inv = np.float32(10000.0) ** (-np.arange(ROPE_HALF, dtype=np.float32) / np.float32(ROPE_HALF))
    for b in range(TB):
        tok = b * P + np.arange(P)
        for half, pos in enumerate((tok // GRID_W, tok % GRID_W)):
            ang = pos[:, None].astype(np.float32) * inv
            for part, sign in ((0, -1.0), (1, 1.0)):
                at = b * HD + half * 2 * ROPE_HALF + part * ROPE_HALF
                t[:, K_COS + at:K_COS + at + ROPE_HALF] = np.cos(ang)
                t[:, K_SIN + at:K_SIN + at + ROPE_HALF] = sign * np.sin(ang)
        key = (1 - b) * P + np.arange(P)
        t[:, K_MASK + b * P:K_MASK + (b + 1) * P] = np.where(
            np.abs(key[None, :] - tok[:, None]) <= WINDOW, 0.0, NEG)
    pool = np.zeros((T, NG, T), np.float32)
    for g, w in enumerate(POOL_WINDOWS):
        for i in range(T):
            lo, hi = max(i - w // 2, 0), min(i - w // 2 + w, T)
            pool[lo:hi, g, i] = 1.0 / (hi - lo)
            pool[i, g, i] -= 1.0
    pool = np.ascontiguousarray(pool.reshape(TB, P, NG, T).transpose(1, 0, 2, 3)).reshape(P, TB * NG * T)
    return t, pool


class Done:

    def __init__(self, eng):
        self.eng, self.n = eng, {}

    def __call__(self, ins, sem, wait=True):
        self.n[sem] = self.n.get(sem, 0) + 1
        ins.then_inc(sem, 1)
        if wait:
            self.eng.wait_ge(sem, self.n[sem])
        return self.n[sem]


def build(nc, x, c, ctx_in, c_ctx, ada_w, ada_b, norm_g, w_qkv, w_o, sink, pool_w, pool_b, pool_scale,
          ffn_gu, ffn_down, router_w, router_b, moe_gu, moe_down, consts, pool_m, out):
    KB = 1024
    base = (nc.sbuf_base + 63) // 64 * 64

    def sb(name, shape, dt, at):
        return nc.alloc_sbuf_tensor_at(name, [shape[0], *shape[1:]], dt, offset=base + at)

    R0, R1, R2 = 0, 48 * KB, 144 * KB
    wqkv = sb("wqkv", [P, KC, QD + 2 * KVD], F32, R0)
    m_raw = [sb(f"m_raw{k}", [P, 4, MS] if k < 4 else [P, 2, D], F32, R0 + 8 * KB * k) for k in range(6)]
    f_raw = [sb(f"f_raw{k}", [P, 4, 2 * FS] if k < 2 else [P, 2, D], F32, R0 + 24 * KB + 8 * KB * k)
             for k in range(3)]

    wo_sb = sb("wo_sb", [P, KC, D], F32, R1 + 16 * KB)
    q_parts = sb("q_parts", [P, H, T], F32R, R0)
    k_hi = sb("k_hi", [P, HKV, KEYS], F32R, R1)
    k_lo = sb("k_lo", [P, HKV, KEYS], F32R, R1 + 8 * KB)
    ada_ring = [sb(f"ada{i}", [P, KC, 512], F32, R1 + 48 * KB + 16 * KB * i) for i in range(3)]
    f_hi = [sb(f"f_hi{k}", [P, 4, 2 * FS] if k < 2 else [P, 2, D], F32R, R1 + 16 * KB * k) for k in range(3)]
    f_lo = [sb(f"f_lo{k}", [P, 4, 2 * FS] if k < 2 else [P, 2, D], F32R, R1 + 16 * KB * k + 8 * KB)
            for k in range(3)]
    m_hi = [sb(f"m_hi{k}", [P, 4, MS] if k < 4 else [P, 2, D], F32R, R1 + 16 * KB * k) for k in range(6)]
    m_lo = [sb(f"m_lo{k}", [P, 4, MS] if k < 4 else [P, 2, D], F32R, R1 + 16 * KB * k + 8 * KB)
            for k in range(6)]
    last_hi = {k: sb(f"last_hi{k}", [P, 2, D], F32R, R1 + 16 * KB * (k - 4)) for k in (4, 5)}
    last_lo = {k: sb(f"last_lo{k}", [P, 2, D], F32R, R1 + 16 * KB * (k - 4) + 8 * KB) for k in (4, 5)}
    pool_mat = sb("pool_mat", [P, TB, NG, T], F32, R1 + 64 * KB)
    pool_w_sb = sb("pool_w_sb", [P, NG, 2, GD], F32, R1 + 72 * KB)
    pool_b_row = sb("pool_b_row", [P, D], F32, R1 + 80 * KB)
    pool_s_row = sb("pool_s_row", [P, D], F32, R1 + 84 * KB)
    mod_rows = sb("mod_rows", [P, 2, D], F32, R1 + 88 * KB)

    ct = sb("consts_sb", [P, K_END], F32, R2)
    cols = sb("cols", [P, 480], F32, R2 + 4 * KB)
    small = sb("small", [P, 256], F32, R2 + 6 * KB)
    ada_acc0 = sb("ada_acc0", [P, 512], F32, R2 + 7 * KB)
    route = sb("route", [P, 256], F32, R2 + 9 * KB)
    tok = sb("tok", [P, TB, D], F32, R2 + 10 * KB)
    S = [R2 + 18 * KB + 8 * KB * i for i in range(6)]
    ctx_tok = sb("ctx_tok", [P, CB, D], F32, S[0])
    rows_in = sb("rows_in", [P, 2, P], F32, S[5])
    ctx_junk = sb("ctx_junk", [P, 2, D], F32, S[4])
    hT = sb("hT", [P, KC, T], F32, S[1])
    mod_two = sb("mod_two", [2, 4, 512], F32, S[1])
    hcT = sb("hcT", [P, KC, C], F32, S[2])
    xn = sb("xn", [P, 2, D], F32, S[3])
    q_tok = [sb(f"q_tok{b}", [P, H, 2, HD], F32, S[2 * b]) for b in range(TB)]
    rope_a = sb("rope_a", [P, 512], F32, S[3])
    rope_b = sb("rope_b", [P, 512], F32, S[3] + 2 * KB)
    k_tok = sb("k_tok", [P, TB + CB, HKV, 2, HD], F32, S[4])
    v_tok = sb("v_tok", [P, TB + CB, KVD], F32, S[5])
    ada_acc1 = sb("ada_acc1", [P, 512], F32, S[3] + 4 * KB)
    ada_acc2 = sb("ada_acc2", [P, 512], F32, R0 + 16 * KB)
    probs = sb("probs", [P, 2, KEYS], F32, S[3])
    probsT = sb("probsT", [P, 2, KEYS], F32, S[3] + 4 * KB)
    o_tok = sb("o_tok", [P, TB, QD], F32, S[1])
    oT = sb("oT", [P, KC, T], F32, S[2])
    g_row = sb("g_row", [P, D], F32, S[0])
    y_tmp = sb("y_tmp", [P, D], F32, S[0] + 4 * KB)
    hf = sb("hf", [P, KC, T], F32, S[2])
    hf_hi = sb("hf_hi", [P, KC, T], F32R, S[4])
    hf_lo = sb("hf_lo", [P, KC, T], F32R, S[1])
    f_act = sb("f_act", [P, TB, FS], F32, S[3])
    fT_hi = sb("fT_hi", [P, 2, TB, P], F32R, S[3] + 2 * KB)
    fT_lo = sb("fT_lo", [P, 2, TB, P], F32R, S[3] + 4 * KB)
    sq_junk = sb("sq_junk", [P, 2, D], F32, S[0])
    pool_y = sb("pool_y", [P, TB, D], F32, S[3])
    g1m_row = sb("g1m_row", [P, D], F32, S[5])
    h_tok = sb("h_tok", [P, TB, D], F32, S[2])
    dT = sb("dT", [P, KC, T], F32, S[1])
    hr = sb("hr", [P, KC, T], F32, S[2])
    xm = sb("xm", [P, TB, D], F32, S[3])
    acc = sb("acc", [P, TB, D], F32, S[1])
    xs_full = sb("xs_full", [P, KC, SLOTS], F32, S[0])
    y_slots = sb("y_slots", [P, D], F32, S[0] + 4 * KB)
    xs_hi = sb("xs_hi", [P, KC, SLOTS], F32R, S[2])
    xs_lo = sb("xs_lo", [P, KC, SLOTS], F32R, S[2] + 4 * KB)
    m_act = sb("m_act", [P, MS], F32, S[4])
    mT_hi = sb("mT_hi", [P, 4, SLOTS], F32R, S[4] + 2 * KB)
    mT_lo = sb("mT_lo", [P, 4, SLOTS], F32R, S[4] + 4 * KB)
    hot = sb("hot", [P, TB, SLOTS], F32, S[4] + 6 * KB)
    hot_g = sb("hot_g", [P, TB, SLOTS], F32, S[4] + 7 * KB)
    hotT = sb("hotT", [P, TB, P], F32, S[5])
    route_w = sb("route_w", [P, KC, E], F32, S[5] + 4 * KB)
    jobs_i = sb("jobs_i", [P, 16], I32, S[5] + 4 * KB + 256)
    jobs_f = sb("jobs_f", [P, 16], F32, S[5] + 4 * KB + 320)
    job_table = sb("job_table", [P, 4, 12], F32, S[5] + 4 * KB + 384)
    job_col = sb("job_col", [P, 4], F32, S[5] + 4 * KB + 576)
    top_i = sb("top_i", [P, 2 * E], U32, S[5] + 4 * KB + 608)

    ident = ct[:, K_ID:K_ID + P]
    upper = ct[:, K_UP:K_UP + P]
    iota = ct[:, K_IOTA:K_IOTA + P]
    ones = ct[:, K_ONE:K_ONE + P]

    def cos_of(b):
        return ct[:, K_COS + b * HD:K_COS + (b + 1) * HD]

    def sin_of(b):
        return ct[:, K_SIN + b * HD:K_SIN + (b + 1) * HD]

    def col(a, n):
        return cols[:, a:a + n]

    N_GAIN = 0
    N_B = 80
    N_M0, N_MC, N_M1 = 176, 224, 240
    N_SC = 288
    N_A = 304
    N_G = 344
    N_SINK, N_NSINK, N_RB = 376, 392, 408

    def gain(layer, which):
        return col(N_GAIN + 16 + (layer * 4 + which) * KC, KC)

    R_L, R_TOP, R_TOPI = 0, 16, 32
    R_D, R_EX, R_DEN, R_G1, R_G2 = 48, 50, 52, 54, 56
    R_H1, R_H2, R_MASK, R_GATE, R_POS, R_CNT, R_OVER, R_RANK = 64, 80, 96, 112, 128, 144, 152, 160
    R_SEL, R_TMP, R_JUNK = 168, 192, 208

    SM_NM, SM_SUM, SM_MAX, SM_ES, SM_DEN, SM_RDEN = 64, 96, 128, 160, 192, 224

    ps = nc.alloc_psum_tensor("ps", [P, 8, 512], F32)

    def bank(i):
        return ps[:, i, :]

    names = """x_in ctx_in wqkv_in0 wqkv_in1 wqkv_in2 consts_in ada_queued tr2_hi ada_summed ada_rows_taken rows_in sink_in rb_in wo_in ada_in0 ada_in1 ada_in2 ada_late_in
        pool_in cols_turned cols_ready silu_ready ada_used acc_ready colsum_ready mod_ready a_ready nsink_ready
        sumsq_ready msq_ready sqrt_ready rstd_ready dve_step xn_ready turn_ready turned_taken
        qkv_ready kv_lat_taken kv_ctx_taken q_taken q_twice tr2_ready tr2_taken
        scores_ready max_ready nmax_ready probs_ready pt_ready pt_taken pv_ready esink_in esink_ready o_taken
        row_ready row_taken wo_ready y_normed
        f_in0 f_in1 f_in2 f_split0 f_split1 f_split2 f_hi0 f_hi1 f_hi2 f_used0 f_used1 f_used2
        f_silu f_act_ready f_turned f_thi f_tlo hf_hi_ready hf_ready
        pooled pooled_taken poolmix_ready pool_y_ready zeroed
        router_ready diff_ready exp_ready mask_ready ranks_ready route_ready
        m_in0 m_in1 m_in2 m_in3 m_in4 m_in5 m_hi0 m_hi1 m_hi2 m_hi3 m_hi4 m_hi5
        m_split0 m_split1 m_split2 m_split3 m_split4 m_split5 m_used0 m_used1 m_used2 m_used3 m_used4 m_used5
        m_silu m_act_ready m_turned m_thi m_tlo job_col_ready hot_ready gathered xs_ready xs_hi_ready xs_split
        y_taken scattered hotg_ready hotg_turned hotT_ready acc_added tok_ready out_done""".split()
    s = {n: nc.alloc_semaphore(n) for n in names}

    ada_v = ada_w.rearrange("l (k p) n -> l p k n", p=P)
    PIECES = 12
    PE_PIECES = 4
    EARLY = PIECES - PE_PIECES + 2
    MIXER_PIECES = 6
    L1_LATE = PIECES - 2
    assert L1_LATE == FSTEPS - 1
    gu_v = ffn_gu[0].rearrange("(k p) n -> p k n", p=P)
    dn_v = ffn_down[0].rearrange("(s q p) n -> s p q n", p=P, q=FS // P)
    mgu_v = moe_gu[0].rearrange("e (k p) n -> e p k n", p=P)
    mdn_v = moe_down[0].rearrange("e (q p) n -> e p q n", p=P)

    NORM_LAT, NORM_CTX, NORM_Y, NORM_F, NORM_POOL_PRE, NORM_POOL, NORM_MOE_PRE, NORM_LAST = 0, 1, 2, 6, 8, 10, 12, 14
    SUMS = [2, 2] + [1] * 14
    SUMS_UNTIL = [sum(SUMS[:n + 1]) for n in range(len(SUMS))]

    def stat(n, what):
        at = 8 * (n % 8) + 2 * what
        return small[:, at:at + SUMS[n]]

    def acc_of(q):
        if not isinstance(q, int) or q >= EARLY or q % 2 == 0:
            return ada_acc0
        return ada_acc1 if q < MIXER_PIECES else ada_acc2

    block = nc.Block()
    block.__enter__()

    @block.sync
    def _(sp):
        sp.dma_start(rows_in[0:8, 0, :], c.rearrange("a (k p) -> (a k) p", p=P)).then_inc(s["rows_in"], 16)
        sp.dma_start(rows_in[8:16, 0, :], c_ctx.rearrange("(k p) -> k p", p=P)).then_inc(s["rows_in"], 16)
        sp.dma_start(ct[:], consts).then_inc(s["consts_in"], 16)
        sp.dma_start(tok[:], x[0].rearrange("(b p) d -> p b d", p=P)).then_inc(s["x_in"], 16)
        sp.dma_start(ctx_tok[:], ctx_in[0].rearrange("(b p) d -> p b d", p=P)).then_inc(s["ctx_in"], 16)
        sp.dma_start(col(N_SINK, H), sink[0].partition_broadcast(P)).then_inc(s["sink_in"], 16)
        sp.dma_start(col(N_RB, E), router_b[0].partition_broadcast(P)).then_inc(s["rb_in"], 16)
        sp.dma_start(route_w[:], router_w[0].rearrange("(k p) e -> p k e", p=P)).then_inc(s["rb_in"], 16)
        qkv_v = w_qkv[0].rearrange("(k p) n -> p k n", p=P)
        for i, after, value in ((2, "ada_queued", 1), (0, "ada_in1", 32), (1, "ada_in2", 32)):
            sp.wait_ge(s[after], value)
            sp.dma_start(wqkv[:, :, 512 * i:512 * i + 512], qkv_v[:, :, 512 * i:512 * i + 512]).then_inc(s[f"wqkv_in{i}"], 16)
        sp.wait_ge(s["ada_in0"], 48)
        sp.dma_start(wo_sb[:], w_o[0].rearrange("(k p) n -> p k n", p=P)).then_inc(s["wo_in"], 16)

        def dense_step(st):
            for k in range(2):
                if not isinstance(st, int):
                    sp.wait_ge(s[f"f_split{k}"], st)
                for half, at in ((0, 0), (1, FF)):
                    sp.dma_start(f_raw[k][:, :, half * FS:half * FS + FS],
                                 gu_v[:, 4 * k:4 * k + 4, bass.ds(st * FS + at, FS)]).then_inc(s[f"f_in{k}"], 16)
            if not isinstance(st, int):
                sp.wait_ge(s["f_split2"], st)
            sp.dma_start(f_raw[2][:], dn_v[bass.ds(st, 1)].rearrange("a p q n -> p (a q) n")
                         if not isinstance(st, int) else dn_v[st]).then_inc(s["f_in2"], 16)

        sp.wait_ge(s["qkv_ready"], 8)
        dense_step(0)
        with sp.Fori(1, FSTEPS) as st:
            dense_step(st)

        def expert_load(k, e, i, step):
            if not isinstance(step, int):
                sp.wait_ge(s[f"m_split{k}"], step + 1)
            if k < 4:
                src = mgu_v[bass.ds(e, 1), :, 4 * (k % 2):4 * (k % 2) + 4, bass.ds(i * MS + (k // 2) * FE, MS)]
            else:
                src = mdn_v[bass.ds(e, 1), :, bass.ds(i * (MS // P) + 2 * (k - 4), 2), :]
            sp.dma_start(m_raw[k][:], src.rearrange("e p k n -> p (e k) n")).then_inc(s[f"m_in{k}"], 16)

        def job_loads(j, e, e_next):
            step = j * MSTEPS
            with sp.Fori(0, MSTEPS - 1) as i:
                for k in range(4):
                    expert_load(k, e, i + 1, step + i + 1)
                for k in (4, 5):
                    expert_load(k, e, i, step + i)
            if e_next is not None:
                for k in range(4):
                    expert_load(k, e_next, 0, step + MSTEPS)
            for k in (4, 5):
                expert_load(k, e, MSTEPS - 1, step + MSTEPS - 1)

        for k in range(4):
            if k == 3:
                sp.wait_ge(s["f_split0"], FSTEPS)
            expert_load(k, 0, 0, 0)
        for k in (1, 2):
            sp.wait_ge(s[f"f_split{k}"], FSTEPS)
        with sp.Fori(0, E - 2) as j:
            job_loads(j, j, j + 1)
        sp.wait_ge(s["route_ready"], 1)
        last_job = sp.value_load(jobs_i[0:1, 15:16], min_val=E - 1, max_val=MAX_JOBS - 1)
        with sp.Fori(E - 2, last_job) as j:
            e = sp.value_load(jobs_i[0:1, bass.ds(j, 1)], min_val=0, max_val=E - 1)
            e_next = sp.value_load(jobs_i[0:1, bass.ds(j + 1, 1)], min_val=0, max_val=E - 1)
            job_loads(j, e, e_next)
        job_loads(last_job, sp.value_load(jobs_i[0:1, bass.ds(last_job, 1)], min_val=0, max_val=E - 1), None)

        for b in range(TB):
            sp.wait_ge(s["tok_ready"], b + 1)
            sp.dma_start(out[0].rearrange("(b p) d -> p b d", p=P)[:, b, :], tok[:, b, :]).then_inc(s["out_done"], 16)
        sp.wait_ge(s["out_done"], 16 * TB)

    @block.gpsimd
    def _(pool):
        for i in range(PIECES + PIECES - L1_LATE):
            l, n = divmod(i, PIECES)
            if i >= 3:
                if i - 3 < PE_PIECES:
                    pool.wait_ge(s["ada_used"], i - 2)
                else:
                    pool.wait_ge(s["acc_ready"], KC * (i - 2 - PE_PIECES))
            pool.dma_start(ada_ring[i % 3][:], ada_v[l, :, :, 512 * n:512 * n + 512]).then_inc(s[f"ada_in{i % 3}"], 16)
            if i == PE_PIECES - 1:
                pool.sem_inc(s["ada_queued"], 1)
        with pool.Fori(0, L1_LATE) as n:
            pool.wait_ge(s["acc_ready"], (n + EARLY) * KC)
            pool.dma_start(ada_ring[0][:], ada_v[1, :, :, bass.ds(n * 512 + 512 * (PIECES - L1_LATE), 512)]
                           ).then_inc(s["ada_late_in"], 16)
        pool.dma_start(pool_mat[:], pool_m.rearrange("p (b g t) -> p b g t", b=TB, g=NG)).then_inc(s["pool_in"], 16)
        pool.dma_start(pool_w_sb[:], pool_w[0].rearrange("g (k p) n -> p g k n", p=P)).then_inc(s["pool_in"], 16)
        pool.dma_start(pool_b_row[:], pool_b[0].partition_broadcast(P)).then_inc(s["pool_in"], 16)
        pool.dma_start(pool_s_row[:], pool_scale[0].partition_broadcast(P)).then_inc(s["pool_in"], 16)

        pool.wait_ge(s["sqrt_ready"], NORM_MOE_PRE + TB)
        pool.memset(acc[:], 0.0).then_inc(s["zeroed"], 1)
        pool.memset(hotT[:], 0.0).then_inc(s["hotT_ready"], 1)
        pool.memset(y_slots[:], 0.0).then_inc(s["y_taken"], 1)

    FILL_BANKS = (1, 2)

    @block.tensor
    def _(pe):
        for k in (4, 5):
            pe.sem_inc(s[f"m_used{k}"], 1)
        pe.sem_inc(s["f_used2"], 1)
        pe.sem_inc(s["f_turned"], 1)
        pe.sem_inc(s["m_turned"], 1)

        pe.wait_ge(s["rows_in"], 64)
        pe.wait_ge(s["consts_in"], 16)
        pe.transpose(ps[:, 0, 0:80], rows_in[0:80, 0, :], ident[0:80, 0:80])
        pe.transpose(ps[:, 0, 80:176], rows_in[0:96, 1, :], ident[0:96, 0:96]).then_inc(s["cols_turned"], 1)

        pe.wait_ge(s["silu_ready"], 1)

        def mod_columns(i):
            pe.wait_ge(s["ada_rows_taken"], i + 1)
            for n in range(4):
                at = 2 * (4 * i + n)
                mm = pe.transpose(ps[:, 0, at:at + 2], mod_two[:, i, n * P:(n + 1) * P], ident[0:2, 0:2])
            mm.then_inc(s["ada_summed"], 1)

        for i in range(PE_PIECES):
            pe.wait_ge(s[f"ada_in{i % 3}"], 16 * (i // 3 + 1))
            for k in range(KC):
                mm = pe.matmul(ps[0:2, 3 + i, :], cols[:, N_SC + 2 * k:N_SC + 2 * k + 2], ada_ring[i % 3][:, k, :],
                               start=(k == 0), stop=(k == KC - 1))
            mm.then_inc(s["ada_used"], 1)
            if i >= 1:
                mod_columns(i - 1)
        mod_columns(PE_PIECES - 1)

        fills = [0]

        def turn_fill(src, f):
            n = fills[0]
            fills[0] += 1
            if n >= 2:
                pe.wait_ge(s["turned_taken"], n - 1)
            for k in range(2):
                for b in range(2):
                    tr = pe.transpose(ps[:, FILL_BANKS[n % 2], (2 * k + b) * P:(2 * k + b + 1) * P],
                                      src[:, b, (2 * f + k) * P:(2 * f + k + 1) * P], ident)
            tr.then_inc(s["turn_ready"], 1)

        for seq in range(2):
            pe.wait_ge(s["xn_ready"], 2 * seq + 2)
            for f in range(4):
                turn_fill((xn, ctx_tok)[seq], f)

        def column_sums(q):
            pe.wait_ge(s["acc_ready"], (q + 1) * KC)
            if isinstance(q, int) and q == 0:
                pe.wait_ge(s["a_ready"], 1)
            else:
                pe.wait_ge(s["mod_ready"], q)
            for n in range(4):
                mm = pe.matmul(ps[:, 0, n:n + 1], acc_of(q)[:, n * P:n * P + P], ones[:, 0:1], start=True, stop=True)
            mm.then_inc(s["colsum_ready"], 1)

        def turn_keys(g):
            if g >= 2:
                pe.wait_ge(s["tr2_taken"], g - 1)
            else:
                pe.wait_ge(s["turned_taken"], 7 + g)
            if g == 0:
                pe.wait_ge(s["kv_lat_taken"], 2)
                pe.wait_ge(s["kv_ctx_taken"], 2)
            for t in range(4):
                tr = pe.transpose(ps[:, 1 + g % 2, t * P:(t + 1) * P], k_tok[:, KEY_ORDER[t], g, :, :], ident)
            tr.then_inc(s["tr2_ready"], 1)

        UNITS = [("lat", 0, 2), ("lat", 1, 2), ("ctx", 0, 2), ("ctx", 1, 2),
                 ("lat", 0, 0), ("lat", 1, 0), ("lat", 0, 1), ("lat", 1, 1)]
        for u, (seq, b, n) in enumerate(UNITS):
            if u == 0:
                pe.wait_ge(s["turned_taken"], 4)
                pe.wait_ge(s["wqkv_in2"], 16)
            if u == 2:
                pe.wait_ge(s["turned_taken"], 8)
            if u in (4, 6):
                pe.wait_ge(s[f"wqkv_in{n}"], 16)
            if u in (4, 5):
                pe.wait_ge(s["kv_lat_taken"], u - 3)
            if u in (6, 7):
                pe.wait_ge(s["kv_ctx_taken"], u - 5)
            src = hT if seq == "lat" else hcT
            for k in range(KC):
                mm = pe.matmul(bank(3 + u % 4), src[:, k, b * P:(b + 1) * P],
                               wqkv[:, k, 512 * n:512 * n + 512], start=(k == 0), stop=(k == KC - 1))
            mm.then_inc(s["qkv_ready"], 1)
            if u >= 2:
                column_sums(u - 2)
            if u == 6:
                for g in (0, 1):
                    turn_keys(g)

        for g in (2, 3):
            turn_keys(g)
        for f in range(H // 2):
            pe.wait_ge(s["q_twice"], 2 * (f // 4) + 2)
            if f not in (2, 3):
                pe.wait_ge(s["tr2_taken"], 3 + f if f < 2 else 1 + f)
            for k in range(2):
                for b in range(TB):
                    tr = pe.transpose(ps[:, 1 + f % 4, (2 * k + b) * P:(2 * k + b + 1) * P],
                                      q_tok[b][:, 2 * f + k, :, :], ident)
            tr.then_inc(s["tr2_ready"], 1)

        OB = [7, 1, 7, 1]
        SB = [3, 4, 2]

        def scores(u):
            b, h = divmod(u, H)
            g = h // GROUP
            if u >= 3:
                pe.wait_ge(s["probs_ready"], u - 2)
            if u == 0:
                pe.wait_ge(s["tr2_taken"], 12)
                pe.wait_ge(s["q_taken"], 4)
            lhs = q_parts[:, h, b * P:(b + 1) * P]
            other = (3 * P, 0)[b]
            pe.matmul(ps[:, SB[u % 3], other:other + P], ident, ct[:, K_MASK + b * P:K_MASK + (b + 1) * P],
                      start=True, stop=False)
            for at, to in ((other, other + P), ((0, 3 * P), (P, KEYS))[b]):
                pe.matmul(ps[:, SB[u % 3], at:to], lhs, k_hi[:, g, at:to], start=(at != other), stop=False)
                mm = pe.matmul(ps[:, SB[u % 3], at:to], lhs, k_lo[:, g, at:to], start=False, stop=True)
            mm.then_inc(s["scores_ready"], 1)

        def turn_probs(u):
            pe.wait_ge(s["probs_ready"], u + 1)
            if u >= 2:
                pe.wait_ge(s["pt_taken"], u - 1)
            for t in range(4):
                tr = pe.transpose(ps[:, 5 + u % 2, t * P:(t + 1) * P], probs[:, u % 2, t * P:(t + 1) * P], ident)
            tr.then_inc(s["pt_ready"], 1)

        def weigh_values(u):
            b, h = divmod(u, H)
            og = u // 8
            if u in (16, 24):
                pe.wait_ge(s["o_taken"], u // 8 - 1)
            pe.wait_ge(s["pt_taken"], u + 1)
            at = (h % 8) * HD
            for t in range(4):
                mm = pe.matmul(ps[:, OB[og], at:at + HD], probsT[:, u % 2, t * P:(t + 1) * P],
                               v_tok[:, KEY_ORDER[t], (h // GROUP) * HD:(h // GROUP + 1) * HD], start=(t == 0), stop=(t == 3))
            mm.then_inc(s["pv_ready"], 1)

        NU = TB * H
        for u in range(NU + 3):
            if u < NU:
                scores(u)
            if 2 <= u <= NU + 1:
                turn_probs(u - 2)
            if u >= 3:
                weigh_values(u - 3)
            if u % KC == 2 and u > KC:
                column_sums(MIXER_PIECES + u // KC - 1)

        for og in range(4):
            pe.wait_ge(s["o_taken"], og + 1)
            pe.wait_ge(s["pt_taken"], NU - 1 + og)
            for k in range(4):
                tr = pe.transpose(ps[:, 5 + og % 2, k * P:(k + 1) * P],
                                  o_tok[:, og // 2, (4 * (og % 2) + k) * P:(4 * (og % 2) + k + 1) * P], ident)
            tr.then_inc(s["pt_ready"], 1)

        def spread_row(src_col, banks, n):
            for f in range(2):
                if n + f >= 2 and n != 6:
                    pe.wait_ge(s["row_taken"], n + f - 1)
                for k in range(4):
                    v = cols[:, src_col + 4 * f + k:src_col + 4 * f + k + 1].to_broadcast([P, P])
                    mm = pe.matmul(ps[:, banks[f], k * P:(k + 1) * P], v, ident, start=True, stop=True)
                mm.then_inc(s["row_ready"], 1)

        pe.wait_ge(s["a_ready"], 3)
        pe.wait_ge(s["o_taken"], 4)
        spread_row(N_G, (0, 7), 0)

        def turn_block(b):
            pe.wait_ge(s["xn_ready"], 5 + b)
            if b == 1:
                pe.wait_ge(s["y_normed"], 1)
            for half in range(2):
                for k in range(4):
                    tr = pe.transpose(ps[:, 1 + 2 * b + half, k * P:(k + 1) * P],
                                      xn[:, b, (4 * half + k) * P:(4 * half + k + 1) * P], ident)
                tr.then_inc(s["turn_ready"], 1)
                fills[0] += 1

        pe.wait_ge(s["wo_in"], 16)
        for b in range(TB):
            pe.wait_ge(s["pt_taken"], NU + 2 * b + 2)
            for half in range(2):
                for k in range(KC):
                    if (b, half, k) == (1, 1, 3):
                        turn_block(0)
                    mm = pe.matmul(bank(3 + 2 * b + half), oT[:, k, b * P:(b + 1) * P],
                                   wo_sb[:, k, 512 * half:512 * half + 512], start=(k == 0), stop=(k == KC - 1))
                mm.then_inc(s["wo_ready"], 1)

        def gate_up_block(k, b):
            for kk in range(4):
                hi = hf_hi[:, 4 * k + kk, b * P:(b + 1) * P]
                lo = hf_lo[:, 4 * k + kk, b * P:(b + 1) * P]
                first, last = k == 0 and kk == 0, k == 1 and kk == 3
                pe.matmul(bank(1 + b), hi, f_hi[k][:, kk, :], start=first, stop=False)
                pe.matmul(bank(1 + b), hi, f_lo[k][:, kk, :], start=False, stop=False)
                mm = pe.matmul(bank(1 + b), lo, f_hi[k][:, kk, :], start=False, stop=last)
            return mm

        def gate_up(st, k):
            pe.wait_ge(s[f"f_split{k}"], st + 1)
            if k == 0:
                pe.wait_ge(s["f_act_ready"], st)
            gate_up_block(k, 0)
            gate_up_block(k, 1).then_inc(s[f"f_used{k}"], 1)

        def gate_up_first():
            pe.wait_ge(s["turned_taken"], 10)
            for b in range(TB):
                for k in range(2):
                    pe.wait_ge(s["hf_ready"], 2 * b + k + 1)
                    pe.wait_ge(s[f"f_split{k}"], 1)
                    mm = gate_up_block(k, b)
                    if b == 1:
                        mm.then_inc(s[f"f_used{k}"], 1)
                    elif k == 0:
                        spread_row(N_G + KC, (0, 7), 2)
                        turn_block(1)

        def turn_act(st):
            pe.wait_ge(s["f_act_ready"], st + 1)
            if not (isinstance(st, int) and st == 0):
                pe.wait_ge(s["f_tlo"], st)
            for q in range(2):
                for b in range(TB):
                    tr = pe.transpose(ps[:, 7, (2 * q + b) * P:(2 * q + b + 1) * P],
                                      f_act[:, b, q * P:(q + 1) * P], ident)
            tr.then_inc(s["f_turned"], 1)

        def down(st, first=False, last=False):
            pe.wait_ge(s["f_split2"], st + 1)
            pe.wait_ge(s["f_tlo"], st + 1)
            for q in range(2):
                for b in range(TB):
                    for lhs, rhs in ((fT_hi, f_hi[2]), (fT_hi, f_lo[2]), (fT_lo, f_hi[2])):
                        for half in range(2):
                            mm = pe.matmul(bank(3 + 2 * b + half), lhs[:, q, b, :], rhs[:, q, 512 * half:512 * half + 512],
                                           start=(first and q == 0 and lhs is fT_hi and rhs is f_hi[2]),
                                           stop=(last and q == 1 and lhs is fT_lo), skip_group_check=True)
            mm.then_inc(s["f_used2"], 1)

        gate_up_first()
        pe.wait_ge(s["row_taken"], 4)
        gate_up(1, 0)
        turn_act(0)
        gate_up(1, 1)
        column_sums(EARLY)
        down(0, first=True)
        with pe.Fori(2, FSTEPS) as st:
            gate_up(st, 0)
            turn_act(st - 1)
            gate_up(st, 1)
            column_sums(st + EARLY - 1)
            down(st - 1)
        turn_act(FSTEPS - 1)
        down(FSTEPS - 1, last=True)

        pe.wait_ge(s["a_ready"], 4)
        pe.wait_ge(s["f_act_ready"], FSTEPS)
        pe.wait_ge(s["f_tlo"], FSTEPS)
        for r, (src, banks) in enumerate(((N_A + 3 * KC, (1, 2)), (N_M1, (7, 0)), (N_G + 2 * KC, (1, 2)))):
            spread_row(src, banks, 2 * r + 4)

        POOL_BANKS = (7, 0, 1, 2)
        pe.wait_ge(s["pool_in"], 64)
        for b in range(TB):
            pe.wait_ge(s["y_normed"], 3 + b)
            for g in range(NG):
                pe.matmul(ps[:, 3 + 2 * b + g // 2, (g % 2) * GD:(g % 2 + 1) * GD], ident,
                          pool_b_row[:, g * GD:(g + 1) * GD], start=(g % 2 == 0), stop=False, skip_group_check=True)

        def pool_group(g, b):
            for k in range(2):
                mm = pe.matmul(ps[:, POOL_BANKS[g], k * T:(k + 1) * T], h_tok[:, b, (2 * g + k) * P:(2 * g + k + 1) * P],
                               pool_mat[:, b, g, :], start=(b == 0 and k == 0), stop=(b == TB - 1), skip_group_check=True)
            if b == TB - 1:
                mm.then_inc(s["pooled"], 1)

        def mix_group(g):
            pe.wait_ge(s["pooled_taken"], g + 1)
            for b in range(TB):
                for k in range(2):
                    mm = pe.matmul(ps[:, 3 + 2 * b + g // 2, (g % 2) * GD:(g % 2 + 1) * GD],
                                   dT[:, 2 * g + k, b * P:(b + 1) * P], pool_w_sb[:, g, k, :],
                                   start=False, stop=(k == 1), skip_group_check=True)
                if g == NG - 1:
                    mm.then_inc(s["poolmix_ready"], 1)

        pe.wait_ge(s["xn_ready"], 7)
        for g in range(NG):
            if g == 0:
                pe.wait_ge(s["row_taken"], 8)
            if g == 2:
                pe.wait_ge(s["row_taken"], 10)
            pool_group(g, 0)
        pe.wait_ge(s["xn_ready"], 8)
        pool_group(0, 1)
        pool_group(1, 1)
        for g in range(2, NG):
            pool_group(g, 1)
            mix_group(g - 2)
        mix_group(NG - 2)
        mix_group(NG - 1)

        pe.wait_ge(s["pooled_taken"], NG)
        pe.wait_ge(s["xn_ready"], 10)
        pe.wait_ge(s["rb_in"], 16 * 2)

        def router(f):
            pe.wait_ge(s["turned_taken"], 13 + f)
            for k in (2 * f, 2 * f + 1):
                for b in range(TB):
                    mm = pe.matmul(ps[:, (7, 0)[b], 0:E], hr[:, k, b * P:(b + 1) * P], route_w[:, k, :],
                                   start=(k == 0), stop=(k == KC - 1))
            if f == 3:
                mm.then_inc(s["router_ready"], 1)

        for f in range(4):
            turn_fill(xm, f)
            if f:
                router(f - 1)
        router(3)
        pe.wait_ge(s["mask_ready"], 1)
        m0, m1 = route[:, R_MASK:R_MASK + E], route[:, R_MASK + E:R_MASK + 2 * E]
        pe.matmul(ps[:, 1, 0:E], upper, m0, start=True, stop=True)
        pe.matmul(ps[:, 1, E:2 * E], upper, m1, start=True, stop=False)
        pe.matmul(ps[:, 1, E:2 * E], ones, m0, start=False, stop=True).then_inc(s["ranks_ready"], 1)
        pe.matmul(ps[:, 2, 0:E], ones, m0, start=True, stop=False)
        pe.matmul(ps[:, 2, 0:E], ones, m1, start=False, stop=True).then_inc(s["ranks_ready"], 1)

        def gather():
            for k in range(KC):
                for b in range(TB):
                    mm = pe.matmul(ps[:, 5 + k // 4, (k % 4) * P:(k % 4 + 1) * P], xm[:, b, k * P:(k + 1) * P],
                                   hot[:, b, :], start=(b == 0), stop=(b == TB - 1))
                if k % 4 == 3:
                    mm.then_inc(s["gathered"], 1)

        def expert_gate_up(k, step):
            pe.wait_ge(s[f"m_split{k}"], step + 2)
            b = 1 + k // 2
            for kk in range(4):
                kc = 4 * (k % 2) + kk
                first, last = kc == 0, kc == KC - 1
                pe.matmul(bank(b), xs_hi[:, kc, :], m_hi[k][:, kk, :], start=first, stop=False)
                pe.matmul(bank(b), xs_hi[:, kc, :], m_lo[k][:, kk, :], start=False, stop=False)
                mm = pe.matmul(bank(b), xs_lo[:, kc, :], m_hi[k][:, kk, :], start=False, stop=last)
            mm.then_inc(s[f"m_used{k}"], 1)

        def expert_turn(step):
            pe.wait_ge(s["m_act_ready"], step + 2)
            pe.wait_ge(s["m_tlo"], step + 1)
            for q in range(4):
                tr = pe.transpose(ps[:, 7, q * P:(q + 1) * P], m_act[:, q * P:(q + 1) * P], ident)
            tr.then_inc(s["m_turned"], 1)

        def expert_down(step, first=False, last=False, split=None):
            high, low = (m_hi, m_lo) if split is None else split
            pe.wait_ge(s["m_tlo"], step + 2)
            for k in (4, 5):
                pe.wait_ge(s[f"m_split{k}"], step + 2)
                for q in range(2):
                    for lhs, rhs in ((mT_hi, high[k]), (mT_hi, low[k]), (mT_lo, high[k])):
                        for half in range(2):
                            mm = pe.matmul(bank(3 + half), lhs[:, 2 * (k - 4) + q, :], rhs[:, q, 512 * half:512 * half + 512],
                                           start=(first and k == 4 and q == 0 and lhs is mT_hi and rhs is high[k]),
                                           stop=(last and k == 5 and q == 1 and lhs is mT_lo), skip_group_check=True)
                mm.then_inc(s[f"m_used{k}"], 1)

        def scatter(j, n):
            b, half = divmod(n, 2)
            pe.matmul(bank((5, 6, 0, 5)[n]), hotT[:, b, :], y_slots[:, 512 * half:512 * half + 512],
                      start=True, stop=True).then_inc(s["scattered"], 1)

        def job(j, last):
            step = j * MSTEPS
            pe.wait_ge(s["m_act_ready"], step + 1)
            for k in range(4):
                if k < 2:
                    pe.wait_ge(s["xs_split"], 2 * j + 1 + k)
                expert_gate_up(k, step)
            pe.wait_ge(s["m_act_ready"], step + 2)
            expert_gate_up(0, step + 1)
            expert_gate_up(1, step + 1)
            expert_turn(step)
            pe.wait_ge(s["y_taken"], j + 1)
            pe.wait_ge(s["hotT_ready"], j + 1)
            for n in range(3):
                scatter(j, n)
            expert_gate_up(2, step + 1)
            expert_gate_up(3, step + 1)
            pe.wait_ge(s["acc_added"], 4 * j + 1)
            scatter(j, 3)
            pe.wait_ge(s["acc_added"], 4 * j + 2)
            pe.wait_ge(s["hotg_ready"], j + 1)
            for b in range(TB):
                tr = pe.transpose(ps[:, 6, b * P:(b + 1) * P], hot_g[:, b, :], ident)
            tr.then_inc(s["hotg_turned"], 1)
            expert_down(step, first=True)
            with pe.Fori(2, MSTEPS) as i:
                st = step + i
                pe.wait_ge(s["m_act_ready"], st + 1)
                expert_gate_up(0, st)
                expert_gate_up(1, st)
                expert_turn(st - 1)
                expert_gate_up(2, st)
                expert_gate_up(3, st)
                expert_down(st - 1)
            expert_turn(step + MSTEPS - 1)
            if not last:
                pe.wait_ge(s["hot_ready"], j + 2)
                pe.wait_ge(s["hotT_ready"], j + 2)
                pe.wait_ge(s["acc_added"], 4 * j + 4)
                gather()
            else:
                pe.wait_ge(s["hotT_ready"], j + 2)
                pe.wait_ge(s["acc_added"], 4 * j + 4)
                for f in range(2):
                    for k in range(4):
                        at = N_G + 3 * KC + 4 * f + k
                        mm = pe.matmul(ps[:, 5 + f, k * P:(k + 1) * P], cols[:, at:at + 1].to_broadcast([P, P]),
                                       ident, start=True, stop=True)
                    mm.then_inc(s["row_ready"], 1)
            expert_down(step + MSTEPS - 1, last=True, split=(last_hi, last_lo) if last else None)

        pe.wait_ge(s["hot_ready"], 1)
        gather()
        pe.wait_ge(s["route_ready"], 1)
        last_job = pe.value_load(jobs_i[0:1, 15:16], min_val=E - 1, max_val=MAX_JOBS - 1)
        with pe.Fori(0, last_job) as j:
            job(j, False)
        j = last_job
        job(j, True)
        pe.wait_ge(s["y_taken"], j + 2)
        pe.wait_ge(s["row_taken"], 12)
        for n in range(3):
            scatter(j, n)
        pe.wait_ge(s["acc_added"], 4 * j + 5)
        scatter(j, 3)

    @block.scalar
    def _(act):
        def squares(n, pairs):
            for b, (src, junk) in enumerate(pairs):
                act.activation(junk, src, ACT.Square, accum_out=stat(n, 0)[:, b:b + 1]).then_inc(s["sumsq_ready"], 1)

        def root(n):
            act.wait_ge(s["msq_ready"], n + 1)
            act.activation(stat(n, 2), stat(n, 1), ACT.Sqrt).then_inc(s["sqrt_ready"], 1)

        def load_table(func, n):
            at = (57, 59, 61, 63, 49, 51)[n]
            act.activation(small[:, at:at + 1], ones[:, 0:1], func)

        act.dma_start(rows_in[16:80, 0, :], norm_g.rearrange("l w (k p) -> (l w k) p", p=P)).then_inc(s["rows_in"], 16)
        act.dma_start(rows_in[0:96, 1, :], ada_b.rearrange("l (k p) -> (l k) p", p=P)).then_inc(s["rows_in"], 16)
        act.wait_ge(s["cols_ready"], 1)
        act.activation(cols[:, N_SC:N_SC + 2 * KC].rearrange("p (k a) -> p k a", a=2),
                       cols[:, 0:2 * KC].rearrange("p (a k) -> p k a", a=2), ACT.Silu).then_inc(s["silu_ready"], 1)
        act.wait_ge(s["x_in"], 16)
        squares(NORM_LAT, [(tok[:, b, :], xn[:, b, :]) for b in range(TB)])
        root(NORM_LAT)
        act.wait_ge(s["ctx_in"], 16)
        squares(NORM_CTX, [(ctx_tok[:, b, :], ctx_junk[:, b, :]) for b in range(CB)])
        root(NORM_CTX)

        for i in range(PE_PIECES):
            act.wait_ge(s["ada_used"], i + 1)
            act.activation(mod_two[:, i, :], ps[0:2, 3 + i, :], ACT.Copy).then_inc(s["ada_rows_taken"], 1)

        for b in range(CB):
            act.wait_ge(s["qkv_ready"], 3 + b)
            kv = bank(3 + 2 + b)
            for twice in range(2):
                act.activation(k_tok[:, TB + b, :, twice, :], kv[:, 0:KVD].rearrange("p (g d) -> p g d", g=HKV), ACT.Copy)
            act.activation(v_tok[:, TB + b, :], kv[:, KVD:2 * KVD], ACT.Copy).then_inc(s["kv_ctx_taken"], 1)
        def copy_queries(n):
            act.wait_ge(s["q_taken"], n + 1)
            heads, b = slice(8 * (n // TB), 8 * (n // TB) + 8), n % TB
            act.activation(q_tok[b][:, heads, 1, :], q_tok[b][:, heads, 0, :], ACT.Copy).then_inc(s["q_twice"], 1)

        def keys_hi(g):
            act.wait_ge(s["tr2_ready"], g + 1)
            act.activation(k_hi[:, g, :], bank(1 + g % 2), ACT.Copy).then_inc(s["tr2_hi"], 1)

        for n in range(3):
            copy_queries(n)
        keys_hi(0)
        keys_hi(1)
        copy_queries(3)
        keys_hi(2)
        keys_hi(3)
        for f in range(H // 2):
            act.wait_ge(s["tr2_ready"], HKV + 1 + f)
            act.activation(q_parts[:, 2 * f:2 * f + 2, :], bank(1 + f % 4).rearrange("p (k t) -> p k t", k=2),
                           ACT.Copy).then_inc(s["tr2_hi"], 1)

        NU = TB * H

        def take_turned(u):
            act.wait_ge(s["pt_ready"], u + 1)
            if u >= 2:
                act.wait_ge(s["pv_ready"], u - 1)
            act.activation(probsT[:, u % 2, :], bank(5 + u % 2), ACT.Copy).then_inc(s["pt_taken"], 1)

        SB = [3, 4, 2]
        for u in range(NU):
            if u >= 2:
                take_turned(u - 2)
            act.wait_ge(s["nmax_ready"], u + 1)
            act.activation(probs[:, u % 2, :], bank(SB[u % 3]), ACT.Exp, bias=small[:, SM_NM + u:SM_NM + u + 1],
                           scale=HD ** -0.5, accum_out=small[:, SM_SUM + u:SM_SUM + u + 1]).then_inc(s["probs_ready"], 1)
            if u % 8 == 7:
                og = u // 8
                act.wait_ge(s["esink_in"], og + 1)
                act.activation(small[:, SM_ES + 8 * og:SM_ES + 8 * og + 8], small[:, SM_ES + 8 * og:SM_ES + 8 * og + 8],
                               ACT.Exp).then_inc(s["esink_ready"], 1)
        take_turned(NU - 2)
        take_turned(NU - 1)
        for og in range(4):
            act.wait_ge(s["pt_ready"], NU + og + 1)
            act.activation(oT[:, 4 * (og % 2):4 * (og % 2) + 4, (og // 2) * P:(og // 2 + 1) * P],
                           bank(5 + og % 2).rearrange("p (k t) -> p k t", k=4), ACT.Copy).then_inc(s["pt_taken"], 1)

        def take_row(dst, banks, n):
            for f in range(2):
                act.wait_ge(s["row_ready"], n + f + 1)
                act.activation(dst[:, 512 * f:512 * f + 512], bank(banks[f]), ACT.Copy).then_inc(s["row_taken"], 1)

        take_row(g_row, (0, 7), 0)

        def dense_hi(k, st):
            act.wait_ge(s[f"f_in{k}"], (st + 1) * (32 if k < 2 else 16))
            if k == 2:
                act.wait_ge(s["f_used2"], st + 1)
            elif not (isinstance(st, int) and st == 0):
                act.wait_ge(s[f"f_used{k}"], st)
            act.activation(f_hi[k][:], f_raw[k][:], ACT.Copy).then_inc(s[f"f_hi{k}"], 1)

        load_table(ACT.Sqrt, 4)
        dense_hi(0, 0)
        for b in range(TB):
            act.wait_ge(s["wo_ready"], 2 * b + 2)
            y = ps[:, 3 + 2 * b:5 + 2 * b, :]
            if b == 1:
                act.wait_ge(s["y_normed"], 1)
            squares(NORM_Y + 2 * b, [(y, y_tmp[:].rearrange("p (a n) -> p a n", a=2))])
            root(NORM_Y + 2 * b)
            if b == 1:
                dense_hi(1, 0)
            act.wait_ge(s["y_normed"], b + 1)
            squares(NORM_Y + 2 * b + 1, [(tok[:, b, :], xn[:, b, :])])
            root(NORM_Y + 2 * b + 1)
            for half in range(2):
                act.wait_ge(s["turned_taken"], 9 + 2 * b + half)
                act.activation(hf_hi[:, 4 * half:4 * half + 4, b * P:(b + 1) * P],
                               hf[:, 4 * half:4 * half + 4, b * P:(b + 1) * P], ACT.Copy).then_inc(s["hf_hi_ready"], 1)

        def dense_silu(st):
            act.wait_ge(s["f_used1"], st + 1)
            act.wait_ge(s["f_turned"], st + 1)
            act.activation(f_act[:], ps[:, 1:3, 0:FS], ACT.Silu).then_inc(s["f_silu"], 1)

        def dense_turned_hi(st):
            act.wait_ge(s["f_turned"], st + 2)
            act.wait_ge(s["f_used2"], st + 1)
            act.activation(fT_hi[:].rearrange("p q b t -> p (q b t)"), bank(7), ACT.Copy).then_inc(s["f_thi"], 1)

        load_table(ACT.Silu, 5)
        take_row(g_row, (0, 7), 2)

        def dense_iteration(st, first=False, last=False):
            if not first:
                dense_turned_hi(st - 1)
            if not last:
                dense_hi(0, st + 1)
            dense_silu(st)
            if not last:
                dense_hi(1, st + 1)
            dense_hi(2, st)

        dense_iteration(0, first=True)
        with act.Fori(1, FSTEPS - 1) as st:
            dense_iteration(st)
        dense_iteration(FSTEPS - 1, last=True)
        dense_turned_hi(FSTEPS - 1)

        load_table(ACT.Sqrt, 0)
        act.wait_ge(s["f_used2"], FSTEPS + 1)
        for b in range(TB):
            squares(NORM_F + b, [(ps[:, 3 + 2 * b:5 + 2 * b, :], xn[:, b, :].rearrange("p (a n) -> p a n", a=2))])
            root(NORM_F + b)
        take_row(mod_rows[:, 0, :], (1, 2), 4)
        take_row(mod_rows[:, 1, :], (7, 0), 6)
        for b in range(TB):
            act.wait_ge(s["y_normed"], 3 + b)
            squares(NORM_POOL_PRE + b, [(tok[:, b, :], xn[:, b, :])])
            root(NORM_POOL_PRE + b)
        take_row(g1m_row, (1, 2), 8)

        def expert_hi(k, step, final=False):
            act.wait_ge(s[f"m_in{k}"], (step + 1) * 16)
            if final:
                act.wait_ge(s[f"m_used{k - 4}"], step + 1)
            elif k >= 4:
                act.wait_ge(s[f"m_used{k}"], step + 1)
            elif not (isinstance(step, int) and step == 0):
                act.wait_ge(s[f"m_used{k}"], step)
            act.activation((last_hi if final else m_hi)[k][:], m_raw[k][:], ACT.Copy).then_inc(s[f"m_hi{k}"], 1)

        expert_hi(0, 0)
        expert_hi(1, 0)
        for g in range(NG):
            act.wait_ge(s["pooled"], g + 1)
            act.activation(dT[:, 2 * g:2 * g + 2, :], bank((7, 0, 1, 2)[g]).rearrange("p (k t) -> p k t", k=2),
                           ACT.Copy).then_inc(s["pooled_taken"], 1)
            if g in (1, 3):
                expert_hi(2 + g // 2, 0)
        for b in range(TB):
            act.wait_ge(s["pool_y_ready"], b + 1)
            squares(NORM_POOL + b, [(pool_y[:, b, :], sq_junk[:, b, :])])
            root(NORM_POOL + b)
        for b in range(TB):
            act.wait_ge(s["y_normed"], 5 + b)
            squares(NORM_MOE_PRE + b, [(tok[:, b, :], sq_junk[:, b, :])])
            root(NORM_MOE_PRE + b)
        load_table(ACT.Exp, 1)
        act.wait_ge(s["diff_ready"], 1)
        act.activation(route[:, R_EX:R_EX + 2], route[:, R_D:R_D + 2], ACT.Exp).then_inc(s["exp_ready"], 1)

        def tokens_hi(j):
            for half in range(2):
                part = slice(4 * half, 4 * half + 4)
                act.wait_ge(s["xs_ready"], 2 * j + half + 1)
                act.activation(xs_hi[:, part, :], xs_full[:, part, :], ACT.Copy).then_inc(s["xs_hi_ready"], 1)

        def expert_silu(step):
            act.wait_ge(s["m_used3"], step + 1)
            act.wait_ge(s["m_turned"], step + 1)
            act.activation(m_act[:], bank(1), ACT.Silu).then_inc(s["m_silu"], 1)

        def expert_turned_hi(step):
            act.wait_ge(s["m_turned"], step + 2)
            act.wait_ge(s["m_used5"], step + 1)
            act.activation(mT_hi[:].rearrange("p q t -> p (q t)"), bank(7), ACT.Copy).then_inc(s["m_thi"], 1)

        def iteration(step, first=False, ahead=True):
            if ahead:
                expert_hi(0, step + 1)
                expert_hi(1, step + 1)
            if not first:
                expert_turned_hi(step - 1)
            if ahead:
                expert_hi(2, step + 1)
            expert_silu(step)
            if ahead:
                expert_hi(3, step + 1)
            expert_hi(4, step, final=not ahead)
            expert_hi(5, step, final=not ahead)

        def job(j, last):
            step = j * MSTEPS
            iteration(step, first=True)
            with act.Fori(1, MSTEPS - 1) as i:
                iteration(step + i)
            end = step + MSTEPS - 1
            iteration(end, ahead=not last)
            expert_turned_hi(end)
            if not last:
                act.wait_ge(s["m_used3"], end + 1)
                tokens_hi(j + 1)
            act.wait_ge(s["m_used5"], end + 2)
            act.wait_ge(s["scattered"], 4 * j + 4)
            act.activation(y_slots[:].rearrange("p (a n) -> p a n", a=2), ps[:, 3:5, :],
                           ACT.Copy).then_inc(s["y_taken"], 1)

        load_table(ACT.Silu, 2)
        tokens_hi(0)
        act.wait_ge(s["route_ready"], 1)
        last_job = act.value_load(jobs_i[0:1, 15:16], min_val=E - 1, max_val=MAX_JOBS - 1)
        with act.Fori(0, last_job) as j:
            job(j, False)
        j = last_job
        job(j, True)
        take_row(xs_full[:].rearrange("p k t -> p (k t)"), (5, 6), 10)
        load_table(ACT.Sqrt, 3)
        for b in range(TB):
            act.wait_ge(s["acc_added"], 4 * j + 6 + 2 * b)
            squares(NORM_LAST + b, [(acc[:, b, :], xm[:, b, :])])
            root(NORM_LAST + b)

    @block.vector
    def _(dve):
        done = Done(dve)
        step_ = s["dve_step"]
        for k in range(6):
            dve.sem_inc(s[f"m_split{k}"], 1)
        dve.sem_inc(s["m_act_ready"], 1)
        dve.sem_inc(s["m_tlo"], 1)

        def inverse_root(n):
            dve.wait_ge(s["sumsq_ready"], SUMS_UNTIL[n])
            dve.tensor_scalar(stat(n, 1), stat(n, 0), 1.0 / D, EPS, ALU.mult, ALU.add).then_inc(s["msq_ready"], 1)
            dve.wait_ge(s["sqrt_ready"], n + 1)
            done(dve.reciprocal(stat(n, 3), stat(n, 2)), s["rstd_ready"])

        dve.wait_ge(s["cols_turned"], 1)
        done(dve.tensor_copy(cols[:, 0:N_M0], ps[:, 0, 0:N_M0]), s["cols_ready"])
        dve.wait_ge(s["sink_in"], 16)
        done(dve.tensor_scalar(col(N_NSINK, H), col(N_SINK, H), -1.0, None, ALU.mult), s["nsink_ready"])
        inverse_root(NORM_LAT)
        for b in range(TB):
            done(dve.tensor_scalar(xn[:, b, :], tok[:, b, :], stat(NORM_LAT, 3)[:, b:b + 1], None, ALU.mult),
                 s["xn_ready"], wait=False)
        inverse_root(NORM_CTX)
        for b in range(CB):
            done(dve.tensor_scalar(ctx_tok[:, b, :], ctx_tok[:, b, :], stat(NORM_CTX, 3)[:, b:b + 1], None, ALU.mult),
                 s["xn_ready"], wait=False)

        def scale_column(at, scale, gain_col, sem=step_):
            done(dve.scalar_tensor_tensor(col(at, KC), scale, 1.0, gain_col, ALU.add, ALU.mult), sem)

        dve.wait_ge(s["ada_summed"], PE_PIECES)
        got = ps[:, 0, 0:4 * KC].rearrange("p (n a) -> p a n", a=2)
        for a, at in ((0, N_M0), (1, N_MC)):
            done(dve.tensor_tensor(col(at, 2 * KC), got[:, a, :], col(N_B, 2 * KC), ALU.add), step_)
        scale_column(N_A, col(N_M0 + KC, KC), gain(0, 0))
        scale_column(N_A + KC, col(N_MC + KC, KC), gain(0, 0), s["a_ready"])

        taken = [0]

        def take_turned(dst, a, shift):
            for f in range(4):
                n = taken[0]
                taken[0] += 1
                dve.wait_ge(s["turn_ready"], n + 1)
                for k in range(2):
                    kc = 2 * f + k
                    ins = dve.tensor_scalar(dst[:, kc, :], ps[:, FILL_BANKS[n % 2], k * T:(k + 1) * T],
                                            cols[:, a + kc:a + kc + 1], cols[:, shift + kc:shift + kc + 1], ALU.mult, ALU.add)
                done(ins, s["turned_taken"], wait=False)

        take_turned(hT, N_A, N_M0)
        take_turned(hcT, N_A + KC, N_MC)

        def take_columns(q):
            dve.wait_ge(s["colsum_ready"], q + 1)
            if isinstance(q, int):
                at = (N_M0 + 16 + 4 * q) if q < 8 else N_M1 + 4 * (q - 8)
                bias = N_B + 16 + 4 * q
                dst, src = col(at, 4), col(bias, 4)
            else:
                dst, src = cols[:, bass.ds(q * 4 + (N_M1 - 32), 4)], cols[:, bass.ds(q * 4 + (N_B + 16), 4)]
            dve.tensor_tensor(dst, ps[:, 0, 0:4], src, ALU.add).then_inc(s["mod_ready"], 1)

        def sum_chunk(q, w, k):
            v, acc_q = cols[:, N_SC + 2 * k:N_SC + 2 * k + 1], acc_of(q)
            if k == 0:
                ins = dve.tensor_scalar(acc_q[:], w[:, k, :], v, None, ALU.mult)
            else:
                dve.wait_ge(s["acc_ready"], q * KC + k)
                ins = dve.scalar_tensor_tensor(acc_q[:], w[:, k, :], v, acc_q[:], ALU.mult, ALU.add)
            ins.then_inc(s["acc_ready"], 1)

        def sum_piece(q, w):
            for k in range(KC):
                sum_chunk(q, w, k)

        def early_chunk(q, k):
            i = q + PE_PIECES
            if k == 0:
                dve.wait_ge(s[f"ada_in{i % 3}"], 16 * (i // 3 + 1))
            sum_chunk(q, ada_ring[i % 3], k)

        def rope(src, b, heads, dsts, sem, wait=True):
            def table(t, part=None):
                v = t.rearrange("p (x a r) -> p x a r", x=2, a=2)
                return v if part is None else v[:, :, part:part + 1, :]
            w = heads * HD
            xv = src.rearrange("p (h x a r) -> p h x a r", h=heads, x=2, a=2)
            av = rope_a[:, 0:w].rearrange("p (h d) -> p h d", h=heads)
            bv = rope_b[:, 0:w].rearrange("p (h x a r) -> p h x a r", h=heads, x=2, a=2)
            done(dve.tensor_tensor(av, src.rearrange("p (h d) -> p h d", h=heads),
                                   cos_of(b).unsqueeze(1).to_broadcast([P, heads, HD]), ALU.mult), step_, wait=False)
            sn = sin_of(b).rearrange("p (x a r) -> p x a r", x=2, a=2)
            for part in range(2):
                for half in range(2):
                    ins = dve.tensor_tensor(bv[:, :, half, part, :], xv[:, :, half, 1 - part, :],
                                            sn[:, half, part, :].unsqueeze(1).to_broadcast([P, heads, ROPE_HALF]), ALU.mult)
            done(ins, step_)
            for n, dst in enumerate(dsts):
                ins = dve.tensor_tensor(dst, av, rope_b[:, 0:w].rearrange("p (h d) -> p h d", h=heads), ALU.add)
            done(ins, sem, wait)

        def low_parts(f):
            dve.wait_ge(s["tr2_hi"], f + 1)
            if f < HKV:
                dve.tensor_tensor(k_lo[:, f, :], bank(1 + f % 2), k_hi[:, f, :].bitcast(F32),
                                  ALU.subtract).then_inc(s["tr2_taken"], 1)
            else:
                f -= HKV
                part = q_parts[HD:P, 2 * f:2 * f + 2, :]
                dve.tensor_tensor(part, ps[HD:P, 1 + f % 4, :].rearrange("p (k t) -> p k t", k=2), part.bitcast(F32),
                                  ALU.subtract).then_inc(s["tr2_taken"], 1)

        UNITS = [("kv", 0), ("kv", 1), None, None, (0, 0), (1, 0), (0, 1), (1, 1)]
        for u, what in enumerate(UNITS):
            if what is not None:
                dve.wait_ge(s["qkv_ready"], u + 1)
                src = bank(3 + u % 4)
                if what[0] == "kv" and u < 2:
                    b = what[1]
                    done(dve.tensor_copy(v_tok[:, b, :], src[:, KVD:2 * KVD]), step_, wait=False)
                    rope(src[:, 0:KVD], b, HKV, [k_tok[:, b, :, i, :] for i in range(2)], s["kv_lat_taken"])
                else:
                    b, n = what
                    rope(src, b, 8, [q_tok[b][:, 8 * n:8 * n + 8, 0, :]], s["q_taken"])
            if u == 6:
                low_parts(0)
                low_parts(1)
            if u == 7:
                low_parts(2)
                low_parts(3)
            if u >= 2:
                take_columns(u - 2)
            for k in range(KC):
                if u < MIXER_PIECES:
                    early_chunk(u, k)
                if u == 7:
                    low_parts(HKV + k)

        NU = TB * H
        OB = [7, 1, 7, 1]
        SB = [3, 4, 2]

        def normalise(og):
            c8 = slice(8 * og, 8 * og + 8)
            part = lambda at: small[:, at + 8 * og:at + 8 * og + 8]
            dve.wait_ge(s["esink_ready"], og + 1)
            done(dve.tensor_tensor(part(SM_DEN), part(SM_SUM), part(SM_ES), ALU.add), step_)
            done(dve.reciprocal(part(SM_RDEN), part(SM_DEN)), step_)
            dve.wait_ge(s["pv_ready"], 8 * (og + 1))
            b, half = divmod(og, 2)
            done(dve.tensor_tensor(o_tok[:, b, 512 * half:512 * half + 512].rearrange("p (h d) -> p h d", h=8),
                                   bank(OB[og]).rearrange("p (h d) -> p h d", h=8),
                                   part(SM_RDEN).unsqueeze(2).to_broadcast([P, 8, HD]), ALU.mult), s["o_taken"], wait=False)

        for u in range(NU):
            h = u % H
            dve.wait_ge(s["scores_ready"], u + 1)
            done(dve.tensor_reduce(small[:, SM_MAX + u:SM_MAX + u + 1], bank(SB[u % 3]), AX.X, ALU.max), s["max_ready"])
            done(dve.tensor_scalar(small[:, SM_NM + u:SM_NM + u + 1], small[:, SM_MAX + u:SM_MAX + u + 1], -(HD ** -0.5),
                                   cols[:, N_NSINK + h:N_NSINK + h + 1], ALU.mult, ALU.min), s["nmax_ready"], wait=(u % 8 == 7))
            if u % 8 == 7:
                og = u // 8
                h0 = 8 * (og % 2)
                done(dve.tensor_tensor(small[:, SM_ES + 8 * og:SM_ES + 8 * og + 8], small[:, SM_NM + 8 * og:SM_NM + 8 * og + 8],
                                       col(N_SINK + h0, 8), ALU.add), s["esink_in"], wait=False)
            if u % 8 == 3 and u > 8:
                normalise(u // 8 - 1)
            if u % KC == 3 and u > KC:
                take_columns(MIXER_PIECES + u // KC - 1)
            early_chunk(MIXER_PIECES + u // KC, u % KC)
        take_columns(EARLY - 1)
        done.n[s["mod_ready"]] = EARLY
        dve.wait_ge(s["mod_ready"], EARLY)
        scale_column(N_A + 2 * KC, col(N_M0 + 4 * KC, KC), gain(0, 2), s["a_ready"])
        done(dve.tensor_tensor(col(N_G + KC, KC), col(N_M0 + 5 * KC, KC), gain(0, 3), ALU.mult), step_)
        done(dve.tensor_tensor(col(N_G, KC), col(N_M0 + 2 * KC, KC), gain(0, 1), ALU.mult), s["a_ready"])
        normalise(3)

        def add_normed(n, b, y, row, scratch, rstd):
            done(dve.scalar_tensor_tensor(scratch, y, rstd, row, ALU.mult, ALU.mult), step_)
            done(dve.tensor_tensor(tok[:, b, :], tok[:, b, :], y_flat(scratch), ALU.add), s["y_normed"])

        def two(v):
            return v.rearrange("p (a n) -> p a n", a=2)

        def y_flat(v):
            return v if len(v.shape) == 2 else v.rearrange("p a n -> p (a n)")

        def dense_lo(k, st):
            dve.wait_ge(s[f"f_hi{k}"], st + 1)
            dve.tensor_tensor(f_lo[k][:], f_raw[k][:], f_hi[k][:].bitcast(F32), ALU.subtract).then_inc(s[f"f_split{k}"], 1)

        dve.wait_ge(s["row_taken"], 2)
        dense_lo(0, 0)
        for b in range(TB):
            inverse_root(NORM_Y + 2 * b)
            add_normed(NORM_Y, b, ps[:, 3 + 2 * b:5 + 2 * b, :], two(g_row[:]), two(y_tmp[:]), stat(NORM_Y + 2 * b, 3))
            if b == 1:
                dense_lo(1, 0)
            inverse_root(NORM_Y + 2 * b + 1)
            done(dve.tensor_scalar(xn[:, b, :], tok[:, b, :], stat(NORM_Y + 2 * b + 1, 3), None, ALU.mult),
                 s["xn_ready"], wait=False)
            part = slice(b * P, (b + 1) * P)
            for half in range(2):
                dve.wait_ge(s["turn_ready"], 9 + 2 * b + half)
                for k in range(4):
                    kc = 4 * half + k
                    a, shift = N_A + 2 * KC + kc, N_M0 + 3 * KC + kc
                    ins = dve.tensor_scalar(hf[:, kc, part], ps[:, 1 + 2 * b + half, k * P:(k + 1) * P],
                                            cols[:, a:a + 1], cols[:, shift:shift + 1], ALU.mult, ALU.add)
                done(ins, s["turned_taken"], wait=False)
            for half in range(2):
                chunks = slice(4 * half, 4 * half + 4)
                dve.wait_ge(s["hf_hi_ready"], 2 * b + half + 1)
                dve.tensor_tensor(hf_lo[:, chunks, part], hf[:, chunks, part], hf_hi[:, chunks, part].bitcast(F32),
                                  ALU.subtract).then_inc(s["hf_ready"], 1)
        taken[0] += 4

        def dense_turned_lo(st):
            dve.wait_ge(s["f_thi"], st + 1)
            dve.tensor_tensor(fT_lo[:].rearrange("p q b t -> p (q b t)"), bank(7),
                              fT_hi[:].rearrange("p q b t -> p (q b t)").bitcast(F32), ALU.subtract).then_inc(s["f_tlo"], 1)

        def dense_iteration(st, first=False, last=False):
            if not first:
                dense_turned_lo(st - 1)
            if not last:
                dense_lo(0, st + 1)
            dve.wait_ge(s["f_silu"], st + 1)
            dve.tensor_tensor(f_act[:], f_act[:], ps[:, 1:3, FS:2 * FS], ALU.mult).then_inc(s["f_act_ready"], 1)
            if not last:
                dense_lo(1, st + 1)
            dense_lo(2, st)
            if not first:
                take_columns(st + EARLY - 1)
            if not last:
                dve.wait_ge(s["ada_late_in"], (st + 1) * 16)
                sum_piece(st + EARLY, ada_ring[0])

        dense_iteration(0, first=True)
        with dve.Fori(1, FSTEPS - 1) as st:
            dense_iteration(st)
        dense_iteration(FSTEPS - 1, last=True)
        dense_turned_lo(FSTEPS - 1)
        dve.wait_ge(s["mod_ready"], EARLY + L1_LATE)
        scale_column(N_A + 3 * KC, col(N_M1 + KC, KC), gain(1, 0))
        scale_column(N_A + 4 * KC, col(N_M1 + 4 * KC, KC), gain(1, 2))
        done(dve.tensor_tensor(col(N_G + 3 * KC, KC), col(N_M1 + 5 * KC, KC), gain(1, 3), ALU.mult), step_)
        done(dve.tensor_tensor(col(N_G + 2 * KC, KC), col(N_M1 + 2 * KC, KC), gain(1, 1), ALU.mult), s["a_ready"])

        dve.wait_ge(s["row_taken"], 4)
        for b in range(TB):
            inverse_root(NORM_F + b)
            add_normed(NORM_F, b, ps[:, 3 + 2 * b:5 + 2 * b, :], two(g_row[:]), two(y_tmp[:]), stat(NORM_F + b, 3))
        for b in range(TB):
            inverse_root(NORM_POOL_PRE + b)
            dve.wait_ge(s["row_taken"], 6)
            done(dve.scalar_tensor_tensor(h_tok[:, b, :], tok[:, b, :], stat(NORM_POOL_PRE + b, 3), mod_rows[:, 0, :],
                                          ALU.mult, ALU.mult), step_)
            dve.wait_ge(s["row_taken"], 8)
            done(dve.tensor_tensor(h_tok[:, b, :], h_tok[:, b, :], mod_rows[:, 1, :], ALU.add), s["xn_ready"], wait=False)

        def expert_lo(k, step, final=False):
            high, low = (last_hi, last_lo) if final else (m_hi, m_lo)
            dve.wait_ge(s[f"m_hi{k}"], step + 1)
            dve.tensor_tensor(low[k][:], m_raw[k][:], high[k][:].bitcast(F32), ALU.subtract).then_inc(s[f"m_split{k}"], 1)

        for k in range(3):
            expert_lo(k, 0)
        for b in range(TB):
            dve.wait_ge(s["poolmix_ready"], b + 1)
            done(dve.tensor_tensor(two(pool_y[:, b, :]), ps[:, 3 + 2 * b:5 + 2 * b, :], two(pool_s_row[:]), ALU.mult),
                 s["pool_y_ready"], wait=(b == 1))
        expert_lo(3, 0)
        dve.wait_ge(s["row_taken"], 10)
        for b in range(TB):
            inverse_root(NORM_POOL + b)
            add_normed(NORM_POOL, b, pool_y[:, b, :], g1m_row[:], pool_y[:, b, :], stat(NORM_POOL + b, 3))
        for b in range(TB):
            inverse_root(NORM_MOE_PRE + b)
            done(dve.tensor_scalar(xm[:, b, :], tok[:, b, :], stat(NORM_MOE_PRE + b, 3), None, ALU.mult),
                 s["xn_ready"], wait=False)
        take_turned(hr, N_A + 4 * KC, N_M1 + 3 * KC)

        def r(at, n=E):
            return route[:, at:at + n]

        def both(at):
            return route[:, at:at + 2 * E].rearrange("p (b e) -> p b e", b=TB)

        def pair(at):
            return route[:, at:at + TB].unsqueeze(2).to_broadcast([P, TB, E])

        experts = ct[:, K_IOTA:K_IOTA + E]
        experts_both = experts.unsqueeze(1).to_broadcast([P, TB, E])
        bias = col(N_RB, E)
        done(dve.memset(job_table[:], -1.0), step_, wait=False)
        done(dve.memset(jobs_f[:], 0.0), step_, wait=False)
        dve.wait_ge(s["router_ready"], 1)
        for b in range(TB):
            done(dve.tensor_tensor(r(R_L + b * E), ps[:, (7, 0)[b], 0:E], bias, ALU.add), step_, wait=(b == 1))
        for b in range(TB):
            done(dve.max(r(R_TOP + b * E), r(R_L + b * E)), step_, wait=(b == 1))
        for b in range(TB):
            done(dve.max_index(top_i[:, b * E:(b + 1) * E], r(R_TOP + b * E), r(R_L + b * E)), step_, wait=False)
        done(dve.tensor_tensor(route[:, R_D:R_D + 2], both(R_TOP)[:, :, 1], both(R_TOP)[:, :, 0], ALU.subtract), s["diff_ready"])
        done(dve.tensor_copy(r(R_TOPI, 2 * E), top_i[:]), step_)
        for n, at in ((0, R_H1), (1, R_H2)):
            done(dve.tensor_tensor(both(at), experts_both, both(R_TOPI)[:, :, n:n + 1].to_broadcast([P, TB, E]),
                                   ALU.is_equal), step_, wait=(n == 1))
        done(dve.tensor_tensor(r(R_MASK, 2 * E), r(R_H1, 2 * E), r(R_H2, 2 * E), ALU.add), s["mask_ready"], wait=False)
        dve.wait_ge(s["exp_ready"], 1)
        done(dve.tensor_scalar(route[:, R_DEN:R_DEN + 2], route[:, R_EX:R_EX + 2], 1.0, None, ALU.add), step_)
        done(dve.reciprocal(route[:, R_G1:R_G1 + 2], route[:, R_DEN:R_DEN + 2]), step_)
        done(dve.tensor_tensor(route[:, R_G2:R_G2 + 2], route[:, R_EX:R_EX + 2], route[:, R_G1:R_G1 + 2], ALU.mult), step_)
        done(dve.tensor_tensor(both(R_H1), both(R_H1), pair(R_G1), ALU.mult), step_, wait=False)
        done(dve.tensor_tensor(both(R_H2), both(R_H2), pair(R_G2), ALU.mult), step_)
        done(dve.tensor_tensor(r(R_GATE, 2 * E), r(R_H1, 2 * E), r(R_H2, 2 * E), ALU.add), step_, wait=False)
        dve.wait_ge(s["ranks_ready"], 1)
        done(dve.scalar_tensor_tensor(r(R_POS, 2 * E), ps[:, 1, 0:2 * E], 1.0, r(R_MASK, 2 * E), ALU.add, ALU.mult), step_)
        done(dve.tensor_scalar(r(R_POS, 2 * E), r(R_POS, 2 * E), -1.0, None, ALU.add), step_)
        for b in range(TB):
            ins = dve.tensor_scalar(hot[:, b, :], iota, route[:, R_POS + b * E:R_POS + b * E + 1], None, ALU.is_equal)
        ins.then_inc(s["hot_ready"], 1)
        dve.wait_ge(s["ranks_ready"], 2)
        done(dve.tensor_copy(r(R_CNT), ps[:, 2, 0:E]), step_)
        done(dve.tensor_scalar(r(R_OVER), r(R_CNT), float(SLOTS), None, ALU.is_gt), step_)
        done(dve.memset(r(R_RANK), 0.0), step_, wait=False)
        done(dve.tensor_copy(job_table[:, 0:2, 0:E], both(R_POS)), step_, wait=False)
        done(dve.tensor_copy(job_table[:, 2:4, 0:E], both(R_GATE)), step_, wait=False)
        done(dve.tensor_copy(jobs_f[:, 0:E], experts), step_, wait=False)
        done(dve.tensor_scalar(r(R_TMP, 2 * E), r(R_POS, 2 * E), -float(SLOTS), None, ALU.add), step_)
        for e in range(1, E):
            done(dve.tensor_tensor(r(R_RANK + e, 1), r(R_RANK + e - 1, 1), r(R_OVER + e - 1, 1), ALU.add), step_)
        for n in range(EXTRA):
            done(dve.scalar_tensor_tensor(r(R_SEL + n * E), r(R_RANK), float(n), r(R_OVER), ALU.is_equal, ALU.mult),
                 step_, wait=(n == EXTRA - 1))
        sel = route[:, R_SEL:R_SEL + EXTRA * E].rearrange("p (n e) -> p n e", e=E)
        products = small[:, SM_NM:SM_NM + 5 * EXTRA * E].rearrange("p (w n e) -> p w n e", w=5, e=E)
        for w, what in enumerate((experts, r(R_TMP), r(R_TMP + E), r(R_GATE), r(R_GATE + E))):
            done(dve.tensor_tensor(products[:, w], sel, what.unsqueeze(1).to_broadcast([P, EXTRA, E]), ALU.mult),
                 step_, wait=(w == 4))
        done(dve.tensor_reduce(jobs_f[:, E:MAX_JOBS], products[:, 0], AX.X, ALU.add), step_, wait=False)
        done(dve.tensor_reduce(job_table[:, :, E:MAX_JOBS], products[:, 1:5], AX.X, ALU.add), step_, wait=False)
        done(dve.tensor_reduce(r(R_JUNK, 1), r(R_OVER), AX.X, ALU.add), step_)
        done(dve.tensor_scalar(jobs_f[:, 15:16], r(R_JUNK, 1), float(E - 1), None, ALU.add), step_)
        done(dve.tensor_copy(jobs_i[:], jobs_f[:]), s["route_ready"])
        last_job = dve.value_load(jobs_i[0:1, 15:16], min_val=E - 1, max_val=MAX_JOBS - 1)

        def job_column(j, count):
            dve.tensor_copy(job_col[:], job_table[:, :, bass.ds(j, 1)] if not isinstance(j, int) else job_table[:, :, j]
                            ).then_inc(s["job_col_ready"], 1)
            dve.wait_ge(s["job_col_ready"], count)

        def one_hot():
            for b in range(TB):
                ins = dve.tensor_scalar(hot[:, b, :], iota, job_col[:, b:b + 1], None, ALU.is_equal)
            ins.then_inc(s["hot_ready"], 1)

        def tokens(j):
            for k in range(KC):
                if k % 4 == 0:
                    dve.wait_ge(s["gathered"], 2 * j + k // 4 + 1)
                a, b = N_A + 4 * KC + k, N_M1 + 3 * KC + k
                ins = dve.tensor_scalar(xs_full[:, k, :], ps[:, 5 + k // 4, (k % 4) * P:(k % 4 + 1) * P],
                                        cols[:, a:a + 1], cols[:, b:b + 1], ALU.mult, ALU.add)
                if k % 4 == 3:
                    ins.then_inc(s["xs_ready"], 1)
            for half in range(2):
                part = slice(4 * half, 4 * half + 4)
                dve.wait_ge(s["xs_hi_ready"], 2 * j + half + 1)
                dve.tensor_tensor(xs_lo[:, part, :], xs_full[:, part, :], xs_hi[:, part, :].bitcast(F32),
                                  ALU.subtract).then_inc(s["xs_split"], 1)

        def add_piece(j, n):
            b, half = divmod(n, 2)
            dve.wait_ge(s["scattered"], 4 * j + n + 1)
            part = acc[:, b, 512 * half:512 * half + 512]
            dve.tensor_tensor(part, part, bank((5, 6, 0, 5)[n]), ALU.add).then_inc(s["acc_added"], 1)

        def expert_turned_lo(step):
            dve.wait_ge(s["m_thi"], step + 1)
            dve.tensor_tensor(mT_lo[:].rearrange("p q t -> p (q t)"), bank(7),
                              mT_hi[:].rearrange("p q t -> p (q t)").bitcast(F32), ALU.subtract).then_inc(s["m_tlo"], 1)

        def expert_act(step):
            dve.wait_ge(s["m_silu"], step + 1)
            dve.tensor_tensor(m_act[:], m_act[:], bank(2), ALU.mult).then_inc(s["m_act_ready"], 1)

        def iteration(step, first=False, ahead=True, before=None, after=None):
            if ahead:
                expert_lo(0, step + 1)
                expert_lo(1, step + 1)
            if not first:
                expert_turned_lo(step - 1)
            if before:
                before()
            if ahead:
                expert_lo(2, step + 1)
            expert_act(step)
            if after:
                after()
            if ahead:
                expert_lo(3, step + 1)
            expert_lo(4, step, final=not ahead)
            expert_lo(5, step, final=not ahead)

        def job(j, last):
            step = j * MSTEPS

            def adds():
                for n in range(3):
                    add_piece(j, n)
                job_column(j, 2 * j + 2)
                for b in range(TB):
                    ins = dve.tensor_scalar(hot_g[:, b, :], iota, job_col[:, b:b + 1], job_col[:, TB + b:TB + b + 1],
                                            ALU.is_equal, ALU.mult)
                ins.then_inc(s["hotg_ready"], 1)

            def turned():
                add_piece(j, 3)
                dve.wait_ge(s["hotg_turned"], j + 1)
                dve.tensor_copy(hotT[:].rearrange("p b t -> p (b t)"), ps[:, 6, 0:TB * P]).then_inc(s["hotT_ready"], 1)
                job_column(j + 1, 2 * j + 3)
                dve.wait_ge(s["gathered"], 2 * j + 2)
                one_hot()

            iteration(step, first=True)
            iteration(step + 1, before=adds, after=turned)
            with dve.Fori(2, MSTEPS - 1) as i:
                iteration(step + i)
            end = step + MSTEPS - 1
            iteration(end, ahead=not last)
            expert_turned_lo(end)
            if not last:
                tokens(j + 1)

        dve.wait_ge(s["zeroed"], 1)
        dve.sem_inc(s["job_col_ready"], 1)
        tokens(0)
        with dve.Fori(0, last_job) as j:
            job(j, False)
        j = last_job
        job(j, True)
        for n in range(4):
            add_piece(j + 1, n)
        dve.wait_ge(s["row_taken"], 12)
        last_row = xs_full[:].rearrange("p k t -> p (k t)")
        for b in range(TB):
            inverse_root(NORM_LAST + b)
            done(dve.scalar_tensor_tensor(acc[:, b, :], acc[:, b, :], stat(NORM_LAST + b, 3), last_row,
                                          ALU.mult, ALU.mult), step_)
            done(dve.tensor_tensor(tok[:, b, :], tok[:, b, :], acc[:, b, :], ALU.add), s["tok_ready"], wait=False)

    block.__exit__(None, None, None)


_INS = ['x', 'c', 'ctx', 'c_ctx', 'ada_w', 'ada_b', 'norm_g', 'attn_w_qkv', 'attn_w_o', 'attn_sink', 'pool_w', 'pool_b',
        'pool_scale', 'ffn_w_gu', 'ffn_w_down', 'router_w', 'router_b', 'moe_w_gu', 'moe_w_down']


def kernel(**inputs):
    import concourse.bacc as bacc
    from concourse.bass_utils import run_bass_kernel_spmd

    nc = bacc.Bacc("TRN2", target_bir_lowering=False, num_devices=1)
    arrays = {f"in_{name}": np.ascontiguousarray(inputs[name]) for name in _INS}
    arrays["in_consts"], arrays["in_pool_m"] = constants()
    args = [nc.dram_tensor(name, a.shape, F32, kind="ExternalInput").ap() for name, a in arrays.items()]
    out = nc.dram_tensor("out_0", (1, T, D), F32, kind="ExternalOutput").ap()
    build(nc, *args, out)
    r = run_bass_kernel_spmd(nc, [arrays], core_ids=[0])
    return np.asarray(r.results[0]["out_0"])
```

```python
from contextlib import ExitStack

import numpy as np

import concourse.bass as bass
from concourse import mybir

P = 128
D = 1024
KC = D // P
T = 256
TB = T // P
C = 256
CB = C // P
H, HKV, HD = 16, 4, 64
GROUP = H // HKV
QD, KVD = H * HD, HKV * HD
KEYS = T + C
WINDOW = 128
GRID_W = 64
ROPE_HALF = HD // 4
POOL_WINDOWS = (2, 4, 8, 16)
NG = len(POOL_WINDOWS)
GD = D // NG
FF = 2816
FS = 256
FSTEPS = FF // FS
E = 8
FE = 3584
MS = 512
MSTEPS = FE // MS
SLOTS = 128
CROWDED = (2 * T) // (SLOTS + 1)
EPS = 1e-6
KEY_ORDER = (0, 2, 3, 1)
NEG = -8e30

F32 = mybir.dt.float32
F32R = mybir.dt.float32r
I32 = mybir.dt.int32
U32 = mybir.dt.uint32
ALU = mybir.AluOpType
ACT = mybir.ActivationFunctionType
AX = mybir.AxisListType

K_ID, K_UP, K_IOTA, K_ONE = 0, P, 2 * P, 3 * P
K_COS, K_SIN = 4 * P, 4 * P + TB * HD
K_MASK = K_SIN + TB * HD
K_END = K_MASK + TB * P


def constants():
    t = np.zeros((P, K_END), np.float32)
    t[:, K_ID:K_ID + P] = np.eye(P)
    t[:, K_UP:K_UP + P] = np.arange(P)[:, None] < np.arange(P)[None, :]
    t[:, K_IOTA:K_IOTA + P] = np.arange(P)[None, :]
    t[:, K_ONE:K_ONE + P] = 1.0
    inv = np.float32(10000.0) ** (-np.arange(ROPE_HALF, dtype=np.float32) / np.float32(ROPE_HALF))
    for b in range(TB):
        tok = b * P + np.arange(P)
        for half, pos in enumerate((tok // GRID_W, tok % GRID_W)):
            ang = pos[:, None].astype(np.float32) * inv
            for part, sign in ((0, -1.0), (1, 1.0)):
                at = b * HD + half * 2 * ROPE_HALF + part * ROPE_HALF
                t[:, K_COS + at:K_COS + at + ROPE_HALF] = np.cos(ang)
                t[:, K_SIN + at:K_SIN + at + ROPE_HALF] = sign * np.sin(ang)
        key = (1 - b) * P + np.arange(P)
        t[:, K_MASK + b * P:K_MASK + (b + 1) * P] = np.where(
            np.abs(key[None, :] - tok[:, None]) <= WINDOW, 0.0, NEG)
    pool = np.zeros((T, NG, T), np.float32)
    for g, w in enumerate(POOL_WINDOWS):
        for i in range(T):
            lo, hi = max(i - w // 2, 0), min(i - w // 2 + w, T)
            pool[lo:hi, g, i] = 1.0 / (hi - lo)
            pool[i, g, i] -= 1.0
    pool = np.ascontiguousarray(pool.reshape(TB, P, NG, T).transpose(1, 0, 2, 3)).reshape(P, TB * NG * T)
    return t, pool


class Done:

    def __init__(self, eng):
        self.eng, self.n = eng, {}

    def __call__(self, ins, sem, wait=True):
        self.n[sem] = self.n.get(sem, 0) + 1
        ins.then_inc(sem, 1)
        if wait:
            self.eng.wait_ge(sem, self.n[sem])
        return self.n[sem]


def build(nc, x, c, ctx_in, c_ctx, ada_w, ada_b, norm_g, w_qkv, w_o, sink, pool_w, pool_b, pool_scale,
          ffn_gu, ffn_down, router_w, router_b, moe_gu, moe_down, consts, pool_m, out):
    KB = 1024
    base = (nc.sbuf_base + 63) // 64 * 64

    def sb(name, shape, dt, at):
        return nc.alloc_sbuf_tensor_at(name, [shape[0], *shape[1:]], dt, offset=base + at)

    R0, R1, R2 = 0, 48 * KB, 144 * KB
    wqkv = sb("wqkv", [P, KC, QD + 2 * KVD], F32, R0)
    m_raw = [sb(f"m_raw{k}", [P, 4, MS] if k < 4 else [P, 2, D], F32, R0 + 8 * KB * k) for k in range(6)]
    f_raw = [sb(f"f_raw{k}", [P, 4, 2 * FS] if k < 2 else [P, 2, D], F32, R0 + 24 * KB + 8 * KB * k)
             for k in range(3)]

    wo_sb = sb("wo_sb", [P, KC, D], F32, R1 + 16 * KB)
    q_parts = sb("q_parts", [P, H, T], F32R, R0)
    k_hi = sb("k_hi", [P, HKV, KEYS], F32R, R1)
    k_lo = sb("k_lo", [P, HKV, KEYS], F32R, R1 + 8 * KB)
    ada_ring = [sb(f"ada{i}", [P, KC, 512], F32, R1 + 48 * KB + 16 * KB * i) for i in range(3)]
    f_hi = [sb(f"f_hi{k}", [P, 4, 2 * FS] if k < 2 else [P, 2, D], F32R, R1 + 16 * KB * k) for k in range(3)]
    f_lo = [sb(f"f_lo{k}", [P, 4, 2 * FS] if k < 2 else [P, 2, D], F32R, R1 + 16 * KB * k + 8 * KB)
            for k in range(3)]
    m_hi = [sb(f"m_hi{k}", [P, 4, MS] if k < 4 else [P, 2, D], F32R, R1 + 16 * KB * k) for k in range(6)]
    m_lo = [sb(f"m_lo{k}", [P, 4, MS] if k < 4 else [P, 2, D], F32R, R1 + 16 * KB * k + 8 * KB)
            for k in range(6)]
    last_hi = {k: sb(f"last_hi{k}", [P, 2, D], F32R, R1 + 16 * KB * (k - 4)) for k in (4, 5)}
    last_lo = {k: sb(f"last_lo{k}", [P, 2, D], F32R, R1 + 16 * KB * (k - 4) + 8 * KB) for k in (4, 5)}
    pool_mat = sb("pool_mat", [P, TB, NG, T], F32, R1 + 64 * KB)
    pool_w_sb = sb("pool_w_sb", [P, NG, 2, GD], F32, R1 + 72 * KB)
    pool_b_row = sb("pool_b_row", [P, D], F32, R1 + 80 * KB)
    pool_s_row = sb("pool_s_row", [P, D], F32, R1 + 84 * KB)
    mod_rows = sb("mod_rows", [P, 2, D], F32, R1 + 88 * KB)

    ct = sb("consts_sb", [P, K_END], F32, R2)
    cols = sb("cols", [P, 480], F32, R2 + 4 * KB)
    small = sb("small", [P, 256], F32, R2 + 6 * KB)
    ada_acc0 = sb("ada_acc0", [P, 512], F32, R2 + 7 * KB)
    route = sb("route", [P, 256], F32, R2 + 9 * KB)
    tok = sb("tok", [P, TB, D], F32, R2 + 10 * KB)
    S = [R2 + 18 * KB + 8 * KB * i for i in range(6)]
    ctx_tok = sb("ctx_tok", [P, CB, D], F32, S[0])
    rows_in = sb("rows_in", [P, 2, P], F32, S[5])
    ctx_junk = sb("ctx_junk", [P, 2, D], F32, S[4])
    hT = sb("hT", [P, KC, T], F32, S[1])
    mod_two = sb("mod_two", [2, 4, 512], F32, S[1])
    hcT = sb("hcT", [P, KC, C], F32, S[2])
    xn = sb("xn", [P, 2, D], F32, S[3])
    q_tok = [sb(f"q_tok{b}", [P, H, 2, HD], F32, S[2 * b]) for b in range(TB)]
    rope_a = sb("rope_a", [P, 512], F32, S[3])
    rope_b = sb("rope_b", [P, 512], F32, S[3] + 2 * KB)
    k_tok = sb("k_tok", [P, TB + CB, HKV, 2, HD], F32, S[4])
    v_tok = sb("v_tok", [P, TB + CB, KVD], F32, S[5])
    ada_acc1 = sb("ada_acc1", [P, 512], F32, S[3] + 4 * KB)
    ada_acc2 = sb("ada_acc2", [P, 512], F32, R0 + 16 * KB)
    probs = sb("probs", [P, 2, KEYS], F32, S[3])
    probsT = sb("probsT", [P, 2, KEYS], F32, S[3] + 4 * KB)
    o_tok = sb("o_tok", [P, TB, QD], F32, S[1])
    oT = sb("oT", [P, KC, T], F32, S[2])
    g_row = sb("g_row", [P, D], F32, S[0])
    y_tmp = sb("y_tmp", [P, D], F32, S[0] + 4 * KB)
    hf = sb("hf", [P, KC, T], F32, S[2])
    hf_hi = sb("hf_hi", [P, KC, T], F32R, S[4])
    hf_lo = sb("hf_lo", [P, KC, T], F32R, S[1])
    f_act = sb("f_act", [P, TB, FS], F32, S[3])
    fT_hi = sb("fT_hi", [P, 2, TB, P], F32R, S[3] + 2 * KB)
    fT_lo = sb("fT_lo", [P, 2, TB, P], F32R, S[3] + 4 * KB)
    sq_junk = sb("sq_junk", [P, 2, D], F32, S[0])
    pool_y = sb("pool_y", [P, TB, D], F32, S[3])
    g1m_row = sb("g1m_row", [P, D], F32, S[5])
    h_tok = sb("h_tok", [P, TB, D], F32, S[2])
    dT = sb("dT", [P, KC, T], F32, S[1])
    hr = sb("hr", [P, KC, T], F32, S[2])
    xm = sb("xm", [P, TB, D], F32, S[3])
    acc = sb("acc", [P, TB, D], F32, S[1])
    last_row = sb("last_row", [P, D], F32, S[0])
    xe_hi = sb("xe_hi", [P, KC, SLOTS], F32R, S[0])
    xe_lo = [sb(f"xe_lo{h}", [P, KC // 2, SLOTS], F32R, (R2 + 7 * KB, S[5] + KB)[h]) for h in range(2)]
    xe_full = [sb(f"xe_full{h}", [P, KC // 2, SLOTS], F32, (R2 + 7 * KB, S[5] + KB)[h]) for h in range(2)]
    ye_slots = sb("ye_slots", [P, D], F32, S[0])
    me_act = sb("me_act", [P, MS], F32, R2 + 2 * KB)
    hotTe = sb("hotTe", [P, TB, P], F32, S[5] + 3 * KB)
    y_slots = sb("y_slots", [P, D], F32, S[0] + 4 * KB)
    xs_hi = sb("xs_hi", [P, KC, SLOTS], F32R, S[2])
    xs_lo = sb("xs_lo", [P, KC, SLOTS], F32R, S[2] + 4 * KB)
    xs_full = sb("xs_full", [P, KC, SLOTS], F32, S[2] + 4 * KB)
    m_act = sb("m_act", [P, MS], F32, S[4])
    mT_hi = sb("mT_hi", [P, 4, SLOTS], F32R, S[4] + 2 * KB)
    mT_lo = sb("mT_lo", [P, 4, SLOTS], F32R, S[4] + 4 * KB)
    hot = sb("hot", [P, TB, SLOTS], F32, S[4] + 6 * KB)
    hot_g = sb("hot_g", [P, TB, SLOTS], F32, S[4] + 7 * KB)
    hotT = sb("hotT", [P, TB, P], F32, S[5])
    route_w = sb("route_w", [P, KC, E], F32, S[5] + 4 * KB)
    jobs_i = sb("jobs_i", [P, 16], I32, S[5] + 4 * KB + 256)
    jobs_f = sb("jobs_f", [P, 16], F32, S[5] + 4 * KB + 320)
    job_table = sb("job_table", [P, 4, 12], F32, S[5] + 4 * KB + 384)
    job_col = sb("job_col", [P, 4], F32, S[5] + 4 * KB + 576)
    top_i = sb("top_i", [P, 2 * E], U32, S[5] + 4 * KB + 608)
    job_col_e = sb("job_col_e", [P, 4], F32, S[5] + 4 * KB + 672)

    ident = ct[:, K_ID:K_ID + P]
    upper = ct[:, K_UP:K_UP + P]
    iota = ct[:, K_IOTA:K_IOTA + P]
    ones = ct[:, K_ONE:K_ONE + P]

    def cos_of(b):
        return ct[:, K_COS + b * HD:K_COS + (b + 1) * HD]

    def sin_of(b):
        return ct[:, K_SIN + b * HD:K_SIN + (b + 1) * HD]

    def col(a, n):
        return cols[:, a:a + n]

    N_GAIN = 0
    N_B = 80
    N_M0, N_MC, N_M1 = 176, 224, 240
    N_SC = 288
    N_A = 304
    N_G = 344
    N_SINK, N_NSINK, N_RB = 376, 392, 408

    def gain(layer, which):
        return col(N_GAIN + 16 + (layer * 4 + which) * KC, KC)

    R_L, R_TOP, R_TOPI = 0, 16, 32
    R_D, R_EX, R_DEN, R_G1, R_G2 = 48, 50, 52, 54, 56
    R_H1, R_H2, R_MASK, R_GATE, R_POS, R_CNT, R_OVER, R_RANK = 64, 80, 96, 112, 128, 144, 152, 160
    R_JUNK = 240

    SM_NM, SM_SUM, SM_MAX, SM_ES, SM_DEN, SM_RDEN = 64, 96, 128, 160, 192, 224

    J_DOUBLE, J_AFTER, J_LAST = 13, 14, 15

    def job_bounds(eng):
        return (eng.value_load(jobs_i[0:1, J_DOUBLE:J_DOUBLE + 1], min_val=1, max_val=CROWDED),
                eng.value_load(jobs_i[0:1, J_AFTER:J_AFTER + 1], min_val=2, max_val=CROWDED + 1),
                eng.value_load(jobs_i[0:1, J_LAST:J_LAST + 1], min_val=E - 1, max_val=E))

    ps = nc.alloc_psum_tensor("ps", [P, 8, 512], F32)

    def bank(i):
        return ps[:, i, :]

    names = """x_in ctx_in wqkv_in0 wqkv_in1 wqkv_in2 consts_in ada_queued tr2_hi ada_summed ada_rows_taken rows_in sink_in rb_in wo_in ada_in0 ada_in1 ada_in2 ada_late_in
        pool_in cols_turned cols_ready silu_ready ada_used acc_ready colsum_ready mod_ready a_ready nsink_ready
        sumsq_ready msq_ready sqrt_ready rstd_ready dve_step xn_ready turn_ready turned_taken
        qkv_ready kv_lat_taken kv_ctx_taken q_taken q_twice tr2_ready tr2_taken
        scores_ready max_ready nmax_ready probs_ready pt_ready pt_taken pv_ready esink_in esink_ready o_taken
        row_ready row_taken wo_ready y_normed
        f_in0 f_in1 f_in2 f_split0 f_split1 f_split2 f_hi0 f_hi1 f_hi2 f_used0 f_used1 f_used2
        f_silu f_act_ready f_turned f_thi f_tlo hf_hi_ready hf_ready
        pooled pooled_taken poolmix_ready pool_y_ready zeroed
        router_ready diff_ready exp_ready mask_ready ranks_ready route_ready
        m_in0 m_in1 m_in2 m_in3 m_in4 m_in5 m_hi0 m_hi1 m_hi2 m_hi3 m_hi4 m_hi5
        m_split0 m_split1 m_split2 m_split3 m_split4 m_split5 m_used0 m_used1 m_used2 m_used3 m_used4 m_used5
        m_silu m_act_ready m_turned m_thi m_tlo job_col_ready hot_ready gathered xs_ready xs_hi_ready xs_split
        e_hot e_gathered e_xs_ready e_xs_hi e_xs_split e_gated e_silu e_act_ready e_turned e_thi e_tlo e_down
        e_col e_hotg e_hotg_turned e_hotT e_y_taken e_scattered e_added
        y_taken scattered hotg_ready hotg_turned hotT_ready acc_added tok_ready out_done""".split()
    s = {n: nc.alloc_semaphore(n) for n in names}

    ada_v = ada_w.rearrange("l (k p) n -> l p k n", p=P)
    PIECES = 12
    PE_PIECES = 4
    EARLY = PIECES - PE_PIECES + 2
    MIXER_PIECES = 6
    L1_LATE = PIECES - 2
    assert L1_LATE == FSTEPS - 1
    gu_v = ffn_gu[0].rearrange("(k p) n -> p k n", p=P)
    dn_v = ffn_down[0].rearrange("(s q p) n -> s p q n", p=P, q=FS // P)
    mgu_v = moe_gu[0].rearrange("e (k p) n -> e p k n", p=P)
    mdn_v = moe_down[0].rearrange("e (q p) n -> e p q n", p=P)

    NORM_LAT, NORM_CTX, NORM_Y, NORM_F, NORM_POOL_PRE, NORM_POOL, NORM_MOE_PRE, NORM_LAST = 0, 1, 2, 6, 8, 10, 12, 14
    SUMS = [2, 2] + [1] * 14
    SUMS_UNTIL = [sum(SUMS[:n + 1]) for n in range(len(SUMS))]

    def stat(n, what):
        at = 8 * (n % 8) + 2 * what
        return small[:, at:at + SUMS[n]]

    def acc_of(q):
        if not isinstance(q, int) or q >= EARLY or q % 2 == 0:
            return ada_acc0
        return ada_acc1 if q < MIXER_PIECES else ada_acc2

    block = nc.Block()
    block.__enter__()

    @block.sync
    def _(sp):
        sp.dma_start(rows_in[0:8, 0, :], c.rearrange("a (k p) -> (a k) p", p=P)).then_inc(s["rows_in"], 16)
        sp.dma_start(rows_in[8:16, 0, :], c_ctx.rearrange("(k p) -> k p", p=P)).then_inc(s["rows_in"], 16)
        sp.dma_start(ct[:], consts).then_inc(s["consts_in"], 16)
        sp.dma_start(tok[:], x[0].rearrange("(b p) d -> p b d", p=P)).then_inc(s["x_in"], 16)
        sp.dma_start(col(N_SINK, H), sink[0].partition_broadcast(P)).then_inc(s["sink_in"], 16)
        sp.dma_start(col(N_RB, E), router_b[0].partition_broadcast(P)).then_inc(s["rb_in"], 16)
        sp.dma_start(route_w[:], router_w[0].rearrange("(k p) e -> p k e", p=P)).then_inc(s["rb_in"], 16)
        qkv_v = w_qkv[0].rearrange("(k p) n -> p k n", p=P)
        sp.wait_ge(s["ada_queued"], 1)
        sp.dma_start(ctx_tok[:], ctx_in[0].rearrange("(b p) d -> p b d", p=P)).then_inc(s["ctx_in"], 16)
        for i, after, value in ((2, "ada_queued", 1), (0, "ada_in1", 32), (1, "ada_in2", 32)):
            sp.wait_ge(s[after], value)
            sp.dma_start(wqkv[:, :, 512 * i:512 * i + 512], qkv_v[:, :, 512 * i:512 * i + 512]).then_inc(s[f"wqkv_in{i}"], 16)
        sp.wait_ge(s["ada_in0"], 48)
        sp.dma_start(wo_sb[:], w_o[0].rearrange("(k p) n -> p k n", p=P)).then_inc(s["wo_in"], 16)

        def dense_step(st):
            for k in range(2):
                if not isinstance(st, int):
                    sp.wait_ge(s[f"f_split{k}"], st)
                for half, at in ((0, 0), (1, FF)):
                    sp.dma_start(f_raw[k][:, :, half * FS:half * FS + FS],
                                 gu_v[:, 4 * k:4 * k + 4, bass.ds(st * FS + at, FS)]).then_inc(s[f"f_in{k}"], 16)
            if not isinstance(st, int):
                sp.wait_ge(s["f_split2"], st)
            sp.dma_start(f_raw[2][:], dn_v[bass.ds(st, 1)].rearrange("a p q n -> p (a q) n")
                         if not isinstance(st, int) else dn_v[st]).then_inc(s["f_in2"], 16)

        sp.wait_ge(s["qkv_ready"], 8)
        dense_step(0)
        with sp.Fori(1, FSTEPS) as st:
            dense_step(st)

        def expert_load(k, e, i, step):
            if not (isinstance(step, int) and step == 0):
                sp.wait_ge(s[f"m_split{k}"], step + 1)
            if k < 4:
                src = mgu_v[bass.ds(e, 1), :, 4 * (k % 2):4 * (k % 2) + 4, bass.ds(i * MS + (k // 2) * FE, MS)]
            else:
                src = mdn_v[bass.ds(e, 1), :, bass.ds(i * (MS // P) + 2 * (k - 4), 2), :]
            sp.dma_start(m_raw[k][:], src.rearrange("e p k n -> p (e k) n")).then_inc(s[f"m_in{k}"], 16)

        def expert_of(j):
            return sp.value_load(jobs_i[0:1, bass.ds(j, 1)] if not isinstance(j, int) else jobs_i[0:1, j:j + 1],
                                 min_val=0, max_val=E - 1)

        def job_loads(j, e, last=False):
            step = j * MSTEPS
            with sp.Fori(0, MSTEPS - 1) as i:
                for k in range(4):
                    expert_load(k, e, i + 1, step + i + 1)
                for k in (4, 5):
                    expert_load(k, e, i, step + i)
            if not last:
                if isinstance(j, int):
                    sp.wait_ge(s["route_ready"], 1)
                e_next = expert_of(j + 1)
                for k in range(4):
                    expert_load(k, e_next, 0, step + MSTEPS)
            for k in (4, 5):
                expert_load(k, e, MSTEPS - 1, step + MSTEPS - 1)

        for k in range(4):
            if k == 3:
                sp.wait_ge(s["f_split0"], FSTEPS)
            expert_load(k, 0, 0, 0)
        for k in (1, 2):
            sp.wait_ge(s[f"f_split{k}"], FSTEPS)
        job_loads(0, 0)
        last_job = job_bounds(sp)[2]
        with sp.Fori(1, last_job) as j:
            job_loads(j, expert_of(j))
        job_loads(last_job, expert_of(last_job), last=True)

        for b in range(TB):
            sp.wait_ge(s["tok_ready"], b + 1)
            sp.dma_start(out[0].rearrange("(b p) d -> p b d", p=P)[:, b, :], tok[:, b, :]).then_inc(s["out_done"], 16)
        sp.wait_ge(s["out_done"], 16 * TB)

    @block.gpsimd
    def _(pool):
        for i in range(PIECES + PIECES - L1_LATE):
            l, n = divmod(i, PIECES)
            if i >= 3:
                if i - 3 < PE_PIECES:
                    pool.wait_ge(s["ada_used"], i - 2)
                else:
                    pool.wait_ge(s["acc_ready"], KC * (i - 2 - PE_PIECES))
            pool.dma_start(ada_ring[i % 3][:], ada_v[l, :, :, 512 * n:512 * n + 512]).then_inc(s[f"ada_in{i % 3}"], 16)
            if i == PE_PIECES - 1:
                pool.sem_inc(s["ada_queued"], 1)
        with pool.Fori(0, L1_LATE) as n:
            pool.wait_ge(s["acc_ready"], (n + EARLY) * KC)
            pool.dma_start(ada_ring[0][:], ada_v[1, :, :, bass.ds(n * 512 + 512 * (PIECES - L1_LATE), 512)]
                           ).then_inc(s["ada_late_in"], 16)
        pool.dma_start(pool_mat[:], pool_m.rearrange("p (b g t) -> p b g t", b=TB, g=NG)).then_inc(s["pool_in"], 16)
        pool.dma_start(pool_w_sb[:], pool_w[0].rearrange("g (k p) n -> p g k n", p=P)).then_inc(s["pool_in"], 16)
        pool.dma_start(pool_b_row[:], pool_b[0].partition_broadcast(P)).then_inc(s["pool_in"], 16)
        pool.dma_start(pool_s_row[:], pool_scale[0].partition_broadcast(P)).then_inc(s["pool_in"], 16)

        pool.wait_ge(s["sqrt_ready"], NORM_MOE_PRE + TB)
        pool.memset(acc[:], 0.0).then_inc(s["zeroed"], 1)
        pool.memset(hotT[:], 0.0).then_inc(s["hotT_ready"], 1)
        pool.memset(y_slots[:], 0.0).then_inc(s["y_taken"], 1)

    FILL_BANKS = (1, 2)

    @block.tensor
    def _(pe):
        for k in (4, 5):
            pe.sem_inc(s[f"m_used{k}"], 1)
        pe.sem_inc(s["f_used2"], 1)
        pe.sem_inc(s["f_turned"], 1)
        pe.sem_inc(s["m_turned"], 1)

        pe.wait_ge(s["rows_in"], 64)
        pe.wait_ge(s["consts_in"], 16)
        pe.transpose(ps[:, 0, 0:80], rows_in[0:80, 0, :], ident[0:80, 0:80])
        pe.transpose(ps[:, 0, 80:176], rows_in[0:96, 1, :], ident[0:96, 0:96]).then_inc(s["cols_turned"], 1)

        pe.wait_ge(s["silu_ready"], 1)

        def mod_columns(i):
            pe.wait_ge(s["ada_rows_taken"], i + 1)
            for n in range(4):
                at = 2 * (4 * i + n)
                mm = pe.transpose(ps[:, 0, at:at + 2], mod_two[:, i, n * P:(n + 1) * P], ident[0:2, 0:2])
            mm.then_inc(s["ada_summed"], 1)

        for i in range(PE_PIECES):
            pe.wait_ge(s[f"ada_in{i % 3}"], 16 * (i // 3 + 1))
            for k in range(KC):
                mm = pe.matmul(ps[0:2, 3 + i, :], cols[:, N_SC + 2 * k:N_SC + 2 * k + 2], ada_ring[i % 3][:, k, :],
                               start=(k == 0), stop=(k == KC - 1))
            mm.then_inc(s["ada_used"], 1)
            if i >= 1:
                mod_columns(i - 1)
        mod_columns(PE_PIECES - 1)

        fills = [0]

        def turn_fill(src, f):
            n = fills[0]
            fills[0] += 1
            if n >= 2:
                pe.wait_ge(s["turned_taken"], n - 1)
            for k in range(2):
                for b in range(2):
                    tr = pe.transpose(ps[:, FILL_BANKS[n % 2], (2 * k + b) * P:(2 * k + b + 1) * P],
                                      src[:, b, (2 * f + k) * P:(2 * f + k + 1) * P], ident)
            tr.then_inc(s["turn_ready"], 1)

        for seq in range(2):
            pe.wait_ge(s["xn_ready"], 2 * seq + 2)
            for f in range(4):
                turn_fill((xn, ctx_tok)[seq], f)

        def column_sums(q):
            pe.wait_ge(s["acc_ready"], (q + 1) * KC)
            if isinstance(q, int) and q == 0:
                pe.wait_ge(s["a_ready"], 1)
            else:
                pe.wait_ge(s["mod_ready"], q)
            for n in range(4):
                mm = pe.matmul(ps[:, 0, n:n + 1], acc_of(q)[:, n * P:n * P + P], ones[:, 0:1], start=True, stop=True)
            mm.then_inc(s["colsum_ready"], 1)

        def turn_keys(g):
            if g >= 2:
                pe.wait_ge(s["tr2_taken"], g - 1)
            else:
                pe.wait_ge(s["turned_taken"], 7 + g)
            if g == 0:
                pe.wait_ge(s["kv_lat_taken"], 2)
                pe.wait_ge(s["kv_ctx_taken"], 2)
            for t in range(4):
                tr = pe.transpose(ps[:, 1 + g % 2, t * P:(t + 1) * P], k_tok[:, KEY_ORDER[t], g, :, :], ident)
            tr.then_inc(s["tr2_ready"], 1)

        UNITS = [("lat", 0, 2), ("lat", 1, 2), ("ctx", 0, 2), ("ctx", 1, 2),
                 ("lat", 0, 0), ("lat", 1, 0), ("lat", 0, 1), ("lat", 1, 1)]
        for u, (seq, b, n) in enumerate(UNITS):
            if u == 0:
                pe.wait_ge(s["turned_taken"], 4)
                pe.wait_ge(s["wqkv_in2"], 16)
            if u == 2:
                pe.wait_ge(s["turned_taken"], 8)
            if u in (4, 6):
                pe.wait_ge(s[f"wqkv_in{n}"], 16)
            if u in (4, 5):
                pe.wait_ge(s["kv_lat_taken"], u - 3)
            if u in (6, 7):
                pe.wait_ge(s["kv_ctx_taken"], u - 5)
            src = hT if seq == "lat" else hcT
            for k in range(KC):
                mm = pe.matmul(bank(3 + u % 4), src[:, k, b * P:(b + 1) * P],
                               wqkv[:, k, 512 * n:512 * n + 512], start=(k == 0), stop=(k == KC - 1))
            mm.then_inc(s["qkv_ready"], 1)
            if u >= 2:
                column_sums(u - 2)
            if u == 6:
                for g in (0, 1):
                    turn_keys(g)

        for g in (2, 3):
            turn_keys(g)
        for f in range(H // 2):
            pe.wait_ge(s["q_twice"], 2 * (f // 4) + 2)
            if f not in (2, 3):
                pe.wait_ge(s["tr2_taken"], 3 + f if f < 2 else 1 + f)
            for k in range(2):
                for b in range(TB):
                    tr = pe.transpose(ps[:, 1 + f % 4, (2 * k + b) * P:(2 * k + b + 1) * P],
                                      q_tok[b][:, 2 * f + k, :, :], ident)
            tr.then_inc(s["tr2_ready"], 1)

        OB = [7, 1, 7, 1]
        SB = [3, 4, 2]

        def scores(u):
            b, h = divmod(u, H)
            g = h // GROUP
            if u >= 3:
                pe.wait_ge(s["probs_ready"], u - 2)
            if u == 0:
                pe.wait_ge(s["tr2_taken"], 12)
                pe.wait_ge(s["q_taken"], 4)
            lhs = q_parts[:, h, b * P:(b + 1) * P]
            other = (3 * P, 0)[b]
            pe.matmul(ps[:, SB[u % 3], other:other + P], ident, ct[:, K_MASK + b * P:K_MASK + (b + 1) * P],
                      start=True, stop=False)
            for at, to in ((other, other + P), ((0, 3 * P), (P, KEYS))[b]):
                pe.matmul(ps[:, SB[u % 3], at:to], lhs, k_hi[:, g, at:to], start=(at != other), stop=False)
                mm = pe.matmul(ps[:, SB[u % 3], at:to], lhs, k_lo[:, g, at:to], start=False, stop=True)
            mm.then_inc(s["scores_ready"], 1)

        def turn_probs(u):
            pe.wait_ge(s["probs_ready"], u + 1)
            if u >= 2:
                pe.wait_ge(s["pt_taken"], u - 1)
            for t in range(4):
                tr = pe.transpose(ps[:, 5 + u % 2, t * P:(t + 1) * P], probs[:, u % 2, t * P:(t + 1) * P], ident)
            tr.then_inc(s["pt_ready"], 1)

        def weigh_values(u):
            b, h = divmod(u, H)
            og = u // 8
            if u in (16, 24):
                pe.wait_ge(s["o_taken"], u // 8 - 1)
            pe.wait_ge(s["pt_taken"], u + 1)
            at = (h % 8) * HD
            for t in range(4):
                mm = pe.matmul(ps[:, OB[og], at:at + HD], probsT[:, u % 2, t * P:(t + 1) * P],
                               v_tok[:, KEY_ORDER[t], (h // GROUP) * HD:(h // GROUP + 1) * HD], start=(t == 0), stop=(t == 3))
            mm.then_inc(s["pv_ready"], 1)

        NU = TB * H
        for u in range(NU + 3):
            if u < NU:
                scores(u)
            if 2 <= u <= NU + 1:
                turn_probs(u - 2)
            if u >= 3:
                weigh_values(u - 3)
            if u % KC == 2 and u > KC:
                column_sums(MIXER_PIECES + u // KC - 1)

        for og in range(4):
            pe.wait_ge(s["o_taken"], og + 1)
            pe.wait_ge(s["pt_taken"], NU - 1 + og)
            for k in range(4):
                tr = pe.transpose(ps[:, 5 + og % 2, k * P:(k + 1) * P],
                                  o_tok[:, og // 2, (4 * (og % 2) + k) * P:(4 * (og % 2) + k + 1) * P], ident)
            tr.then_inc(s["pt_ready"], 1)

        def spread_row(src_col, banks, n):
            for f in range(2):
                if n + f >= 2 and n != 6:
                    pe.wait_ge(s["row_taken"], n + f - 1)
                for k in range(4):
                    v = cols[:, src_col + 4 * f + k:src_col + 4 * f + k + 1].to_broadcast([P, P])
                    mm = pe.matmul(ps[:, banks[f], k * P:(k + 1) * P], v, ident, start=True, stop=True)
                mm.then_inc(s["row_ready"], 1)

        pe.wait_ge(s["a_ready"], 3)
        pe.wait_ge(s["o_taken"], 4)
        spread_row(N_G, (0, 7), 0)

        def turn_block(b):
            pe.wait_ge(s["xn_ready"], 5 + b)
            if b == 1:
                pe.wait_ge(s["y_normed"], 1)
            for half in range(2):
                for k in range(4):
                    tr = pe.transpose(ps[:, 1 + 2 * b + half, k * P:(k + 1) * P],
                                      xn[:, b, (4 * half + k) * P:(4 * half + k + 1) * P], ident)
                tr.then_inc(s["turn_ready"], 1)
                fills[0] += 1

        pe.wait_ge(s["wo_in"], 16)
        for b in range(TB):
            pe.wait_ge(s["pt_taken"], NU + 2 * b + 2)
            for half in range(2):
                for k in range(KC):
                    if (b, half, k) == (1, 1, 3):
                        turn_block(0)
                    mm = pe.matmul(bank(3 + 2 * b + half), oT[:, k, b * P:(b + 1) * P],
                                   wo_sb[:, k, 512 * half:512 * half + 512], start=(k == 0), stop=(k == KC - 1))
                mm.then_inc(s["wo_ready"], 1)

        def gate_up_block(k, b):
            for kk in range(4):
                hi = hf_hi[:, 4 * k + kk, b * P:(b + 1) * P]
                lo = hf_lo[:, 4 * k + kk, b * P:(b + 1) * P]
                first, last = k == 0 and kk == 0, k == 1 and kk == 3
                pe.matmul(bank(1 + b), hi, f_hi[k][:, kk, :], start=first, stop=False)
                pe.matmul(bank(1 + b), hi, f_lo[k][:, kk, :], start=False, stop=False)
                mm = pe.matmul(bank(1 + b), lo, f_hi[k][:, kk, :], start=False, stop=last)
            return mm

        def gate_up(st, k):
            pe.wait_ge(s[f"f_split{k}"], st + 1)
            if k == 0:
                pe.wait_ge(s["f_act_ready"], st)
            gate_up_block(k, 0)
            gate_up_block(k, 1).then_inc(s[f"f_used{k}"], 1)

        def gate_up_first():
            pe.wait_ge(s["turned_taken"], 10)
            for b in range(TB):
                for k in range(2):
                    pe.wait_ge(s["hf_ready"], 2 * b + k + 1)
                    pe.wait_ge(s[f"f_split{k}"], 1)
                    mm = gate_up_block(k, b)
                    if b == 1:
                        mm.then_inc(s[f"f_used{k}"], 1)
                    elif k == 0:
                        spread_row(N_G + KC, (0, 7), 2)
                        turn_block(1)

        def turn_act(st):
            pe.wait_ge(s["f_act_ready"], st + 1)
            if not (isinstance(st, int) and st == 0):
                pe.wait_ge(s["f_tlo"], st)
            for q in range(2):
                for b in range(TB):
                    tr = pe.transpose(ps[:, 7, (2 * q + b) * P:(2 * q + b + 1) * P],
                                      f_act[:, b, q * P:(q + 1) * P], ident)
            tr.then_inc(s["f_turned"], 1)

        def down(st, first=False, last=False):
            pe.wait_ge(s["f_split2"], st + 1)
            pe.wait_ge(s["f_tlo"], st + 1)
            for q in range(2):
                for b in range(TB):
                    for lhs, rhs in ((fT_hi, f_hi[2]), (fT_hi, f_lo[2]), (fT_lo, f_hi[2])):
                        for half in range(2):
                            mm = pe.matmul(bank(3 + 2 * b + half), lhs[:, q, b, :], rhs[:, q, 512 * half:512 * half + 512],
                                           start=(first and q == 0 and lhs is fT_hi and rhs is f_hi[2]),
                                           stop=(last and q == 1 and lhs is fT_lo), skip_group_check=True)
            mm.then_inc(s["f_used2"], 1)

        gate_up_first()
        pe.wait_ge(s["row_taken"], 4)
        gate_up(1, 0)
        turn_act(0)
        gate_up(1, 1)
        column_sums(EARLY)
        down(0, first=True)
        with pe.Fori(2, FSTEPS) as st:
            gate_up(st, 0)
            turn_act(st - 1)
            gate_up(st, 1)
            column_sums(st + EARLY - 1)
            down(st - 1)
        turn_act(FSTEPS - 1)
        down(FSTEPS - 1, last=True)

        pe.wait_ge(s["a_ready"], 4)
        pe.wait_ge(s["f_act_ready"], FSTEPS)
        pe.wait_ge(s["f_tlo"], FSTEPS)
        for r, (src, banks) in enumerate(((N_A + 3 * KC, (1, 2)), (N_M1, (7, 0)), (N_G + 2 * KC, (1, 2)))):
            spread_row(src, banks, 2 * r + 4)

        POOL_BANKS = (7, 0, 1, 2)
        pe.wait_ge(s["pool_in"], 64)
        for b in range(TB):
            pe.wait_ge(s["y_normed"], 3 + b)
            for g in range(NG):
                pe.matmul(ps[:, 3 + 2 * b + g // 2, (g % 2) * GD:(g % 2 + 1) * GD], ident,
                          pool_b_row[:, g * GD:(g + 1) * GD], start=(g % 2 == 0), stop=False, skip_group_check=True)

        def pool_group(g, b):
            for k in range(2):
                mm = pe.matmul(ps[:, POOL_BANKS[g], k * T:(k + 1) * T], h_tok[:, b, (2 * g + k) * P:(2 * g + k + 1) * P],
                               pool_mat[:, b, g, :], start=(b == 0 and k == 0), stop=(b == TB - 1), skip_group_check=True)
            if b == TB - 1:
                mm.then_inc(s["pooled"], 1)

        def mix_group(g):
            pe.wait_ge(s["pooled_taken"], g + 1)
            for b in range(TB):
                for k in range(2):
                    mm = pe.matmul(ps[:, 3 + 2 * b + g // 2, (g % 2) * GD:(g % 2 + 1) * GD],
                                   dT[:, 2 * g + k, b * P:(b + 1) * P], pool_w_sb[:, g, k, :],
                                   start=False, stop=(k == 1), skip_group_check=True)
                if g == NG - 1:
                    mm.then_inc(s["poolmix_ready"], 1)

        pe.wait_ge(s["xn_ready"], 7)
        for g in range(NG):
            if g == 0:
                pe.wait_ge(s["row_taken"], 8)
            if g == 2:
                pe.wait_ge(s["row_taken"], 10)
            pool_group(g, 0)
        pe.wait_ge(s["xn_ready"], 8)
        pool_group(0, 1)
        pool_group(1, 1)
        for g in range(2, NG):
            pool_group(g, 1)
            mix_group(g - 2)
        mix_group(NG - 2)
        mix_group(NG - 1)

        pe.wait_ge(s["pooled_taken"], NG)
        pe.wait_ge(s["xn_ready"], 10)
        pe.wait_ge(s["rb_in"], 16 * 2)

        def router(f):
            pe.wait_ge(s["turned_taken"], 13 + f)
            for k in (2 * f, 2 * f + 1):
                for b in range(TB):
                    mm = pe.matmul(ps[:, (7, 0)[b], 0:E], hr[:, k, b * P:(b + 1) * P], route_w[:, k, :],
                                   start=(k == 0), stop=(k == KC - 1))
            if f == 3:
                mm.then_inc(s["router_ready"], 1)

        for f in range(4):
            turn_fill(xm, f)
            if f:
                router(f - 1)
        router(3)
        pe.wait_ge(s["mask_ready"], 1)
        m0, m1 = route[:, R_MASK:R_MASK + E], route[:, R_MASK + E:R_MASK + 2 * E]
        pe.matmul(ps[:, 1, 0:E], upper, m0, start=True, stop=True)
        pe.matmul(ps[:, 1, E:2 * E], upper, m1, start=True, stop=False)
        pe.matmul(ps[:, 1, E:2 * E], ones, m0, start=False, stop=True).then_inc(s["ranks_ready"], 1)
        pe.matmul(ps[:, 2, 0:E], ones, m0, start=True, stop=False)
        pe.matmul(ps[:, 2, 0:E], ones, m1, start=False, stop=True).then_inc(s["ranks_ready"], 1)

        def gather(sem, banks=(5, 6)):
            for k in range(KC):
                for b in range(TB):
                    mm = pe.matmul(ps[:, banks[k // 4], (k % 4) * P:(k % 4 + 1) * P], xm[:, b, k * P:(k + 1) * P],
                                   hot[:, b, :], start=(b == 0), stop=(b == TB - 1))
                if k % 4 == 3:
                    mm.then_inc(sem, 1)

        def gate_up_slot(k, x_hi, x_lo):
            b = 1 + k // 2
            for kk in range(4):
                kc = 4 * (k % 2) + kk
                first, last = kc == 0, kc == KC - 1
                pe.matmul(bank(b), x_hi(kc), m_hi[k][:, kk, :], start=first, stop=False)
                pe.matmul(bank(b), x_hi(kc), m_lo[k][:, kk, :], start=False, stop=False)
                mm = pe.matmul(bank(b), x_lo(kc), m_hi[k][:, kk, :], start=False, stop=last)
            return mm

        def expert_gate_up(k, step):
            pe.wait_ge(s[f"m_split{k}"], step + 2)
            gate_up_slot(k, lambda kc: xs_hi[:, kc, :], lambda kc: xs_lo[:, kc, :]).then_inc(s[f"m_used{k}"], 1)

        def expert_turn(step):
            pe.wait_ge(s["m_act_ready"], step + 2)
            pe.wait_ge(s["m_tlo"], step + 1)
            for q in range(4):
                tr = pe.transpose(ps[:, 7, q * P:(q + 1) * P], m_act[:, q * P:(q + 1) * P], ident)
            tr.then_inc(s["m_turned"], 1)

        def down_slot(k, to, high, low, first, last):
            for q in range(2):
                for lhs, rhs in ((mT_hi, high[k]), (mT_hi, low[k]), (mT_lo, high[k])):
                    for half in range(2):
                        mm = pe.matmul(bank(to + half), lhs[:, 2 * (k - 4) + q, :], rhs[:, q, 512 * half:512 * half + 512],
                                       start=(first and k == 4 and q == 0 and lhs is mT_hi and rhs is high[k]),
                                       stop=(last and k == 5 and q == 1 and lhs is mT_lo), skip_group_check=True)
            return mm

        def expert_down(step, first=False, last=False, split=None):
            high, low = (m_hi, m_lo) if split is None else split
            pe.wait_ge(s["m_tlo"], step + 2)
            for k in (4, 5):
                pe.wait_ge(s[f"m_split{k}"], step + 2)
                down_slot(k, 3, high, low, first, last).then_inc(s[f"m_used{k}"], 1)

        def scatter(j, n):
            b, half = divmod(n, 2)
            pe.matmul(bank((5, 6, 0, 5)[n]), hotT[:, b, :], y_slots[:, 512 * half:512 * half + 512],
                      start=True, stop=True).then_inc(s["scattered"], 1)

        def outputs_back(j):
            pe.wait_ge(s["y_taken"], j + 1)
            pe.wait_ge(s["hotT_ready"], j + 1)
            for n in range(3):
                scatter(j, n)

        def outputs_back_end(j):
            pe.wait_ge(s["acc_added"], 4 * j + 1)
            scatter(j, 3)
            pe.wait_ge(s["acc_added"], 4 * j + 2)
            pe.wait_ge(s["hotg_ready"], j + 1)
            for b in range(TB):
                tr = pe.transpose(ps[:, 6, b * P:(b + 1) * P], hot_g[:, b, :], ident)
            tr.then_inc(s["hotg_turned"], 1)

        def extra_turn(v):
            pe.wait_ge(s["e_act_ready"], v + 1)
            for q in range(4):
                tr = pe.transpose(ps[:, 7, q * P:(q + 1) * P], me_act[:, q * P:(q + 1) * P], ident)
            tr.then_inc(s["e_turned"], 1)

        def extra_down(v, step, first=False, last=False):
            pe.wait_ge(s["e_tlo"], v + 1)
            for k in (4, 5):
                pe.wait_ge(s[f"m_split{k}"], step + 2)
                mm = down_slot(k, 5, m_hi, m_lo, first, last)
            if last:
                mm.then_inc(s["e_down"], 1)

        def extra_step(c, i, step):
            v = c * MSTEPS + i
            first = isinstance(i, int) and i == 0
            pe.wait_ge(s["m_act_ready"], step + 1)
            for k in range(4):
                if first and k < 2:
                    pe.wait_ge(s["e_xs_split"], 2 * c + 1 + k)
                pe.wait_ge(s[f"m_split{k}"], step + 2)
                mm = gate_up_slot(k, lambda kc: xe_hi[:, kc, :], lambda kc: xe_lo[kc // 4][:, kc % 4, :])
                if k == 1 and not first:
                    extra_turn(v - 1)
            mm.then_inc(s["e_gated"], 1)
            if first:
                outputs_back(c + 1)
            else:
                extra_down(v - 1, step - 1, first=isinstance(i, int) and i == 1)
            pe.wait_ge(s["e_act_ready"], v + 1)

        def job(j, last, c=None):
            step = j * MSTEPS
            if c is not None:
                pe.wait_ge(s["e_hot"], c + 1)
                pe.wait_ge(s["xs_ready"], 2 * j + 2)
                gather(s["e_gathered"])
                extra_step(c, 0, step)
            pe.wait_ge(s["m_act_ready"], step + 1)
            for k in range(4):
                if k < 2:
                    pe.wait_ge(s["xs_split"], 2 * j + 1 + k)
                expert_gate_up(k, step)
            if c is not None:
                outputs_back_end(j)
                pe.wait_ge(s["acc_added"], 4 * j + 4)
                pe.wait_ge(s["hotT_ready"], j + 2)
                extra_step(c, 1, step + 1)
            pe.wait_ge(s["m_act_ready"], step + 2)
            expert_gate_up(0, step + 1)
            expert_gate_up(1, step + 1)
            expert_turn(step)
            if c is None:
                outputs_back(j)
            expert_gate_up(2, step + 1)
            expert_gate_up(3, step + 1)
            if c is None:
                outputs_back_end(j)
            else:
                pe.wait_ge(s["e_hotg"], c + 1)
                for b in range(TB):
                    tr = pe.transpose(ps[:, 0, b * P:(b + 1) * P], hot_g[:, b, :], ident)
                tr.then_inc(s["e_hotg_turned"], 1)
            expert_down(step, first=True)
            with pe.Fori(2, MSTEPS) as i:
                st = step + i
                if c is not None:
                    extra_step(c, i, st)
                pe.wait_ge(s["m_act_ready"], st + 1)
                expert_gate_up(0, st)
                expert_gate_up(1, st)
                expert_turn(st - 1)
                expert_gate_up(2, st)
                expert_gate_up(3, st)
                expert_down(st - 1)
            end = step + MSTEPS - 1
            if c is not None:
                extra_turn(c * MSTEPS + MSTEPS - 1)
                pe.wait_ge(s["hot_ready"], j + 2)
                pe.wait_ge(s["m_act_ready"], end + 2)
                gather(s["gathered"], (1, 2))
                extra_down(c * MSTEPS + MSTEPS - 1, end, last=True)
                expert_turn(end)
                expert_down(end, last=True)
                pe.wait_ge(s["e_y_taken"], c + 1)
                pe.wait_ge(s["e_hotT"], c + 1)
                for n in range(4):
                    b, half = divmod(n, 2)
                    pe.matmul(bank((5, 6, 0, 7)[n]), hotTe[:, b, :], ye_slots[:, 512 * half:512 * half + 512],
                              start=True, stop=True).then_inc(s["e_scattered"], 1)
                pe.wait_ge(s["e_added"], 4 * c + 4)
                return
            expert_turn(end)
            if not last:
                pe.wait_ge(s["hot_ready"], j + 2)
                pe.wait_ge(s["hotT_ready"], j + 2)
                pe.wait_ge(s["acc_added"], 4 * j + 4)
                gather(s["gathered"])
            else:
                pe.wait_ge(s["hotT_ready"], j + 2)
                pe.wait_ge(s["acc_added"], 4 * j + 4)
                for f in range(2):
                    for k in range(4):
                        at = N_G + 3 * KC + 4 * f + k
                        mm = pe.matmul(ps[:, 5 + f, k * P:(k + 1) * P], cols[:, at:at + 1].to_broadcast([P, P]),
                                       ident, start=True, stop=True)
                    mm.then_inc(s["row_ready"], 1)
            expert_down(end, last=True, split=(last_hi, last_lo) if last else None)

        pe.wait_ge(s["hot_ready"], 1)
        gather(s["gathered"])
        job(0, False)
        pe.wait_ge(s["route_ready"], 1)
        doubles, after, last_job = job_bounds(pe)
        with pe.Fori(0, doubles) as c:
            job(c + 1, False, c)
        with pe.Fori(after, last_job) as j:
            job(j, False)
        j = last_job
        job(j, True)
        pe.wait_ge(s["y_taken"], j + 2)
        pe.wait_ge(s["row_taken"], 12)
        for n in range(3):
            scatter(j, n)
        pe.wait_ge(s["acc_added"], 4 * j + 5)
        scatter(j, 3)

    @block.scalar
    def _(act):
        def squares(n, pairs):
            for b, (src, junk) in enumerate(pairs):
                act.activation(junk, src, ACT.Square, accum_out=stat(n, 0)[:, b:b + 1]).then_inc(s["sumsq_ready"], 1)

        def root(n):
            act.wait_ge(s["msq_ready"], n + 1)
            act.activation(stat(n, 2), stat(n, 1), ACT.Sqrt).then_inc(s["sqrt_ready"], 1)

        def load_table(func, n):
            at = (57, 59, 61, 63, 49, 51)[n]
            act.activation(small[:, at:at + 1], ones[:, 0:1], func)

        act.dma_start(rows_in[16:80, 0, :], norm_g.rearrange("l w (k p) -> (l w k) p", p=P)).then_inc(s["rows_in"], 16)
        act.dma_start(rows_in[0:96, 1, :], ada_b.rearrange("l (k p) -> (l k) p", p=P)).then_inc(s["rows_in"], 16)
        act.wait_ge(s["cols_ready"], 1)
        act.activation(cols[:, N_SC:N_SC + 2 * KC].rearrange("p (k a) -> p k a", a=2),
                       cols[:, 0:2 * KC].rearrange("p (a k) -> p k a", a=2), ACT.Silu).then_inc(s["silu_ready"], 1)
        act.wait_ge(s["x_in"], 16)
        squares(NORM_LAT, [(tok[:, b, :], xn[:, b, :]) for b in range(TB)])
        root(NORM_LAT)
        act.wait_ge(s["ctx_in"], 16)
        squares(NORM_CTX, [(ctx_tok[:, b, :], ctx_junk[:, b, :]) for b in range(CB)])
        root(NORM_CTX)

        for i in range(PE_PIECES):
            act.wait_ge(s["ada_used"], i + 1)
            act.activation(mod_two[:, i, :], ps[0:2, 3 + i, :], ACT.Copy).then_inc(s["ada_rows_taken"], 1)

        for b in range(CB):
            act.wait_ge(s["qkv_ready"], 3 + b)
            kv = bank(3 + 2 + b)
            for twice in range(2):
                act.activation(k_tok[:, TB + b, :, twice, :], kv[:, 0:KVD].rearrange("p (g d) -> p g d", g=HKV), ACT.Copy)
            act.activation(v_tok[:, TB + b, :], kv[:, KVD:2 * KVD], ACT.Copy).then_inc(s["kv_ctx_taken"], 1)
        def copy_queries(n):
            act.wait_ge(s["q_taken"], n + 1)
            heads, b = slice(8 * (n // TB), 8 * (n // TB) + 8), n % TB
            act.activation(q_tok[b][:, heads, 1, :], q_tok[b][:, heads, 0, :], ACT.Copy).then_inc(s["q_twice"], 1)

        def keys_hi(g):
            act.wait_ge(s["tr2_ready"], g + 1)
            act.activation(k_hi[:, g, :], bank(1 + g % 2), ACT.Copy).then_inc(s["tr2_hi"], 1)

        for n in range(3):
            copy_queries(n)
        keys_hi(0)
        keys_hi(1)
        copy_queries(3)
        keys_hi(2)
        keys_hi(3)
        for f in range(H // 2):
            act.wait_ge(s["tr2_ready"], HKV + 1 + f)
            act.activation(q_parts[:, 2 * f:2 * f + 2, :], bank(1 + f % 4).rearrange("p (k t) -> p k t", k=2),
                           ACT.Copy).then_inc(s["tr2_hi"], 1)

        NU = TB * H

        def take_turned(u):
            act.wait_ge(s["pt_ready"], u + 1)
            if u >= 2:
                act.wait_ge(s["pv_ready"], u - 1)
            act.activation(probsT[:, u % 2, :], bank(5 + u % 2), ACT.Copy).then_inc(s["pt_taken"], 1)

        SB = [3, 4, 2]
        for u in range(NU):
            if u >= 2:
                take_turned(u - 2)
            act.wait_ge(s["nmax_ready"], u + 1)
            act.activation(probs[:, u % 2, :], bank(SB[u % 3]), ACT.Exp, bias=small[:, SM_NM + u:SM_NM + u + 1],
                           scale=HD ** -0.5, accum_out=small[:, SM_SUM + u:SM_SUM + u + 1]).then_inc(s["probs_ready"], 1)
            if u % 8 == 7:
                og = u // 8
                act.wait_ge(s["esink_in"], og + 1)
                act.activation(small[:, SM_ES + 8 * og:SM_ES + 8 * og + 8], small[:, SM_ES + 8 * og:SM_ES + 8 * og + 8],
                               ACT.Exp).then_inc(s["esink_ready"], 1)
        take_turned(NU - 2)
        take_turned(NU - 1)
        for og in range(4):
            act.wait_ge(s["pt_ready"], NU + og + 1)
            act.activation(oT[:, 4 * (og % 2):4 * (og % 2) + 4, (og // 2) * P:(og // 2 + 1) * P],
                           bank(5 + og % 2).rearrange("p (k t) -> p k t", k=4), ACT.Copy).then_inc(s["pt_taken"], 1)

        def take_row(dst, banks, n):
            for f in range(2):
                act.wait_ge(s["row_ready"], n + f + 1)
                act.activation(dst[:, 512 * f:512 * f + 512], bank(banks[f]), ACT.Copy).then_inc(s["row_taken"], 1)

        take_row(g_row, (0, 7), 0)

        def dense_hi(k, st):
            act.wait_ge(s[f"f_in{k}"], (st + 1) * (32 if k < 2 else 16))
            if k == 2:
                act.wait_ge(s["f_used2"], st + 1)
            elif not (isinstance(st, int) and st == 0):
                act.wait_ge(s[f"f_used{k}"], st)
            act.activation(f_hi[k][:], f_raw[k][:], ACT.Copy).then_inc(s[f"f_hi{k}"], 1)

        load_table(ACT.Sqrt, 4)
        dense_hi(0, 0)
        for b in range(TB):
            act.wait_ge(s["wo_ready"], 2 * b + 2)
            y = ps[:, 3 + 2 * b:5 + 2 * b, :]
            if b == 1:
                act.wait_ge(s["y_normed"], 1)
            squares(NORM_Y + 2 * b, [(y, y_tmp[:].rearrange("p (a n) -> p a n", a=2))])
            root(NORM_Y + 2 * b)
            if b == 1:
                dense_hi(1, 0)
            act.wait_ge(s["y_normed"], b + 1)
            squares(NORM_Y + 2 * b + 1, [(tok[:, b, :], xn[:, b, :])])
            root(NORM_Y + 2 * b + 1)
            for half in range(2):
                act.wait_ge(s["turned_taken"], 9 + 2 * b + half)
                act.activation(hf_hi[:, 4 * half:4 * half + 4, b * P:(b + 1) * P],
                               hf[:, 4 * half:4 * half + 4, b * P:(b + 1) * P], ACT.Copy).then_inc(s["hf_hi_ready"], 1)

        def dense_silu(st):
            act.wait_ge(s["f_used1"], st + 1)
            act.wait_ge(s["f_turned"], st + 1)
            act.activation(f_act[:], ps[:, 1:3, 0:FS], ACT.Silu).then_inc(s["f_silu"], 1)

        def dense_turned_hi(st):
            act.wait_ge(s["f_turned"], st + 2)
            act.wait_ge(s["f_used2"], st + 1)
            act.activation(fT_hi[:].rearrange("p q b t -> p (q b t)"), bank(7), ACT.Copy).then_inc(s["f_thi"], 1)

        load_table(ACT.Silu, 5)
        take_row(g_row, (0, 7), 2)

        def dense_iteration(st, first=False, last=False):
            if not first:
                dense_turned_hi(st - 1)
            if not last:
                dense_hi(0, st + 1)
            dense_silu(st)
            if not last:
                dense_hi(1, st + 1)
            dense_hi(2, st)

        dense_iteration(0, first=True)
        with act.Fori(1, FSTEPS - 1) as st:
            dense_iteration(st)
        dense_iteration(FSTEPS - 1, last=True)
        dense_turned_hi(FSTEPS - 1)

        load_table(ACT.Sqrt, 0)
        act.wait_ge(s["f_used2"], FSTEPS + 1)
        for b in range(TB):
            squares(NORM_F + b, [(ps[:, 3 + 2 * b:5 + 2 * b, :], xn[:, b, :].rearrange("p (a n) -> p a n", a=2))])
            root(NORM_F + b)
        take_row(mod_rows[:, 0, :], (1, 2), 4)
        take_row(mod_rows[:, 1, :], (7, 0), 6)
        for b in range(TB):
            act.wait_ge(s["y_normed"], 3 + b)
            squares(NORM_POOL_PRE + b, [(tok[:, b, :], xn[:, b, :])])
            root(NORM_POOL_PRE + b)
        take_row(g1m_row, (1, 2), 8)

        def expert_hi(k, step, final=False):
            act.wait_ge(s[f"m_in{k}"], (step + 1) * 16)
            if final:
                act.wait_ge(s[f"m_used{k - 4}"], step + 1)
            elif k >= 4:
                act.wait_ge(s[f"m_used{k}"], step + 1)
            elif not (isinstance(step, int) and step == 0):
                act.wait_ge(s[f"m_used{k}"], step)
            act.activation((last_hi if final else m_hi)[k][:], m_raw[k][:], ACT.Copy).then_inc(s[f"m_hi{k}"], 1)

        expert_hi(0, 0)
        expert_hi(1, 0)
        for g in range(NG):
            act.wait_ge(s["pooled"], g + 1)
            act.activation(dT[:, 2 * g:2 * g + 2, :], bank((7, 0, 1, 2)[g]).rearrange("p (k t) -> p k t", k=2),
                           ACT.Copy).then_inc(s["pooled_taken"], 1)
            if g in (1, 3):
                expert_hi(2 + g // 2, 0)
        for b in range(TB):
            act.wait_ge(s["pool_y_ready"], b + 1)
            squares(NORM_POOL + b, [(pool_y[:, b, :], sq_junk[:, b, :])])
            root(NORM_POOL + b)
        for b in range(TB):
            act.wait_ge(s["y_normed"], 5 + b)
            squares(NORM_MOE_PRE + b, [(tok[:, b, :], sq_junk[:, b, :])])
            root(NORM_MOE_PRE + b)
        load_table(ACT.Exp, 1)
        act.wait_ge(s["diff_ready"], 1)
        act.activation(route[:, R_EX:R_EX + 2], route[:, R_D:R_D + 2], ACT.Exp).then_inc(s["exp_ready"], 1)

        def tokens_hi(j):
            for half in range(2):
                part = slice(4 * half, 4 * half + 4)
                act.wait_ge(s["xs_ready"], 2 * j + half + 1)
                act.activation(xs_hi[:, part, :], xs_full[:, part, :], ACT.Copy).then_inc(s["xs_hi_ready"], 1)

        def expert_silu(step):
            act.wait_ge(s["m_used3"], step + 1)
            act.wait_ge(s["m_turned"], step + 1)
            act.activation(m_act[:], bank(1), ACT.Silu).then_inc(s["m_silu"], 1)

        def expert_turned_hi(step):
            act.wait_ge(s["m_turned"], step + 2)
            act.wait_ge(s["m_used5"], step + 1)
            act.activation(mT_hi[:].rearrange("p q t -> p (q t)"), bank(7), ACT.Copy).then_inc(s["m_thi"], 1)

        def iteration(step, first=False, ahead=True):
            if ahead:
                expert_hi(0, step + 1)
                expert_hi(1, step + 1)
            if not first:
                expert_turned_hi(step - 1)
            if ahead:
                expert_hi(2, step + 1)
            expert_silu(step)
            if ahead:
                expert_hi(3, step + 1)
            expert_hi(4, step, final=not ahead)
            expert_hi(5, step, final=not ahead)

        def extra_turned_hi(v):
            act.wait_ge(s["e_turned"], v + 1)
            act.activation(mT_hi[:].rearrange("p q t -> p (q t)"), bank(7), ACT.Copy).then_inc(s["e_thi"], 1)

        def extra_step(c, i):
            v = c * MSTEPS + i
            if not (isinstance(i, int) and i == 0):
                extra_turned_hi(v - 1)
            act.wait_ge(s["e_gated"], v + 1)
            act.activation(me_act[:], bank(1), ACT.Silu).then_inc(s["e_silu"], 1)

        def job(j, last, c=None):
            step = j * MSTEPS
            if c is not None:
                for half in range(2):
                    part = slice(4 * half, 4 * half + 4)
                    act.wait_ge(s["e_xs_ready"], 2 * c + half + 1)
                    act.activation(xe_hi[:, part, :], xe_full[half][:], ACT.Copy).then_inc(s["e_xs_hi"], 1)
                extra_step(c, 0)
            iteration(step, first=True)
            if c is not None:
                extra_step(c, 1)
                iteration(step + 1)
            with act.Fori(1 if c is None else 2, MSTEPS - 1) as i:
                if c is not None:
                    extra_step(c, i)
                iteration(step + i)
            end = step + MSTEPS - 1
            if c is not None:
                extra_step(c, MSTEPS - 1)
            iteration(end, ahead=not last)
            if c is not None:
                extra_turned_hi(c * MSTEPS + MSTEPS - 1)
                tokens_hi(j + 1)
            expert_turned_hi(end)
            if c is not None:
                act.wait_ge(s["e_down"], c + 1)
                act.activation(ye_slots[:].rearrange("p (a n) -> p a n", a=2), ps[:, 5:7, :],
                               ACT.Copy).then_inc(s["e_y_taken"], 1)
            elif not last:
                act.wait_ge(s["m_used3"], end + 1)
                tokens_hi(j + 1)
            act.wait_ge(s["m_used5"], end + 2)
            act.wait_ge(s["scattered"], 4 * j + 4)
            act.activation(y_slots[:].rearrange("p (a n) -> p a n", a=2), ps[:, 3:5, :],
                           ACT.Copy).then_inc(s["y_taken"], 1)

        load_table(ACT.Silu, 2)
        tokens_hi(0)
        job(0, False)
        act.wait_ge(s["route_ready"], 1)
        doubles, after, last_job = job_bounds(act)
        with act.Fori(0, doubles) as c:
            job(c + 1, False, c)
        with act.Fori(after, last_job) as j:
            job(j, False)
        j = last_job
        job(j, True)
        take_row(last_row, (5, 6), 10)
        load_table(ACT.Sqrt, 3)
        for b in range(TB):
            act.wait_ge(s["acc_added"], 4 * j + 6 + 2 * b)
            squares(NORM_LAST + b, [(acc[:, b, :], xm[:, b, :])])
            root(NORM_LAST + b)

    @block.vector
    def _(dve):
        done = Done(dve)
        step_ = s["dve_step"]
        for k in range(6):
            dve.sem_inc(s[f"m_split{k}"], 1)
        dve.sem_inc(s["m_act_ready"], 1)
        dve.sem_inc(s["m_tlo"], 1)

        def inverse_root(n):
            dve.wait_ge(s["sumsq_ready"], SUMS_UNTIL[n])
            dve.tensor_scalar(stat(n, 1), stat(n, 0), 1.0 / D, EPS, ALU.mult, ALU.add).then_inc(s["msq_ready"], 1)
            dve.wait_ge(s["sqrt_ready"], n + 1)
            done(dve.reciprocal(stat(n, 3), stat(n, 2)), s["rstd_ready"])

        dve.wait_ge(s["cols_turned"], 1)
        done(dve.tensor_copy(cols[:, 0:N_M0], ps[:, 0, 0:N_M0]), s["cols_ready"])
        dve.wait_ge(s["sink_in"], 16)
        done(dve.tensor_scalar(col(N_NSINK, H), col(N_SINK, H), -1.0, None, ALU.mult), s["nsink_ready"])
        inverse_root(NORM_LAT)
        for b in range(TB):
            done(dve.tensor_scalar(xn[:, b, :], tok[:, b, :], stat(NORM_LAT, 3)[:, b:b + 1], None, ALU.mult),
                 s["xn_ready"], wait=False)
        inverse_root(NORM_CTX)
        for b in range(CB):
            done(dve.tensor_scalar(ctx_tok[:, b, :], ctx_tok[:, b, :], stat(NORM_CTX, 3)[:, b:b + 1], None, ALU.mult),
                 s["xn_ready"], wait=False)

        def scale_column(at, scale, gain_col, sem=step_):
            done(dve.scalar_tensor_tensor(col(at, KC), scale, 1.0, gain_col, ALU.add, ALU.mult), sem)

        dve.wait_ge(s["ada_summed"], PE_PIECES)
        got = ps[:, 0, 0:4 * KC].rearrange("p (n a) -> p a n", a=2)
        for a, at in ((0, N_M0), (1, N_MC)):
            done(dve.tensor_tensor(col(at, 2 * KC), got[:, a, :], col(N_B, 2 * KC), ALU.add), step_)
        scale_column(N_A, col(N_M0 + KC, KC), gain(0, 0))
        scale_column(N_A + KC, col(N_MC + KC, KC), gain(0, 0), s["a_ready"])

        taken = [0]

        def take_turned(dst, a, shift):
            for f in range(4):
                n = taken[0]
                taken[0] += 1
                dve.wait_ge(s["turn_ready"], n + 1)
                for k in range(2):
                    kc = 2 * f + k
                    ins = dve.tensor_scalar(dst[:, kc, :], ps[:, FILL_BANKS[n % 2], k * T:(k + 1) * T],
                                            cols[:, a + kc:a + kc + 1], cols[:, shift + kc:shift + kc + 1], ALU.mult, ALU.add)
                done(ins, s["turned_taken"], wait=False)

        take_turned(hT, N_A, N_M0)
        take_turned(hcT, N_A + KC, N_MC)

        def take_columns(q):
            dve.wait_ge(s["colsum_ready"], q + 1)
            if isinstance(q, int):
                at = (N_M0 + 16 + 4 * q) if q < 8 else N_M1 + 4 * (q - 8)
                bias = N_B + 16 + 4 * q
                dst, src = col(at, 4), col(bias, 4)
            else:
                dst, src = cols[:, bass.ds(q * 4 + (N_M1 - 32), 4)], cols[:, bass.ds(q * 4 + (N_B + 16), 4)]
            dve.tensor_tensor(dst, ps[:, 0, 0:4], src, ALU.add).then_inc(s["mod_ready"], 1)

        def sum_chunk(q, w, k):
            v, acc_q = cols[:, N_SC + 2 * k:N_SC + 2 * k + 1], acc_of(q)
            if k == 0:
                ins = dve.tensor_scalar(acc_q[:], w[:, k, :], v, None, ALU.mult)
            else:
                dve.wait_ge(s["acc_ready"], q * KC + k)
                ins = dve.scalar_tensor_tensor(acc_q[:], w[:, k, :], v, acc_q[:], ALU.mult, ALU.add)
            ins.then_inc(s["acc_ready"], 1)

        def sum_piece(q, w):
            for k in range(KC):
                sum_chunk(q, w, k)

        def early_chunk(q, k):
            i = q + PE_PIECES
            if k == 0:
                dve.wait_ge(s[f"ada_in{i % 3}"], 16 * (i // 3 + 1))
            sum_chunk(q, ada_ring[i % 3], k)

        def rope(src, b, heads, dsts, sem, wait=True):
            def table(t, part=None):
                v = t.rearrange("p (x a r) -> p x a r", x=2, a=2)
                return v if part is None else v[:, :, part:part + 1, :]
            w = heads * HD
            xv = src.rearrange("p (h x a r) -> p h x a r", h=heads, x=2, a=2)
            av = rope_a[:, 0:w].rearrange("p (h d) -> p h d", h=heads)
            bv = rope_b[:, 0:w].rearrange("p (h x a r) -> p h x a r", h=heads, x=2, a=2)
            done(dve.tensor_tensor(av, src.rearrange("p (h d) -> p h d", h=heads),
                                   cos_of(b).unsqueeze(1).to_broadcast([P, heads, HD]), ALU.mult), step_, wait=False)
            sn = sin_of(b).rearrange("p (x a r) -> p x a r", x=2, a=2)
            for part in range(2):
                for half in range(2):
                    ins = dve.tensor_tensor(bv[:, :, half, part, :], xv[:, :, half, 1 - part, :],
                                            sn[:, half, part, :].unsqueeze(1).to_broadcast([P, heads, ROPE_HALF]), ALU.mult)
            done(ins, step_)
            for n, dst in enumerate(dsts):
                ins = dve.tensor_tensor(dst, av, rope_b[:, 0:w].rearrange("p (h d) -> p h d", h=heads), ALU.add)
            done(ins, sem, wait)

        def low_parts(f):
            dve.wait_ge(s["tr2_hi"], f + 1)
            if f < HKV:
                dve.tensor_tensor(k_lo[:, f, :], bank(1 + f % 2), k_hi[:, f, :].bitcast(F32),
                                  ALU.subtract).then_inc(s["tr2_taken"], 1)
            else:
                f -= HKV
                part = q_parts[HD:P, 2 * f:2 * f + 2, :]
                dve.tensor_tensor(part, ps[HD:P, 1 + f % 4, :].rearrange("p (k t) -> p k t", k=2), part.bitcast(F32),
                                  ALU.subtract).then_inc(s["tr2_taken"], 1)

        UNITS = [("kv", 0), ("kv", 1), None, None, (0, 0), (1, 0), (0, 1), (1, 1)]
        for u, what in enumerate(UNITS):
            if what is not None:
                dve.wait_ge(s["qkv_ready"], u + 1)
                src = bank(3 + u % 4)
                if what[0] == "kv" and u < 2:
                    b = what[1]
                    done(dve.tensor_copy(v_tok[:, b, :], src[:, KVD:2 * KVD]), step_, wait=False)
                    rope(src[:, 0:KVD], b, HKV, [k_tok[:, b, :, i, :] for i in range(2)], s["kv_lat_taken"])
                else:
                    b, n = what
                    rope(src, b, 8, [q_tok[b][:, 8 * n:8 * n + 8, 0, :]], s["q_taken"])
            if u == 6:
                low_parts(0)
                low_parts(1)
            if u == 7:
                low_parts(2)
                low_parts(3)
            if u >= 2:
                take_columns(u - 2)
            for k in range(KC):
                if u < MIXER_PIECES:
                    early_chunk(u, k)
                if u == 7:
                    low_parts(HKV + k)

        NU = TB * H
        OB = [7, 1, 7, 1]
        SB = [3, 4, 2]

        def normalise(og):
            c8 = slice(8 * og, 8 * og + 8)
            part = lambda at: small[:, at + 8 * og:at + 8 * og + 8]
            dve.wait_ge(s["esink_ready"], og + 1)
            done(dve.tensor_tensor(part(SM_DEN), part(SM_SUM), part(SM_ES), ALU.add), step_)
            done(dve.reciprocal(part(SM_RDEN), part(SM_DEN)), step_)
            dve.wait_ge(s["pv_ready"], 8 * (og + 1))
            b, half = divmod(og, 2)
            done(dve.tensor_tensor(o_tok[:, b, 512 * half:512 * half + 512].rearrange("p (h d) -> p h d", h=8),
                                   bank(OB[og]).rearrange("p (h d) -> p h d", h=8),
                                   part(SM_RDEN).unsqueeze(2).to_broadcast([P, 8, HD]), ALU.mult), s["o_taken"], wait=False)

        for u in range(NU):
            h = u % H
            dve.wait_ge(s["scores_ready"], u + 1)
            done(dve.tensor_reduce(small[:, SM_MAX + u:SM_MAX + u + 1], bank(SB[u % 3]), AX.X, ALU.max), s["max_ready"])
            done(dve.tensor_scalar(small[:, SM_NM + u:SM_NM + u + 1], small[:, SM_MAX + u:SM_MAX + u + 1], -(HD ** -0.5),
                                   cols[:, N_NSINK + h:N_NSINK + h + 1], ALU.mult, ALU.min), s["nmax_ready"], wait=(u % 8 == 7))
            if u % 8 == 7:
                og = u // 8
                h0 = 8 * (og % 2)
                done(dve.tensor_tensor(small[:, SM_ES + 8 * og:SM_ES + 8 * og + 8], small[:, SM_NM + 8 * og:SM_NM + 8 * og + 8],
                                       col(N_SINK + h0, 8), ALU.add), s["esink_in"], wait=False)
            if u % 8 == 3 and u > 8:
                normalise(u // 8 - 1)
            if u % KC == 3 and u > KC:
                take_columns(MIXER_PIECES + u // KC - 1)
            early_chunk(MIXER_PIECES + u // KC, u % KC)
        take_columns(EARLY - 1)
        done.n[s["mod_ready"]] = EARLY
        dve.wait_ge(s["mod_ready"], EARLY)
        scale_column(N_A + 2 * KC, col(N_M0 + 4 * KC, KC), gain(0, 2), s["a_ready"])
        done(dve.tensor_tensor(col(N_G + KC, KC), col(N_M0 + 5 * KC, KC), gain(0, 3), ALU.mult), step_)
        done(dve.tensor_tensor(col(N_G, KC), col(N_M0 + 2 * KC, KC), gain(0, 1), ALU.mult), s["a_ready"])
        normalise(3)

        def add_normed(n, b, y, row, scratch, rstd):
            done(dve.scalar_tensor_tensor(scratch, y, rstd, row, ALU.mult, ALU.mult), step_)
            done(dve.tensor_tensor(tok[:, b, :], tok[:, b, :], y_flat(scratch), ALU.add), s["y_normed"])

        def two(v):
            return v.rearrange("p (a n) -> p a n", a=2)

        def y_flat(v):
            return v if len(v.shape) == 2 else v.rearrange("p a n -> p (a n)")

        def dense_lo(k, st):
            dve.wait_ge(s[f"f_hi{k}"], st + 1)
            dve.tensor_tensor(f_lo[k][:], f_raw[k][:], f_hi[k][:].bitcast(F32), ALU.subtract).then_inc(s[f"f_split{k}"], 1)

        dve.wait_ge(s["row_taken"], 2)
        dense_lo(0, 0)
        for b in range(TB):
            inverse_root(NORM_Y + 2 * b)
            add_normed(NORM_Y, b, ps[:, 3 + 2 * b:5 + 2 * b, :], two(g_row[:]), two(y_tmp[:]), stat(NORM_Y + 2 * b, 3))
            if b == 1:
                dense_lo(1, 0)
            inverse_root(NORM_Y + 2 * b + 1)
            done(dve.tensor_scalar(xn[:, b, :], tok[:, b, :], stat(NORM_Y + 2 * b + 1, 3), None, ALU.mult),
                 s["xn_ready"], wait=False)
            part = slice(b * P, (b + 1) * P)
            for half in range(2):
                dve.wait_ge(s["turn_ready"], 9 + 2 * b + half)
                for k in range(4):
                    kc = 4 * half + k
                    a, shift = N_A + 2 * KC + kc, N_M0 + 3 * KC + kc
                    ins = dve.tensor_scalar(hf[:, kc, part], ps[:, 1 + 2 * b + half, k * P:(k + 1) * P],
                                            cols[:, a:a + 1], cols[:, shift:shift + 1], ALU.mult, ALU.add)
                done(ins, s["turned_taken"], wait=False)
            for half in range(2):
                chunks = slice(4 * half, 4 * half + 4)
                dve.wait_ge(s["hf_hi_ready"], 2 * b + half + 1)
                dve.tensor_tensor(hf_lo[:, chunks, part], hf[:, chunks, part], hf_hi[:, chunks, part].bitcast(F32),
                                  ALU.subtract).then_inc(s["hf_ready"], 1)
        taken[0] += 4

        def dense_turned_lo(st):
            dve.wait_ge(s["f_thi"], st + 1)
            dve.tensor_tensor(fT_lo[:].rearrange("p q b t -> p (q b t)"), bank(7),
                              fT_hi[:].rearrange("p q b t -> p (q b t)").bitcast(F32), ALU.subtract).then_inc(s["f_tlo"], 1)

        def dense_iteration(st, first=False, last=False):
            if not first:
                dense_turned_lo(st - 1)
            if not last:
                dense_lo(0, st + 1)
            dve.wait_ge(s["f_silu"], st + 1)
            dve.tensor_tensor(f_act[:], f_act[:], ps[:, 1:3, FS:2 * FS], ALU.mult).then_inc(s["f_act_ready"], 1)
            if not last:
                dense_lo(1, st + 1)
            dense_lo(2, st)
            if not first:
                take_columns(st + EARLY - 1)
            if not last:
                dve.wait_ge(s["ada_late_in"], (st + 1) * 16)
                sum_piece(st + EARLY, ada_ring[0])

        dense_iteration(0, first=True)
        with dve.Fori(1, FSTEPS - 1) as st:
            dense_iteration(st)
        dense_iteration(FSTEPS - 1, last=True)
        dense_turned_lo(FSTEPS - 1)
        dve.wait_ge(s["mod_ready"], EARLY + L1_LATE)
        scale_column(N_A + 3 * KC, col(N_M1 + KC, KC), gain(1, 0))
        scale_column(N_A + 4 * KC, col(N_M1 + 4 * KC, KC), gain(1, 2))
        done(dve.tensor_tensor(col(N_G + 3 * KC, KC), col(N_M1 + 5 * KC, KC), gain(1, 3), ALU.mult), step_)
        done(dve.tensor_tensor(col(N_G + 2 * KC, KC), col(N_M1 + 2 * KC, KC), gain(1, 1), ALU.mult), s["a_ready"])

        dve.wait_ge(s["row_taken"], 4)
        for b in range(TB):
            inverse_root(NORM_F + b)
            add_normed(NORM_F, b, ps[:, 3 + 2 * b:5 + 2 * b, :], two(g_row[:]), two(y_tmp[:]), stat(NORM_F + b, 3))
        for b in range(TB):
            inverse_root(NORM_POOL_PRE + b)
            dve.wait_ge(s["row_taken"], 6)
            done(dve.scalar_tensor_tensor(h_tok[:, b, :], tok[:, b, :], stat(NORM_POOL_PRE + b, 3), mod_rows[:, 0, :],
                                          ALU.mult, ALU.mult), step_)
            dve.wait_ge(s["row_taken"], 8)
            done(dve.tensor_tensor(h_tok[:, b, :], h_tok[:, b, :], mod_rows[:, 1, :], ALU.add), s["xn_ready"], wait=False)

        def expert_lo(k, step, final=False):
            high, low = (last_hi, last_lo) if final else (m_hi, m_lo)
            dve.wait_ge(s[f"m_hi{k}"], step + 1)
            dve.tensor_tensor(low[k][:], m_raw[k][:], high[k][:].bitcast(F32), ALU.subtract).then_inc(s[f"m_split{k}"], 1)

        for k in range(3):
            expert_lo(k, 0)
        for b in range(TB):
            dve.wait_ge(s["poolmix_ready"], b + 1)
            done(dve.tensor_tensor(two(pool_y[:, b, :]), ps[:, 3 + 2 * b:5 + 2 * b, :], two(pool_s_row[:]), ALU.mult),
                 s["pool_y_ready"], wait=(b == 1))
        expert_lo(3, 0)
        dve.wait_ge(s["row_taken"], 10)
        for b in range(TB):
            inverse_root(NORM_POOL + b)
            add_normed(NORM_POOL, b, pool_y[:, b, :], g1m_row[:], pool_y[:, b, :], stat(NORM_POOL + b, 3))
        for b in range(TB):
            inverse_root(NORM_MOE_PRE + b)
            done(dve.tensor_scalar(xm[:, b, :], tok[:, b, :], stat(NORM_MOE_PRE + b, 3), None, ALU.mult),
                 s["xn_ready"], wait=False)
        take_turned(hr, N_A + 4 * KC, N_M1 + 3 * KC)

        def r(at, n=E):
            return route[:, at:at + n]

        def both(at):
            return route[:, at:at + 2 * E].rearrange("p (b e) -> p b e", b=TB)

        def pair(at):
            return route[:, at:at + TB].unsqueeze(2).to_broadcast([P, TB, E])

        experts = ct[:, K_IOTA:K_IOTA + E]
        experts_both = experts.unsqueeze(1).to_broadcast([P, TB, E])
        bias = col(N_RB, E)
        done(dve.memset(job_table[:], -1.0), step_, wait=False)
        done(dve.memset(jobs_f[:], 0.0), step_, wait=False)
        dve.wait_ge(s["router_ready"], 1)
        for b in range(TB):
            done(dve.tensor_tensor(r(R_L + b * E), ps[:, (7, 0)[b], 0:E], bias, ALU.add), step_, wait=(b == 1))
        for b in range(TB):
            done(dve.max(r(R_TOP + b * E), r(R_L + b * E)), step_, wait=(b == 1))
        for b in range(TB):
            done(dve.max_index(top_i[:, b * E:(b + 1) * E], r(R_TOP + b * E), r(R_L + b * E)), step_, wait=False)
        done(dve.tensor_tensor(route[:, R_D:R_D + 2], both(R_TOP)[:, :, 1], both(R_TOP)[:, :, 0], ALU.subtract), s["diff_ready"])
        done(dve.tensor_copy(r(R_TOPI, 2 * E), top_i[:]), step_)
        for n, at in ((0, R_H1), (1, R_H2)):
            done(dve.tensor_tensor(both(at), experts_both, both(R_TOPI)[:, :, n:n + 1].to_broadcast([P, TB, E]),
                                   ALU.is_equal), step_, wait=(n == 1))
        done(dve.tensor_tensor(r(R_MASK, 2 * E), r(R_H1, 2 * E), r(R_H2, 2 * E), ALU.add), s["mask_ready"], wait=False)
        dve.wait_ge(s["exp_ready"], 1)
        done(dve.tensor_scalar(route[:, R_DEN:R_DEN + 2], route[:, R_EX:R_EX + 2], 1.0, None, ALU.add), step_)
        done(dve.reciprocal(route[:, R_G1:R_G1 + 2], route[:, R_DEN:R_DEN + 2]), step_)
        done(dve.tensor_tensor(route[:, R_G2:R_G2 + 2], route[:, R_EX:R_EX + 2], route[:, R_G1:R_G1 + 2], ALU.mult), step_)
        done(dve.tensor_tensor(both(R_H1), both(R_H1), pair(R_G1), ALU.mult), step_, wait=False)
        done(dve.tensor_tensor(both(R_H2), both(R_H2), pair(R_G2), ALU.mult), step_)
        done(dve.tensor_tensor(r(R_GATE, 2 * E), r(R_H1, 2 * E), r(R_H2, 2 * E), ALU.add), step_, wait=False)
        dve.wait_ge(s["ranks_ready"], 1)
        done(dve.scalar_tensor_tensor(r(R_POS, 2 * E), ps[:, 1, 0:2 * E], 1.0, r(R_MASK, 2 * E), ALU.add, ALU.mult), step_)
        done(dve.tensor_scalar(r(R_POS, 2 * E), r(R_POS, 2 * E), -1.0, None, ALU.add), step_)
        for b in range(TB):
            ins = dve.tensor_scalar(hot[:, b, :], iota, route[:, R_POS + b * E:R_POS + b * E + 1], None, ALU.is_equal)
        ins.then_inc(s["hot_ready"], 1)
        dve.wait_ge(s["ranks_ready"], 2)
        done(dve.tensor_copy(r(R_CNT), ps[:, 2, 0:E]), step_)
        def split_tokens(n, full, high, low, gathered, ready, hi_ready, split, banks=(5, 6)):
            for k in range(KC):
                if k % 4 == 0:
                    dve.wait_ge(gathered, 2 * n + k // 4 + 1)
                a, b = N_A + 4 * KC + k, N_M1 + 3 * KC + k
                ins = dve.tensor_scalar(full(k // 4)[:, k % 4, :], ps[:, banks[k // 4], (k % 4) * P:(k % 4 + 1) * P],
                                        cols[:, a:a + 1], cols[:, b:b + 1], ALU.mult, ALU.add)
                if k % 4 == 3:
                    ins.then_inc(ready, 1)
            for half in range(2):
                dve.wait_ge(hi_ready, 2 * n + half + 1)
                dve.tensor_tensor(low(half), full(half), high(half).bitcast(F32), ALU.subtract).then_inc(split, 1)

        def tokens(j, banks=(5, 6)):
            split_tokens(j, lambda h: xs_full[:, 4 * h:4 * h + 4, :],
                         lambda h: xs_hi[:, 4 * h:4 * h + 4, :], lambda h: xs_lo[:, 4 * h:4 * h + 4, :],
                         s["gathered"], s["xs_ready"], s["xs_hi_ready"], s["xs_split"], banks)

        R_CR, R_N, R_RK, R_PLACE, R_O = R_CNT, R_JUNK, R_RANK, R_RANK + E, 176
        done(dve.tensor_scalar(r(R_OVER), r(R_CNT), float(SLOTS), None, ALU.is_gt), step_)
        done(dve.tensor_copy(r(R_CR), r(R_OVER)), step_)
        done(dve.memset(r(R_CR, 1), 0.0), step_)
        done(dve.tensor_reduce(r(R_N, 1), r(R_CR), AX.X, ALU.add), step_)
        done(dve.scalar_tensor_tensor(r(R_CR + E - 1, 1), r(R_N, 1), 0.0, r(R_CR + E - 1, 1), ALU.is_equal, ALU.add), step_)
        done(dve.tensor_reduce(r(R_N, 1), r(R_CR), AX.X, ALU.add), step_, wait=False)
        done(dve.memset(r(R_RK), 0.0), step_)
        for e in range(2, E):
            done(dve.tensor_tensor(r(R_RK + e, 1), r(R_RK + e - 1, 1), r(R_CR + e - 1, 1), ALU.add), step_)
        tokens(0)
        a, b = r(R_N + 1), r(R_PLACE)
        done(dve.tensor_tensor(a, experts, r(R_RK), ALU.subtract), step_, wait=False)
        done(dve.tensor_scalar(b, r(R_RK), 1.0, None, ALU.add), step_)
        done(dve.tensor_scalar(a, a, r(R_N, 1), None, ALU.add), step_)
        done(dve.tensor_tensor(b, b, a, ALU.subtract), step_)
        done(dve.tensor_tensor(b, b, r(R_CR), ALU.mult), step_)
        done(dve.tensor_tensor(b, b, a, ALU.add), step_)
        done(dve.memset(r(R_PLACE, 1), 0.0), step_)
        order = route[:, R_O:R_O + E * E].rearrange("p (n e) -> p n e", e=E)
        done(dve.tensor_tensor(order, experts.unsqueeze(2).to_broadcast([P, E, E]),
                               b.unsqueeze(1).to_broadcast([P, E, E]), ALU.is_equal), step_)
        products = small[:, SM_NM:SM_NM + 3 * E * E].rearrange("p (w n e) -> p w n e", w=3, e=E)
        sources = [(experts, jobs_f[:, 0:E])] + [(r(at + b * E), job_table[:, 2 * w + b, 0:E])
                                                 for w, at in enumerate((R_POS, R_GATE)) for b in range(TB)]
        for some in (sources[:3], sources[3:]):
            for n, (what, _) in enumerate(some):
                done(dve.tensor_tensor(products[:, n], order, what.unsqueeze(1).to_broadcast([P, E, E]), ALU.mult),
                     step_, wait=(n == len(some) - 1))
            for n, (_, to) in enumerate(some):
                done(dve.tensor_reduce(to, products[:, n], AX.X, ALU.add), step_, wait=(n == len(some) - 1))
        done(dve.tensor_scalar(job_table[:, 0:2, E], both(R_POS)[:, :, 0], -float(SLOTS), None, ALU.add), step_, wait=False)
        done(dve.tensor_copy(job_table[:, 2:4, E], both(R_GATE)[:, :, 0]), step_, wait=False)
        done(dve.tensor_copy(jobs_f[:, J_DOUBLE:J_DOUBLE + 1], r(R_N, 1)), step_, wait=False)
        done(dve.tensor_scalar(jobs_f[:, J_AFTER:J_AFTER + 1], r(R_N, 1), 1.0, None, ALU.add), step_, wait=False)
        done(dve.tensor_scalar(jobs_f[:, J_LAST:J_LAST + 1], r(R_OVER, 1), float(E - 1), None, ALU.add), step_)
        done(dve.tensor_copy(jobs_i[:], jobs_f[:]), s["route_ready"])
        doubles, after, last_job = job_bounds(dve)

        def job_column(j, count):
            dve.tensor_copy(job_col[:], job_table[:, :, bass.ds(j, 1)] if not isinstance(j, int) else job_table[:, :, j]
                            ).then_inc(s["job_col_ready"], 1)
            dve.wait_ge(s["job_col_ready"], count)

        def one_hot():
            for b in range(TB):
                ins = dve.tensor_scalar(hot[:, b, :], iota, job_col[:, b:b + 1], None, ALU.is_equal)
            ins.then_inc(s["hot_ready"], 1)

        def extra_turned_lo(v):
            dve.wait_ge(s["e_thi"], v + 1)
            dve.tensor_tensor(mT_lo[:].rearrange("p q t -> p (q t)"), bank(7),
                              mT_hi[:].rearrange("p q t -> p (q t)").bitcast(F32), ALU.subtract).then_inc(s["e_tlo"], 1)

        def extra_step(c, i):
            v = c * MSTEPS + i
            if not (isinstance(i, int) and i == 0):
                extra_turned_lo(v - 1)
            dve.wait_ge(s["e_silu"], v + 1)
            dve.tensor_tensor(me_act[:], me_act[:], bank(2), ALU.mult).then_inc(s["e_act_ready"], 1)

        def add_piece(j, n):
            b, half = divmod(n, 2)
            dve.wait_ge(s["scattered"], 4 * j + n + 1)
            part = acc[:, b, 512 * half:512 * half + 512]
            dve.tensor_tensor(part, part, bank((5, 6, 0, 5)[n]), ALU.add).then_inc(s["acc_added"], 1)

        def expert_turned_lo(step):
            dve.wait_ge(s["m_thi"], step + 1)
            dve.tensor_tensor(mT_lo[:].rearrange("p q t -> p (q t)"), bank(7),
                              mT_hi[:].rearrange("p q t -> p (q t)").bitcast(F32), ALU.subtract).then_inc(s["m_tlo"], 1)

        def expert_act(step):
            dve.wait_ge(s["m_silu"], step + 1)
            dve.tensor_tensor(m_act[:], m_act[:], bank(2), ALU.mult).then_inc(s["m_act_ready"], 1)

        def iteration(step, first=False, ahead=True, before=None, after=None):
            if ahead:
                expert_lo(0, step + 1)
                expert_lo(1, step + 1)
            if not first:
                expert_turned_lo(step - 1)
            if before:
                before()
            if ahead:
                expert_lo(2, step + 1)
            expert_act(step)
            if after:
                after()
            if ahead:
                expert_lo(3, step + 1)
            expert_lo(4, step, final=not ahead)
            expert_lo(5, step, final=not ahead)

        def job(j, last, c=None):
            step = j * MSTEPS

            def adds():
                for n in range(3):
                    add_piece(j, n)
                job_column(j, 2 * j + 2)
                for b in range(TB):
                    ins = dve.tensor_scalar(hot_g[:, b, :], iota, job_col[:, b:b + 1], job_col[:, TB + b:TB + b + 1],
                                            ALU.is_equal, ALU.mult)
                ins.then_inc(s["hotg_ready"], 1)

            def turned():
                add_piece(j, 3)
                dve.wait_ge(s["hotg_turned"], j + 1)
                dve.tensor_copy(hotT[:].rearrange("p b t -> p (b t)"), ps[:, 6, 0:TB * P]).then_inc(s["hotT_ready"], 1)
                job_column(j + 1, 2 * j + 3)
                dve.wait_ge(s["gathered"], 2 * j + 2)
                one_hot()

            def extra_gates():
                for b in range(TB):
                    ins = dve.tensor_scalar(hot_g[:, b, :], iota, job_col_e[:, b:b + 1], job_col_e[:, TB + b:TB + b + 1],
                                            ALU.is_equal, ALU.mult)
                ins.then_inc(s["e_hotg"], 1)

            def extra_gates_turned():
                dve.wait_ge(s["e_hotg_turned"], c + 1)
                dve.tensor_copy(hotTe[:].rearrange("p b t -> p (b t)"), ps[:, 0, 0:TB * P]).then_inc(s["e_hotT"], 1)

            if c is None:
                iteration(step, first=True)
                iteration(step + 1, before=adds, after=turned)
            else:
                dve.tensor_scalar(job_col_e[:, 0:TB], job_col[:, 0:TB], -float(SLOTS), None, ALU.add)
                dve.tensor_copy(job_col_e[:, TB:2 * TB], job_col[:, TB:2 * TB]).then_inc(s["e_col"], 1)
                dve.wait_ge(s["e_col"], c + 1)
                for b in range(TB):
                    ins = dve.tensor_scalar(hot[:, b, :], iota, job_col_e[:, b:b + 1], None, ALU.is_equal)
                ins.then_inc(s["e_hot"], 1)
                split_tokens(c, lambda h: xe_full[h][:], lambda h: xe_hi[:, 4 * h:4 * h + 4, :], lambda h: xe_lo[h][:],
                             s["e_gathered"], s["e_xs_ready"], s["e_xs_hi"], s["e_xs_split"])
                extra_step(c, 0)
                iteration(step, first=True, before=adds, after=turned)
                extra_step(c, 1)
                iteration(step + 1, before=extra_gates, after=extra_gates_turned)
            with dve.Fori(2, MSTEPS - 1) as i:
                if c is not None:
                    extra_step(c, i)
                iteration(step + i)
            end = step + MSTEPS - 1
            if c is not None:
                extra_step(c, MSTEPS - 1)
            iteration(end, ahead=not last)
            if c is not None:
                extra_turned_lo(c * MSTEPS + MSTEPS - 1)
                tokens(j + 1, (1, 2))
            expert_turned_lo(end)
            if c is not None:
                for n in range(4):
                    b, half = divmod(n, 2)
                    dve.wait_ge(s["e_scattered"], 4 * c + n + 1)
                    part = acc[:, b, 512 * half:512 * half + 512]
                    dve.tensor_tensor(part, part, bank((5, 6, 0, 7)[n]), ALU.add).then_inc(s["e_added"], 1)
            elif not last:
                tokens(j + 1)

        dve.wait_ge(s["zeroed"], 1)
        dve.sem_inc(s["job_col_ready"], 1)
        job(0, False)
        with dve.Fori(0, doubles) as c:
            job(c + 1, False, c)
        with dve.Fori(after, last_job) as j:
            job(j, False)
        j = last_job
        job(j, True)
        for n in range(4):
            add_piece(j + 1, n)
        dve.wait_ge(s["row_taken"], 12)
        for b in range(TB):
            inverse_root(NORM_LAST + b)
            done(dve.scalar_tensor_tensor(acc[:, b, :], acc[:, b, :], stat(NORM_LAST + b, 3), last_row[:],
                                          ALU.mult, ALU.mult), step_)
            done(dve.tensor_tensor(tok[:, b, :], tok[:, b, :], acc[:, b, :], ALU.add), s["tok_ready"], wait=False)

    block.__exit__(None, None, None)


_INS = ['x', 'c', 'ctx', 'c_ctx', 'ada_w', 'ada_b', 'norm_g', 'attn_w_qkv', 'attn_w_o', 'attn_sink', 'pool_w', 'pool_b',
        'pool_scale', 'ffn_w_gu', 'ffn_w_down', 'router_w', 'router_b', 'moe_w_gu', 'moe_w_down']


def kernel(**inputs):
    import concourse.bacc as bacc
    from concourse.bass_utils import run_bass_kernel_spmd

    nc = bacc.Bacc("TRN2", target_bir_lowering=False, num_devices=1)
    arrays = {f"in_{name}": np.ascontiguousarray(inputs[name]) for name in _INS}
    arrays["in_consts"], arrays["in_pool_m"] = constants()
    args = [nc.dram_tensor(name, a.shape, F32, kind="ExternalInput").ap() for name, a in arrays.items()]
    out = nc.dram_tensor("out_0", (1, T, D), F32, kind="ExternalOutput").ap()
    build(nc, *args, out)
    r = run_bass_kernel_spmd(nc, [arrays], core_ids=[0])
    return np.asarray(r.results[0]["out_0"])
```
